# Optimizing a Trainium2 kernel written in Bass

```python
import jax, jax.numpy as jnp
from jax import lax
import numpy as np

D_MODEL = 1024
BATCH = 1
SEQ = 256
DEPTH = 1
DEC_BATCH = 1
DEC_SEQ = 1024
PAST_LEN = 128

GRID_W = 64
GLA_HEADS = 4
GLA_DK = 128
GLA_DV = 256
GLA_RANK = 16
GLA_GATE_NORM = 16.0
GLA_CHUNK = 64
GLA_QK = GLA_HEADS * GLA_DK
GLA_V = GLA_HEADS * GLA_DV
ATT_HEADS = 8
ATT_KV_HEADS = 2
ATT_HD = 128
ATT_Q = ATT_HEADS * ATT_HD
ATT_KV = ATT_KV_HEADS * ATT_HD
ROPE_THETA = 10000.0
Q_BLOCK = 128
N_EXPERTS = 16
CAPACITY_FACTOR = 2
EXPERT_FF = 2048
EPS = 1e-6
IN_SPLITS = (GLA_QK, GLA_QK, GLA_V, GLA_V, GLA_RANK, GLA_RANK, ATT_Q, ATT_KV, ATT_KV, D_MODEL, D_MODEL)
D_IN = GLA_QK * 2 + GLA_V * 2 + GLA_RANK * 2 + ATT_Q + ATT_KV * 2 + D_MODEL * 2

kernel_name = 'hybrid_gla_gqa_ec_encoder'

def _split_points():
    pts, acc = [], 0
    for w in IN_SPLITS[:-1]:
        acc += w
        pts.append(acc)
    return pts

def _rmsnorm(x, g):
    xf = x.astype(jnp.float32)
    y = xf * lax.rsqrt(jnp.mean(xf * xf, axis=-1, keepdims=True) + EPS) * g.astype(jnp.float32)
    return y.astype(x.dtype)

def _gla_one_direction(q, k, v, lg):
    B, H, S, dk = q.shape
    dv = v.shape[-1]
    C = GLA_CHUNK
    N = S // C
    q = q.reshape(B, H, N, C, dk)
    k = k.reshape(B, H, N, C, dk)
    v = v.reshape(B, H, N, C, dv)
    b = jnp.cumsum(lg.reshape(B, H, N, C, dk), axis=3)
    bT = b[:, :, :, -1:, :]
    q_t = q * jnp.exp(b)
    k_t = k * jnp.exp(-b)
    k_hat = k * jnp.exp(bT - b)
    mask = jnp.tril(jnp.ones((C, C), dtype=bool))
    A = jnp.where(mask, jnp.einsum('bhnid,bhnjd->bhnij', q_t, k_t), 0.0)
    o_intra = jnp.einsum('bhnij,bhnjv->bhniv', A, v)
    U = jnp.einsum('bhncd,bhncv->bhndv', k_hat, v)
    decay = jnp.exp(bT[:, :, :, 0, :])

    def step(state, inp):
        q_n, U_n, d_n = inp
        o_n = jnp.einsum('bhcd,bhdv->bhcv', q_n, state)
        return d_n[..., None] * state + U_n, o_n

    s0 = jnp.zeros((B, H, dk, dv), jnp.float32)
    _, o_inter = lax.scan(step, s0, (jnp.moveaxis(q_t, 2, 0), jnp.moveaxis(U, 2, 0), jnp.moveaxis(decay, 2, 0)))
    o = o_intra + jnp.moveaxis(o_inter, 0, 2)
    return o.reshape(B, H, S, dv)

def _gla_branch(q, k, v, g, r_f, r_b, w_gk_f, b_gk_f, w_gk_b, b_gk_b, gla_norm):
    B, S, _ = q.shape

    def heads(t, d):
        return t.reshape(B, S, GLA_HEADS, d).transpose(0, 2, 1, 3).astype(jnp.float32)

    qh = heads(q, GLA_DK) * (GLA_DK ** -0.5)
    kh = heads(k, GLA_DK)
    vh = heads(v, GLA_DV)
    lg_f = heads(jax.nn.log_sigmoid((r_f @ w_gk_f + b_gk_f).astype(jnp.float32)) / GLA_GATE_NORM, GLA_DK)
    lg_b = heads(jax.nn.log_sigmoid((r_b @ w_gk_b + b_gk_b).astype(jnp.float32)) / GLA_GATE_NORM, GLA_DK)
    o_f = _gla_one_direction(qh, kh, vh, lg_f)
    o_b = jnp.flip(_gla_one_direction(jnp.flip(qh, 2), jnp.flip(kh, 2), jnp.flip(vh, 2), jnp.flip(lg_b, 2)), 2)
    o = _rmsnorm(o_f + o_b, gla_norm)
    o = o.transpose(0, 2, 1, 3).reshape(B, S, GLA_V)
    return (o * jax.nn.silu(g.astype(jnp.float32))).astype(q.dtype)

def _axial_rope_tables(S):
    rows = S // GRID_W
    pos_r = jnp.repeat(jnp.arange(rows), GRID_W).astype(jnp.float32)
    pos_c = jnp.tile(jnp.arange(GRID_W), rows).astype(jnp.float32)
    half = ATT_HD // 2
    inv = ROPE_THETA ** (-jnp.arange(0, half, 2, dtype=jnp.float32) / half)
    ang = jnp.concatenate([pos_r[:, None] * inv, pos_c[:, None] * inv], axis=-1)
    return jnp.cos(ang), jnp.sin(ang)

def _apply_rope(x, cos, sin):
    xf = x.astype(jnp.float32).reshape(x.shape[:-1] + (ATT_HD // 2, 2))
    x0, x1 = xf[..., 0], xf[..., 1]
    out = jnp.stack([x0 * cos - x1 * sin, x0 * sin + x1 * cos], axis=-1)
    return out.reshape(x.shape)

def _gqa_branch(q, k, v, q_norm, k_norm):
    B, S, _ = q.shape
    G = ATT_HEADS // ATT_KV_HEADS
    qh = q.reshape(B, S, ATT_HEADS, ATT_HD).transpose(0, 2, 1, 3)
    kh = k.reshape(B, S, ATT_KV_HEADS, ATT_HD).transpose(0, 2, 1, 3)
    vh = v.reshape(B, S, ATT_KV_HEADS, ATT_HD).transpose(0, 2, 1, 3).astype(jnp.float32)
    cos, sin = _axial_rope_tables(S)
    qh = _apply_rope(_rmsnorm(qh, q_norm), cos, sin) * (ATT_HD ** -0.5)
    kh = _apply_rope(_rmsnorm(kh, k_norm), cos, sin)
    nb = S // Q_BLOCK
    qb = qh.reshape(B, ATT_KV_HEADS, G, nb, Q_BLOCK, ATT_HD).transpose(3, 0, 1, 2, 4, 5)

    def block(q_blk):
        s = jnp.einsum('bhgqd,bhkd->bhgqk', q_blk, kh)
        p = jax.nn.softmax(s, axis=-1)
        return jnp.einsum('bhgqk,bhkd->bhgqd', p, vh)

    o = lax.map(block, qb)
    o = o.transpose(1, 3, 4, 2, 0, 5)
    return o.reshape(B, S, ATT_Q).astype(q.dtype)

def _expert_choice_ffn(h, w_router, w_e_gate, w_e_up, w_e_down):
    B, S, D = h.shape
    T = B * S
    cap = CAPACITY_FACTOR * T // N_EXPERTS
    ht = h.reshape(T, D)
    aff = jax.nn.softmax((ht @ w_router).astype(jnp.float32), axis=-1)
    gate_vals, idx = lax.top_k(aff.T, cap)
    xe = ht[idx]
    hid = jax.nn.silu(jnp.einsum('ecd,edf->ecf', xe, w_e_gate)) * jnp.einsum('ecd,edf->ecf', xe, w_e_up)
    ye = jnp.einsum('ecf,efd->ecd', hid, w_e_down) * gate_vals[..., None].astype(h.dtype)
    out = jnp.zeros((T, D), ye.dtype).at[idx.reshape(-1)].add(ye.reshape(-1, D))
    return out.reshape(B, S, D).astype(h.dtype)

def _layer(x, norm_mix, w_in, w_gk_f, b_gk_f, w_gk_b, b_gk_b, gla_norm, q_norm, k_norm,
           w_o_gla, w_o_att, w_out, norm_ffn, w_router, w_e_gate, w_e_up, w_e_down):
    h = _rmsnorm(x, norm_mix)
    proj = h @ w_in
    gq, gk, gv, gg, r_f, r_b, aq, ak, av, z_a, z_b = jnp.split(proj, _split_points(), axis=-1)
    o_a = _gla_branch(gq, gk, gv, gg, r_f, r_b, w_gk_f, b_gk_f, w_gk_b, b_gk_b, gla_norm)
    o_b = _gqa_branch(aq, ak, av, q_norm, k_norm)
    merged = jax.nn.sigmoid(z_a) * (o_a @ w_o_gla) + jax.nn.sigmoid(z_b) * (o_b @ w_o_att)
    x = x + merged @ w_out
    x = x + _expert_choice_ffn(_rmsnorm(x, norm_ffn), w_router, w_e_gate, w_e_up, w_e_down)
    return x

def _trunk(x, params):
    for l in range(DEPTH):
        x = _layer(x, *[p[l] for p in params])
    return x

def setup_inputs(seed: int = 0) -> dict:
    key = jax.random.key(seed)
    ks = jax.random.split(key, 24)
    L = DEPTH

    def nrm(k, shape, scale):
        return jax.random.normal(k, shape, jnp.float32) * scale

    return {
        'x_prompt': nrm(ks[0], (BATCH, SEQ, D_MODEL), 1.0),
        'x_sample': nrm(ks[1], (DEC_BATCH, DEC_SEQ, D_MODEL), 1.0),
        'norm_mix': 1.0 + nrm(ks[2], (L, D_MODEL), 0.02),
        'w_in': nrm(ks[3], (L, D_MODEL, D_IN), D_MODEL ** -0.5),
        'w_gk_f': nrm(ks[4], (L, GLA_RANK, GLA_QK), GLA_RANK ** -0.5),
        'b_gk_f': nrm(ks[5], (L, GLA_QK), 0.1),
        'w_gk_b': nrm(ks[6], (L, GLA_RANK, GLA_QK), GLA_RANK ** -0.5),
        'b_gk_b': nrm(ks[7], (L, GLA_QK), 0.1),
        'gla_norm': 1.0 + nrm(ks[8], (L, GLA_DV), 0.02),
        'q_norm': 1.0 + nrm(ks[9], (L, ATT_HD), 0.02),
        'k_norm': 1.0 + nrm(ks[10], (L, ATT_HD), 0.02),
        'w_o_gla': nrm(ks[11], (L, GLA_V, D_MODEL), GLA_V ** -0.5),
        'w_o_att': nrm(ks[12], (L, ATT_Q, D_MODEL), ATT_Q ** -0.5),
        'w_out': nrm(ks[13], (L, D_MODEL, D_MODEL), D_MODEL ** -0.5),
        'norm_ffn': 1.0 + nrm(ks[14], (L, D_MODEL), 0.02),
        'w_router': nrm(ks[15], (L, D_MODEL, N_EXPERTS), D_MODEL ** -0.5),
        'w_e_gate': nrm(ks[16], (L, N_EXPERTS, D_MODEL, EXPERT_FF), D_MODEL ** -0.5),
        'w_e_up': nrm(ks[17], (L, N_EXPERTS, D_MODEL, EXPERT_FF), D_MODEL ** -0.5),
        'w_e_down': nrm(ks[18], (L, N_EXPERTS, EXPERT_FF, D_MODEL), EXPERT_FF ** -0.5),
    }

def reference(x_prompt, x_sample, norm_mix, w_in, w_gk_f, b_gk_f, w_gk_b, b_gk_b, gla_norm, q_norm, k_norm,
              w_o_gla, w_o_att, w_out, norm_ffn, w_router, w_e_gate, w_e_up, w_e_down):
    params = (norm_mix, w_in, w_gk_f, b_gk_f, w_gk_b, b_gk_b, gla_norm, q_norm, k_norm,
              w_o_gla, w_o_att, w_out, norm_ffn, w_router, w_e_gate, w_e_up, w_e_down)
    y_prompt = _trunk(x_prompt, params)
    y_sample = _trunk(x_sample, params)
    return (y_prompt, y_sample)


_drawn_inputs = setup_inputs


def setup_inputs(seed=0):
    import zlib

    import numpy as np

    out = dict(_drawn_inputs(seed))
    spreads = {}
    factors = {'norm_mix': 3.031,
     'b_gk_f': 3.864,
     'b_gk_b': 3.975,
     'gla_norm': 5.108,
     'q_norm': 8.0,
     'k_norm': 8.0,
     'norm_ffn': 3.506}
    for name, (base, spread) in spreads.items():
        noise = np.random.default_rng([zlib.crc32(name.encode()), seed]).standard_normal(out[name].shape)
        drawn = base * np.exp(spread * noise) if base else spread * noise
        out[name] = __import__('jax').numpy.asarray(drawn.astype(out[name].dtype))
    for name, factor in factors.items():
        out[name] = (out[name] * factor).astype(out[name].dtype)
    return out
```

```python
from contextlib import ExitStack

import numpy as np

import concourse.bass as bass
from concourse import mybir

ALU = mybir.AluOpType
ACT = mybir.ActivationFunctionType
AX = mybir.AxisListType
F32 = mybir.dt.float32
F32R = mybir.dt.float32r
BF16 = mybir.dt.bfloat16
U32 = mybir.dt.uint32
U8 = mybir.dt.uint8

P = 128
D = 1024
TS, TP = 1024, 256
T = TS + TP
NT, NTS = T // P, TS // P
KC = D // P
GRID_W = 64
GH, DK, DV, RANK, CH = 4, 128, 256, 16, 64
NCH, NCHS = T // CH, TS // CH
GATE_NORM = 16.0
AH, KVH, HD = 8, 2, 128
GR = AH // KVH
NE, FF = 16, 2048
CS, CP = 2 * TS // NE, 2 * TP // NE
CT = CS + CP
EPS = 1e-6
UW = 512
MU = UW // P
NB, NA = 7, 6
G_Q, G_KV, G_V, G_G = 0, 2, 3, 5
C_Q, C_K, C_ZA, C_ZB = 0, 512, 1024, 2048
TOK3 = [(0, 512), (512, 1024), (1024, T)]


CR = 8
ST = 16


class Phase:

    def __init__(self, nc, ctx, tag):
        self.nc, self.ctx, self.tag, self.counted, self.stores = nc, ctx, tag, [], []
        self.passed = self.ctx.enter_context(nc.semaphore(f"{tag}_passed"))

    def sb(self, name, shape, dt=F32):
        return self.ctx.enter_context(self.nc.sbuf_tensor(f"{self.tag}_{name}", shape, dt))

    def ps(self, name, shape):
        return self.ctx.enter_context(self.nc.psum_tensor(f"{self.tag}_{name}", shape, F32))

    def landed(self, name, n=1):
        s = [self.nc.alloc_semaphore(f"{self.tag}_{name}{i}") for i in range(n)]
        return s if n > 1 else s[0]

    def stored(self, name, n):
        s = [self.ctx.enter_context(self.nc.semaphore(f"{self.tag}_{name}{i}")) for i in range(n)]
        self.stores += s
        return s

    def done(self, *names):
        s = [self.ctx.enter_context(self.nc.semaphore(f"{self.tag}_{n}")) for n in names]
        self.counted += s
        return s if len(s) > 1 else s[0]

    def start(self, sp):
        for s in self.counted:
            sp.sem_inc(s, CR)
        for s in self.stores:
            sp.sem_inc(s, ST)

    def settle(self, eng):
        eng.sem_inc(self.passed, 1)

    def clear(self):
        with self.nc.Block() as block:

            @block.gpsimd
            def _(pool):
                for s in self.counted + self.stores + [self.passed]:
                    pool.sem_clear(s)


def three_passes(pe, out, a, b, first, last):
    pe.matmul(out, a[0], b[0], start=first, stop=False)
    pe.matmul(out, a[0], b[1], start=False, stop=False)
    return pe.matmul(out, a[1], b[0], start=False, stop=last)


def channel_tile(pe, banks, w, act, full):
    for k in range(KC):
        for part, other in ((0, 0), (0, 1), (1, 0)):
            for c, (a, b) in enumerate(TOK3):
                mm = pe.matmul(banks[:, c, 0:b - a], w(part, k), act(other, k, a, b),
                               start=(k == 0 and part == other), stop=(k == KC - 1 and part == 1))
                if k == KC - 1 and part == 1:
                    mm.then_inc(full, 1)


def project(nc, x, w_cols, norm_mix, cst, act_hl, proj_t, proj_c, rT):
    with ExitStack() as ctx:
        ph = Phase(nc, ctx, "pj")
        gamma = ph.sb("gamma", [P, D])
        ssq, root, rstd = ph.sb("ssq", [P, 2]), ph.sb("root", [P, 2]), ph.sb("rstd", [P, 2])
        raw = ph.sb("w_raw", [P, 2, KC, UW])
        xs = raw[:, 1].rearrange("p k c -> p (k c)").rearrange("p (j s d) -> p j s d", j=2, s=2)
        xt, xn = xs[:, 0], xs[:, 1]
        whi, wlo = ph.sb("w_hi", [P, 2, KC, UW], F32R), ph.sb("w_lo", [P, 2, KC, UW], F32R)
        rraw = ph.sb("r_raw", [P, KC, 2 * RANK])
        rhi, rlo = ph.sb("r_hi", [P, KC, 2 * RANK], F32R), ph.sb("r_lo", [P, KC, 2 * RANK], F32R)
        stage = ph.sb("stage", [P, 2, UW])
        ps_c, ps_t = ph.ps("ps_chan", [P, 2, 3, 512]), ph.ps("ps_tok", [P, 2, 512])
        gamma_in, x_in, w_in, r_in = ph.landed("gamma_in"), ph.landed("x_in", 2), ph.landed("w_in", 2), ph.landed("r_in")
        squared, rooted, inverted, x_ready = ph.done("squared", "rooted", "inverted", "x_ready")
        turned, h_hi, h_lo = ph.done("turned", "h_hi", "h_lo")
        w_hi, w_lo, r_hi, r_lo = ph.done("w_hid", "w_lod", "r_hid", "r_lod")
        p_full, p_out = ph.done("p_full", "p_out")
        stored = ph.stored("stored", 2)
        x_d = x.rearrange("(n p) d -> p n d", p=P)
        w_d = w_cols.rearrange("(k p) c -> p k c", p=P)
        t_d = proj_t.rearrange("(n p) c -> p n c", p=P)
        tok_n, chan_n = NB * NT, NA * MU * 3
        turn_ps = ps_c[:, 0, 0:2].rearrange("p a (k t) -> p (a k) t", t=P)

        with nc.Block() as block:

            @block.sync
            def _(sp):
                def store(q, s, dst, width):
                    sp.wait_ge(p_out, CR + q + 1)
                    sp.dma_start(dst, stage[:, s, 0:width]).then_inc(stored[s], 16)

                ph.start(sp)
                with sp.Fori(0, NB) as n:
                    for t in range(NT):
                        store(n * NT + t, t % 2, t_d[:, t, bass.ds(n * UW, UW)], UW)
                with sp.Fori(0, NA) as n:
                    for q in range(3 * MU):
                        a, b = TOK3[q % 3]
                        store(tok_n + n * (3 * MU) + q, q % 2, proj_c[bass.ds(n * UW + q // 3 * P, P), a:b], b - a)
                for s in range(2):
                    sp.wait_ge(stored[s], ST + 16 * (tok_n + chan_n) // 2)

            @block.gpsimd
            def _(pool):
                def load_w(n, s):
                    pool.wait_ge(w_lo, CR + n - 1)
                    pool.dma_start(raw[:, s], w_d[:, :, bass.ds(n * UW, UW)]).then_inc(w_in[s], 16)

                pool.dma_start(gamma[:], norm_mix.to_broadcast([P, D])).then_inc(gamma_in, 16)
                with pool.Fori(0, NT // 2) as i:
                    for s in range(2):
                        pool.wait_ge(x_ready, CR + 2 * i + s - 1)
                        pool.dma_start(xt[:, s], x_d[:, bass.ds(2 * i + s, 1)].rearrange("p n d -> p (n d)")).then_inc(x_in[s], 16)
                pool.dma_start(rraw[:], w_d[:, :, (NA + NB) * UW:(NA + NB) * UW + 2 * RANK]).then_inc(r_in, 16)
                load_w(0, 0)
                pool.wait_ge(h_lo, CR + NT)
                load_w(1, 1)
                with pool.Fori(1, (NB + NA) // 2) as i:
                    for s in range(2):
                        load_w(2 * i + s, s)
                load_w(NB + NA - 1, 0)

            @block.scalar
            def _(act):
                with act.Fori(0, NT // 2) as i:
                    for s in range(2):
                        n = 2 * i + s
                        act.wait_ge(x_in[s], 16 * i + 16)
                        act.activation(xn[:, s], xt[:, s], ACT.Square, accum_out=ssq[:, s:s + 1]).then_inc(squared, 1)
                        act.wait_ge(squared, CR + n + 1)
                        act.activation(root[:, s:s + 1], ssq[:, s:s + 1], ACT.Sqrt, scale=1.0 / D,
                                       bias=cst["eps"]).then_inc(rooted, 1)
                        act.wait_ge(turned, CR + n + 1)
                        act.activation(act_hl[:, 0, :, bass.ds(n * P, P)], turn_ps, ACT.Copy).then_inc(h_hi, 1)

                def hi(s, landed):
                    act.wait_ge(w_in[s], landed)
                    act.activation(whi[:, s], raw[:, s], ACT.Copy).then_inc(w_hi, 1)

                def evac(q, s, use, src, width):
                    act.wait_ge(p_full, CR + q + 1)
                    act.wait_ge(stored[s], ST + 16 * use)
                    act.activation(stage[:, s, 0:width], src, ACT.Copy).then_inc(p_out, 1)

                def evac_tok(n):
                    for t in range(NT):
                        evac(n * NT + t, t % 2, n * (NT // 2) + t // 2, ps_t[:, t % 2], UW)

                def evac_chan(n):
                    for q in range(3 * MU):
                        a, b = TOK3[q % 3]
                        evac(tok_n + n * (3 * MU) + q, q % 2, tok_n // 2 + n * (3 * MU // 2) + q // 2,
                             ps_c[:, q // 3 % 2, q % 3, 0:b - a], b - a)

                act.wait_ge(r_in, 16)
                act.activation(rhi[:], rraw[:], ACT.Copy).then_inc(r_hi, 1)
                hi(0, 16)
                hi(1, 16)
                with act.Fori(0, NB // 2) as i:
                    for s in range(2):
                        evac_tok(2 * i + s)
                        hi(s, 16 * i + 32)
                evac_tok(NB - 1)
                hi(0, 16 * (NB // 2) + 32)
                with act.Fori(0, NA // 2 - 1) as i:
                    for s in range(2):
                        evac_chan(2 * i + s)
                        hi(1 - s, 16 * i + 16 * (NB // 2 + 2 + s))
                for n in range(NA - 2, NA):
                    evac_chan(n)
                for d in range(2):
                    act.wait_ge(p_full, CR + tok_n + chan_n + 1)
                    act.activation(rT[d][:], ps_c[0:RANK, d].rearrange("p c n -> p (c n)")[:, 0:T], ACT.Copy).then_inc(p_out, 1)

            @block.vector
            def _(dve):
                dve.wait_ge(gamma_in, 16)
                with dve.Fori(0, NT // 2) as i:
                    for s in range(2):
                        n = 2 * i + s
                        dve.wait_ge(rooted, CR + n + 1)
                        dve.reciprocal(rstd[:, s:s + 1], root[:, s:s + 1]).then_inc(inverted, 1)
                        dve.wait_ge(inverted, CR + n + 1)
                        dve.scalar_tensor_tensor(out=xn[:, s], in0=xt[:, s], scalar=rstd[:, s:s + 1], in1=gamma[:],
                                                 op0=ALU.mult, op1=ALU.mult).then_inc(x_ready, 1)
                        dve.wait_ge(h_hi, CR + n + 1)
                        dve.tensor_tensor(act_hl[:, 1, :, bass.ds(n * P, P)], turn_ps,
                                          act_hl[:, 0, :, bass.ds(n * P, P)].bitcast(F32), ALU.subtract).then_inc(h_lo, 1)

                def lo(s, n):
                    dve.wait_ge(w_hi, CR + n + 1)
                    dve.tensor_tensor(wlo[:, s], raw[:, s], whi[:, s].bitcast(F32), ALU.subtract).then_inc(w_lo, 1)

                dve.wait_ge(r_hi, CR + 1)
                dve.tensor_tensor(rlo[:], rraw[:], rhi[:].bitcast(F32), ALU.subtract).then_inc(r_lo, 1)
                with dve.Fori(0, (NB + NA) // 2) as i:
                    for s in range(2):
                        lo(s, 2 * i + s)
                lo(0, NB + NA - 1)

            @block.tensor
            def _(pe):
                with pe.Fori(0, NT // 2) as i:
                    for s in range(2):
                        n = 2 * i + s
                        pe.wait_ge(x_ready, CR + n + 1)
                        pe.wait_ge(h_lo, CR + n)
                        for k in range(KC):
                            tr = pe.transpose(ps_c[:, 0, k // 4, k % 4 * P:k % 4 * P + P], xn[:, s, k * P:(k + 1) * P], cst["ident"])
                        tr.then_inc(turned, 1)
                pe.wait_ge(h_lo, CR + NT)

                def unit_tok(n, s):
                    pe.wait_ge(w_lo, CR + n + 1)
                    for t in range(NT):
                        pe.wait_ge(p_out, CR + n * NT + t - 1)
                        for k in range(KC):
                            mm = three_passes(pe, ps_t[:, t % 2], [act_hl[:, j, k, t * P:(t + 1) * P] for j in range(2)],
                                              (whi[:, s, k], wlo[:, s, k]), k == 0, k == KC - 1)
                        mm.then_inc(p_full, 1)

                def unit_chan(n, s):
                    pe.wait_ge(w_lo, CR + NB + n + 1)
                    for m in range(MU):
                        pe.wait_ge(p_out, CR + tok_n + (n * MU + m - 1) * 3)
                        channel_tile(pe, ps_c[:, m % 2], lambda j, k: (whi, wlo)[j][:, s, k, m * P:(m + 1) * P],
                                     lambda j, k, a, b: act_hl[:, j, k, a:b], p_full)

                with pe.Fori(0, NB // 2) as i:
                    for s in range(2):
                        unit_tok(2 * i + s, s)
                unit_tok(NB - 1, 0)
                with pe.Fori(0, NA // 2) as i:
                    for s in range(2):
                        unit_chan(2 * i + s, 1 - s)
                pe.wait_ge(r_lo, CR + 1)
                pe.wait_ge(p_out, CR + tok_n + chan_n)
                for d in range(2):
                    for c, (a, b) in enumerate(TOK3):
                        for k in range(KC):
                            cols = slice(d * RANK, (d + 1) * RANK)
                            mm = three_passes(pe, ps_c[0:RANK, d, c, 0:b - a], (rhi[:, k, cols], rlo[:, k, cols]),
                                              [act_hl[:, j, k, a:b] for j in range(2)], k == 0, k == KC - 1)
                mm.then_inc(p_full, 1)

        ph.clear()


def pairs(t, e):
    return t.rearrange("... (d e) -> ... d e", e=2)[..., e]


def keys(nc, proj_t, k_norm, cos, sin, cst, kT, vv):
    with ExitStack() as ctx:
        ph = Phase(nc, ctx, "ky")
        W = KVH * HD
        kv = ph.sb("kv", [P, NT, 2 * W])
        kn, kr = ph.sb("normed", [P, NT, KVH, HD]), ph.sb("rotated", [P, NT, KVH, HD])
        ka, kb = ph.sb("a", [P, NT, KVH, HD // 2]), ph.sb("b", [P, NT, KVH, HD // 2])
        tabs, gk = ph.sb("tables", [P, 2, NT, HD // 2]), ph.sb("g", [P, HD])
        ss, root, inv = (ph.sb(n, [P, NT, KVH]) for n in ("ss", "root", "inv"))
        ps = ph.ps("turned", [P, KVH, T])
        kv_in, tab_in = ph.landed("kv_in", 2), ph.landed("tab_in")
        step, summed, rooted, first, turned, k_hi, k_lo, v_hi, v_lo = ph.done(
            "step", "summed", "rooted", "first", "tp", "k_hid", "k_lod", "v_hid", "v_lod")
        k = kv[:, :, 0:W].rearrange("p n (h d) -> p n h d", d=HD)
        tab = [tabs[:, j].unsqueeze(2).broadcast_to([P, NT, KVH, HD // 2]) for j in range(2)]

        with nc.Block() as block:

            @block.sync
            def _(sp):
                ph.start(sp)
                for j in range(2):
                    half = slice(j * NT // 2, (j + 1) * NT // 2)
                    sp.dma_start(kv[:, half], proj_t.rearrange("(n p) c -> p n c", p=P)[:, half, G_KV * UW:(G_KV + 1) * UW]).then_inc(kv_in[j], 16)
                for j, src in enumerate((cos, sin)):
                    sp.dma_start(tabs[:, j], src.rearrange("(n p) d -> p n d", p=P)).then_inc(tab_in, 16)
                sp.dma_start(gk[:], k_norm.to_broadcast([P, HD])).then_inc(tab_in, 16)

            @block.scalar
            def _(act):
                act.wait_ge(kv_in[0], 16)
                act.wait_ge(kv_in[1], 16)
                act.activation(vv[:, 0], kv[:, :, W:2 * W], ACT.Copy).then_inc(v_hi, 1)
                act.wait_ge(summed, CR + 1)
                act.activation(root[:], ss[:], ACT.Sqrt, scale=1.0 / HD, bias=cst["eps"]).then_inc(rooted, 1)
                act.wait_ge(turned, CR + 1)
                act.activation(kT[:, 0], ps[:], ACT.Copy).then_inc(k_hi, 1)

            @block.gpsimd
            def _(pool):
                for e in range(2):
                    pool.wait_ge(step, CR + 3 + 2 * e)
                    pool.tensor_tensor(ka[:], pairs(kn[:], e), tab[0], ALU.mult).then_inc(first, 1)

            @block.vector
            def _(dve):
                dve.wait_ge(kv_in[0], 16)
                dve.wait_ge(kv_in[1], 16)
                dve.wait_ge(tab_in, 48)
                dve.tensor_tensor(kn[:], k, k, ALU.mult).then_inc(step, 1)
                dve.wait_ge(step, CR + 1)
                dve.tensor_reduce(ss[:], kn[:], AX.X, ALU.add).then_inc(summed, 1)
                dve.wait_ge(v_hi, CR + 1)
                dve.tensor_tensor(vv[:, 1], kv[:, :, W:2 * W], vv[:, 0].bitcast(F32), ALU.subtract).then_inc(v_lo, 1)
                dve.wait_ge(rooted, CR + 1)
                dve.reciprocal(inv[:], root[:]).then_inc(summed, 1)
                dve.wait_ge(summed, CR + 2)
                dve.tensor_tensor(kn[:], k, inv[:].unsqueeze(3).broadcast_to([P, NT, KVH, HD]), ALU.mult).then_inc(step, 1)
                dve.wait_ge(step, CR + 2)
                dve.tensor_tensor(kn[:], kn[:], gk[:].unsqueeze(1).unsqueeze(1).broadcast_to([P, NT, KVH, HD]), ALU.mult).then_inc(step, 1)
                dve.wait_ge(step, CR + 3)
                for e, op in ((0, ALU.subtract), (1, ALU.add)):
                    dve.tensor_tensor(kb[:], pairs(kn[:], 1 - e), tab[1], ALU.mult).then_inc(step, 1)
                    dve.wait_ge(step, CR + 4 + 2 * e)
                    dve.wait_ge(first, CR + 1 + e)
                    dve.tensor_tensor(pairs(kr[:], e), ka[:], kb[:], op).then_inc(step, 1)
                    dve.wait_ge(step, CR + 5 + 2 * e)
                dve.wait_ge(k_hi, CR + 1)
                dve.tensor_tensor(kT[:, 1], ps[:], kT[:, 0].bitcast(F32), ALU.subtract).then_inc(k_lo, 1)

            @block.tensor
            def _(pe):
                pe.wait_ge(step, CR + 7)
                for h in range(KVH):
                    for n in range(NT):
                        tr = pe.transpose(ps[:, h, n * P:(n + 1) * P], kr[:, n, h], cst["ident"])
                tr.then_inc(turned, 1)

        ph.clear()


def attention(nc, proj_t, q_norm, cos, sin, cst, kT, vv, act_hl):
    with ExitStack() as ctx:
        ph = Phase(nc, ctx, "at")
        qT = ph.sb("qT", [P, 2, AH, P], F32R)
        pT = ph.sb("pT", [P, 2, NTS, GR, P], F32R)
        prob = ph.sb("prob", [P, 2, TS])
        q_in, q_n, q_r = (ph.sb(n, [P, AH, HD]) for n in ("q_in", "q_normed", "q_rotated"))
        q_a, q_b = (ph.sb(n, [P, AH, HD // 2]) for n in ("q_a", "q_b"))
        tabs, gq, gqs = ph.sb("tables", [P, 2, NT, HD // 2]), ph.sb("g", [P, HD]), ph.sb("g_scaled", [P, HD])
        q_ss, q_root, q_inv = (ph.sb(n, [P, AH]) for n in ("q_ss", "q_root", "q_inv"))
        nmax, rsum, rinv = (ph.sb(n, [P, 2]) for n in ("nmax", "rsum", "rinv"))
        ps_s, ps_p = ph.ps("ps_scores", [P, 2, TS]), ph.ps("ps_probs", [P, 2, 4, P])
        ps_o, ps_q = ph.ps("ps_out", [P, GR, P]), ph.ps("ps_q", [P, GR, P])
        tab_in, q_land = ph.landed("tab_in"), ph.landed("q_land")
        g_ready, q_sq, q_sum, q_rt, q_iv, q_step, q_tp, q_hi, q_lo = ph.done(
            "g_ready", "q_sq", "q_sum", "q_rt", "q_iv", "q_step", "q_tp", "q_hid", "q_lod")
        s_full, s_max, s_exp, r_iv, p_ready = ph.done("s_full", "s_max", "s_exp", "r_iv", "p_ready")
        p_tp, p_hi, p_lo, o_full, o_hi, o_lo = ph.done("p_tp", "p_hid", "p_lod", "o_full", "o_hid", "o_lod")
        QS = 8

        def out_slots(n, g):
            if isinstance(n, int) and n >= NTS:
                dst = [act_hl[:, j, 2 * g + n - NTS::4, TS:].rearrange("p e (r q) -> p r q e", r=GR) for j in range(2)]
                return dst, ps_o[:].rearrange("p r (q e) -> p r q e", e=2)
            dst = [act_hl[:, j, bass.ds(n, 1), g:TS:2].rearrange("p o (r q) -> p (o r) q", r=GR) for j in range(2)]
            return dst, ps_o[:]

        def tiles(eng, body):
            with eng.Fori(0, NTS) as n:
                body(n, TS)
            for n in range(NTS, NT):
                body(n, TP)

        with nc.Block() as block:

            @block.sync
            def _(sp):
                ph.start(sp)
                for j, src in enumerate((cos, sin)):
                    sp.dma_start(tabs[:, j], src.rearrange("(n p) d -> p n d", p=P)).then_inc(tab_in, 16)
                sp.dma_start(gq[:], q_norm.to_broadcast([P, HD])).then_inc(tab_in, 16)

            @block.gpsimd
            def _(pool):
                def prepare(n, sl):
                    pool.dma_start(q_in[:].rearrange("p h d -> p (h d)"),
                                   proj_t.rearrange("(n p) c -> p n c", p=P)[:, sl, 0:AH * HD].rearrange("p n c -> p (n c)")
                                   ).then_inc(q_land, 16)
                    pool.wait_ge(q_land, 16 * n + 16)
                    pool.tensor_tensor(q_n[:], q_in[:], q_in[:], ALU.mult).then_inc(q_sq, 1)
                    pool.wait_ge(q_iv, CR + n + 1)
                    pool.tensor_tensor(q_n[:], q_in[:], q_inv[:].unsqueeze(2).broadcast_to([P, AH, HD]), ALU.mult).then_inc(q_step, 1)
                    b = CR + QS * n
                    pool.wait_ge(q_step, b + 1)
                    pool.tensor_tensor(q_n[:], q_n[:], gqs[:].unsqueeze(1).broadcast_to([P, AH, HD]), ALU.mult).then_inc(q_step, 1)
                    pool.wait_ge(q_step, b + 2)
                    pool.wait_ge(q_tp, CR + 2 * n)
                    pool.wait_ge(tab_in, 48)
                    cs, sn = (tabs[:, j, sl].broadcast_to([P, AH, HD // 2]) for j in range(2))
                    for e, op in ((0, ALU.subtract), (1, ALU.add)):
                        ph.settle(pool)
                        pool.tensor_tensor(q_a[:], pairs(q_n[:], e), cs, ALU.mult).then_inc(q_step, 1)
                        pool.tensor_tensor(q_b[:], pairs(q_n[:], 1 - e), sn, ALU.mult).then_inc(q_step, 1)
                        pool.wait_ge(q_step, b + 4 + 3 * e)
                        pool.tensor_tensor(pairs(q_r[:], e), q_a[:], q_b[:], op).then_inc(q_step, 1)
                        pool.wait_ge(q_step, b + 5 + 3 * e)

                pool.wait_ge(g_ready, CR + 1)
                with pool.Fori(0, NT) as n:
                    prepare(n, bass.ds(n, 1))

            @block.scalar
            def _(act):
                def q_norms(n):
                    act.wait_ge(q_sum, CR + n + 1)
                    act.activation(q_root[:], q_ss[:], ACT.Sqrt, scale=1.0 / HD, bias=cst["eps"]).then_inc(q_rt, 1)

                def q_high(n):
                    for g in range(2):
                        act.wait_ge(q_tp, CR + 2 * n + g + 1)
                        act.activation(qT[:, 0, GR * g:GR * g + GR], ps_q[:], ACT.Copy).then_inc(q_hi, 1)

                def exp(H, s, L):
                    act.wait_ge(s_max, CR + H + 1)
                    act.wait_ge(p_tp, CR + 2 * H - 2)
                    act.activation(prob[:, s, 0:L], ps_s[:, s, 0:L], ACT.Exp, bias=nmax[:, s:s + 1],
                                   accum_out=rsum[:, s:s + 1]).then_inc(s_exp, 1)

                def high(n, h, L):
                    H, hb = 8 * n + h, L // P // 2
                    for j in range(2):
                        act.wait_ge(p_tp, CR + 2 * H + j + 1)
                        act.wait_ge(o_full, CR + 2 * n + h // GR)
                        act.activation(pT[:, 0, hb * j:hb * j + hb, h % GR], ps_p[:, j, 0:hb], ACT.Copy).then_inc(p_hi, 1)

                def body(n, L):
                    more, L2 = not isinstance(n, int) or n < NT - 1, L
                    for h in range(AH):
                        H = 8 * n + h
                        if h < AH - 1:
                            exp(H + 1, (h + 1) % 2, L)
                        if h == 1 and more:
                            q_norms(n + 1)
                        if h == AH - 2 and more:
                            q_high(n + 1)
                        high(n, h, L)
                        if h % GR == GR - 1:
                            g = h // GR
                            dst, src = out_slots(n, g)
                            act.wait_ge(o_full, CR + 2 * n + g + 1)
                            act.activation(dst[0], src, ACT.Copy).then_inc(o_hi, 1)
                    if more:
                        exp(8 * n + 8, 0, TP if isinstance(n, int) else TS)

                q_norms(0)
                q_high(0)
                exp(0, 0, TS)
                with act.Fori(0, NTS - 1) as n:
                    body(n, TS)
                for n in range(NTS - 1, NT):
                    body(n, TS if n < NTS else TP)

            @block.vector
            def _(dve):
                def q_norms(n):
                    dve.wait_ge(q_sq, CR + n + 1)
                    dve.tensor_reduce(q_ss[:], q_n[:], AX.X, ALU.add).then_inc(q_sum, 1)

                def q_inverse(n):
                    dve.wait_ge(q_rt, CR + n + 1)
                    dve.reciprocal(q_inv[:], q_root[:]).then_inc(q_iv, 1)

                def q_low(n):
                    for g in range(2):
                        dve.wait_ge(q_hi, CR + 2 * n + g + 1)
                        sl = slice(GR * g, GR * g + GR)
                        dve.tensor_tensor(qT[:, 1, sl], ps_q[:], qT[:, 0, sl].bitcast(F32), ALU.subtract).then_inc(q_lo, 1)

                def row_max(H, s, L):
                    dve.wait_ge(s_full, CR + H + 1)
                    dve.wait_ge(s_exp, CR + H - 1)
                    dve.tensor_reduce(nmax[:, s:s + 1], ps_s[:, s, 0:L], AX.X, ALU.max, negate=True).then_inc(s_max, 1)

                def scale(H, s, L):
                    dve.wait_ge(s_exp, CR + H + 1)
                    dve.reciprocal(rinv[:, s:s + 1], rsum[:, s:s + 1]).then_inc(r_iv, 1)
                    dve.wait_ge(r_iv, CR + H + 1)
                    dve.tensor_scalar(prob[:, s, 0:L], prob[:, s, 0:L], rinv[:, s:s + 1], None, ALU.mult).then_inc(p_ready, 1)

                def low(n, h, L):
                    H, hb = 8 * n + h, L // P // 2
                    for j in range(2):
                        dve.wait_ge(p_hi, CR + 2 * H + j + 1)
                        dst = slice(hb * j, hb * j + hb)
                        dve.tensor_tensor(pT[:, 1, dst, h % GR], ps_p[:, j, 0:hb], pT[:, 0, dst, h % GR].bitcast(F32), ALU.subtract).then_inc(p_lo, 1)

                def body(n, L):
                    more = not isinstance(n, int) or n < NT - 1
                    for h in range(AH):
                        H = 8 * n + h
                        if h < AH - 1:
                            row_max(H + 1, (h + 1) % 2, L)
                        if h == 1 and more:
                            q_norms(n + 1)
                        if h == 2 and more:
                            q_inverse(n + 1)
                        if h == AH - 2 and more:
                            q_low(n + 1)
                        if h < AH - 1:
                            scale(H + 1, (h + 1) % 2, L)
                        low(n, h, L)
                        if h % GR == GR - 1:
                            g = h // GR
                            dst, src = out_slots(n, g)
                            dve.wait_ge(o_hi, CR + 2 * n + g + 1)
                            dve.tensor_tensor(dst[1], src, dst[0].bitcast(F32), ALU.subtract).then_inc(o_lo, 1)
                    if more:
                        L2 = TP if isinstance(n, int) else TS
                        row_max(8 * n + 8, 0, L2)
                        scale(8 * n + 8, 0, L2)

                dve.wait_ge(tab_in, 48)
                dve.tensor_scalar(gqs[:], gq[:], float(HD) ** -0.5, None, ALU.mult).then_inc(g_ready, 1)
                q_norms(0)
                q_inverse(0)
                q_low(0)
                row_max(0, 0, TS)
                scale(0, 0, TS)
                with dve.Fori(0, NTS - 1) as n:
                    body(n, TS)
                for n in range(NTS - 1, NT):
                    body(n, TS if n < NTS else TP)

            @block.tensor
            def _(pe):
                def turn_q(n):
                    pe.wait_ge(q_step, CR + QS * n + QS)
                    for g in range(2):
                        pe.wait_ge(q_lo, CR + 2 * n + g)
                        for r in range(GR):
                            tr = pe.transpose(ps_q[:, r], q_r[:, GR * g + r], cst["ident"])
                        tr.then_inc(q_tp, 1)

                def scores(n, h, L):
                    H = 8 * n + h
                    k0 = 0 if L == TS else TS
                    pe.wait_ge(q_lo, CR + 2 * n + h // GR + 1)
                    pe.wait_ge(s_exp, CR + H - 1)
                    for c in range(0, L, 512):
                        w = min(512, L)
                        mm = three_passes(pe, ps_s[:, h % 2, c:c + w], [qT[:, j, h] for j in range(2)],
                                          [kT[:, j, h // GR, k0 + c:k0 + c + w] for j in range(2)], True, True)
                    mm.then_inc(s_full, 1)

                def turn_p(n, h, L):
                    H, hb = 8 * n + h, L // P // 2
                    pe.wait_ge(p_ready, CR + H + 1)
                    for j in range(2):
                        pe.wait_ge(p_lo, CR + 2 * H + j - 1)
                        for b in range(hb):
                            kb = hb * j + b
                            tr = pe.transpose(ps_p[:, j, b], prob[:, h % 2, kb * P:(kb + 1) * P], cst["ident"])
                        tr.then_inc(p_tp, 1)

                def values(n, g, L):
                    pe.wait_ge(p_lo, CR + 16 * n + 8 * g + 8)
                    pe.wait_ge(o_lo, CR + 2 * n + g)
                    kb0, nk = (0, NTS) if L == TS else (NTS, NT - NTS)
                    for b in range(nk):
                        mm = three_passes(pe, ps_o[:], [vv[:, j, kb0 + b, g * HD:(g + 1) * HD] for j in range(2)],
                                          [pT[:, j, b] for j in range(2)], b == 0, b == nk - 1)
                    mm.then_inc(o_full, 1)

                def body(n, L):
                    more = not isinstance(n, int) or n < NT - 1
                    for h in range(AH):
                        if h < AH - 1:
                            scores(n, h + 1, L)
                        if h == AH - 2 and more:
                            turn_q(n + 1)
                        turn_p(n, h, L)
                        if h % GR == GR - 1:
                            values(n, h // GR, L)
                    if more:
                        scores(n + 1, 0, TP if isinstance(n, int) else TS)

                turn_q(0)
                scores(0, 0, TS)
                with pe.Fori(0, NTS - 1) as n:
                    body(n, TS)
                for n in range(NTS - 1, NT):
                    body(n, TS if n < NTS else TP)

        ph.clear()


def mix(nc, tag, act_hl, w, z_rows, out, add=None):
    with ExitStack() as ctx:
        ph = Phase(nc, ctx, tag)
        WC = 2 * P
        raw = ph.sb("w_raw", [P, 2, KC, WC])
        whl = [ph.sb(n, [P, 2, KC, WC], F32R) for n in ("w_hi", "w_lo")]
        z, sig, o = ph.sb("z", [P, 2, T]), ph.sb("sig", [P, 2, T]), ph.sb("o", [P, 2, T])
        extra = ph.sb("add", [P, 2, T]) if add is not None else None
        ps = ph.ps("ps", [P, 2, 4, 512])
        w_in, z_in, a_in = ph.landed("w_in", 2), ph.landed("z_in", 2), ph.landed("a_in", 2)
        w_hi, w_lo, full, sig_done, gated, summed = ph.done("w_hid", "w_lod", "full", "sig_done", "gated", "summed")
        stored = ph.stored("stored", 2)
        w_d = w.rearrange("(k p) c -> p k c", p=P)
        NU, PU = D // WC, WC // P
        ready = summed if add is not None else gated

        NT8 = D // P
        units = [(u, u % 2) for u in range(NU)]
        tiles = [(t, t % 2, t // PU, t % PU) for t in range(NT8)]

        with nc.Block() as block:

            @block.sync
            def _(sp):
                ph.start(sp)
                for t, s, _u, _m in tiles:
                    sp.wait_ge(ready, CR + t + 1)
                    sp.dma_start(out[t * P:(t + 1) * P], o[:, s]).then_inc(stored[s], 16)
                for s in range(2):
                    sp.wait_ge(stored[s], ST + 16 * NT8 // 2)

            @block.gpsimd
            def _(pool):
                for u, s in units:
                    pool.wait_ge(w_lo, CR + u - 1)
                    pool.dma_start(raw[:, s], w_d[:, :, u * WC:(u + 1) * WC]).then_inc(w_in[s], 16)
                    for t in range(u * PU, (u + 1) * PU):
                        pool.wait_ge(gated, CR + t - 1)
                        pool.dma_start(z[:, t % 2], z_rows[t * P:(t + 1) * P]).then_inc(z_in[t % 2], 16)
                        if add is not None:
                            pool.wait_ge(summed, CR + t - 1)
                            pool.dma_start(extra[:, t % 2], add[t * P:(t + 1) * P]).then_inc(a_in[t % 2], 16)

            @block.scalar
            def _(act):
                def high(u, s):
                    act.wait_ge(w_in[s], 16 * (u // 2) + 16)
                    if u >= 2:
                        act.wait_ge(full, CR + (u - 1) * PU * 3)
                    act.activation(whl[0][:, s], raw[:, s], ACT.Copy).then_inc(w_hi, 1)

                high(0, 0)
                for t, s, u, m in tiles:
                    if m == 0 and u + 1 < NU:
                        high(u + 1, (u + 1) % 2)
                    act.wait_ge(z_in[s], 16 * (t // 2) + 16)
                    act.wait_ge(gated, CR + t - 1)
                    act.activation(sig[:, s], z[:, s], ACT.Sigmoid).then_inc(sig_done, 1)

            @block.vector
            def _(dve):
                def low(u, s):
                    dve.wait_ge(w_hi, CR + u + 1)
                    dve.tensor_tensor(whl[1][:, s], raw[:, s], whl[0][:, s].bitcast(F32), ALU.subtract).then_inc(w_lo, 1)

                low(0, 0)
                for t, s, u, m in tiles:
                    if m == 0 and u + 1 < NU:
                        low(u + 1, (u + 1) % 2)
                    dve.wait_ge(sig_done, CR + t + 1)
                    dve.wait_ge(full, CR + 3 * t + 3)
                    dve.wait_ge(stored[s], ST + 16 * (t // 2))
                    dve.tensor_tensor(o[:, s], ps[:, s, 0:3].rearrange("p c n -> p (c n)")[:, 0:T], sig[:, s], ALU.mult).then_inc(gated, 1)
                    if add is not None:
                        dve.wait_ge(gated, CR + t + 1)
                        dve.wait_ge(a_in[s], 16 * (t // 2) + 16)
                        dve.tensor_tensor(o[:, s], o[:, s], extra[:, s], ALU.add).then_inc(summed, 1)

            @block.tensor
            def _(pe):
                for t, s, u, m in tiles:
                    if m == 0:
                        pe.wait_ge(w_lo, CR + u + 1)
                    pe.wait_ge(gated, CR + t - 1)
                    channel_tile(pe, ps[:, s], lambda j, k: whl[j][:, u % 2, k, m * P:(m + 1) * P],
                                 lambda j, k, a, b: act_hl[:, j, k, a:b], full)

        ph.clear()


def gla(nc, proj_t, proj_c, wg, bg, g_norm, masks, rT, cst, act_hl):
    with ExitStack() as ctx:
        ph = Phase(nc, ctx, "gl")
        qk = ph.sb("qk", [P, 2, T])
        v, g = ph.sb("v", [P, NT, DV]), ph.sb("g", [P, NT, DV])
        wgate, bias = ph.sb("w_gate", [RANK, 2, DK]), ph.sb("bias", [P, 2])
        gnorm = ph.sb("gnorm", [P, DV])
        starts = ph.sb("starts", [P, T + CH], BF16)
        mask = ph.sb("mask", [P, 2, P], U8)
        z, b, e = ph.sb("z", [P, T]), ph.sb("b", [P, T]), ph.sb("e", [P, T])
        decay = ph.sb("decay", [P, 2, NCH])
        qt, kt = ph.sb("q_t", [P, 2, T]), ph.sb("k_t", [P, 2, T])
        khT = ph.sb("k_hat_turned", [P, NT, DK])
        S = ph.sb("states", [P, 2, NCH - 1, DV])
        A = ph.sb("A", [P, 2, 2, P])
        Asum = e[:, 0:2 * P].rearrange("p (s n) -> p s n", s=2)
        o_n = z[:, 0:2 * DV].rearrange("p (s n) -> p s n", s=2)
        oss, oroot, oinv = (ph.sb(n, [P, 2]) for n in ("oss", "oroot", "oinv"))
        pp = ph.ps("ps", [P, 8, 512])
        gate_ps = pp[:, 0:3].rearrange("p c n -> p (c n)")[:, 0:T]
        kh_ps = pp[:, 5:8].rearrange("p c n -> p (c n)")[:, 0:T]
        u_ps, a_ps = [pp[:, 3, 0:DV], pp[:, 4, 0:DV]], [pp[:, 5], pp[:, 6]]
        o_ps, t_ps = u_ps, pp[:, 7, 0:DV].rearrange("p (c t) -> p c t", c=2)
        const_in, qk_in, v_in, g_in, w_in = (ph.landed(n) for n in ("const_in", "qk_in", "v_in", "g_in", "w_in"))
        set_up, gates, z_done, m_step, lg_done, b_done, d_done, e_done, dec_done = ph.done(
            "set_up", "gates", "z_done", "m_step", "lg_done", "b_done", "d_done", "e_done", "dec_done")
        q_prod, k_prod, kh_tp, kh_out, u_full, moved, silu_done = ph.done(
            "q_prod", "k_prod", "kh_tp", "kh_out", "u_full", "moved", "silu_done")
        a_full, a_cut, a_sum, o_full, ssd, rooted, o_inv, o_scaled, o_ready, o_tp, o_hi, o_lo = ph.done(
            "a_full", "a_cut", "a_sum", "o_full", "ssd", "rooted", "o_iv", "o_scaled", "o_ready", "o_tp", "o_hid", "o_lod")
        NU = NCH - 2
        order = [list(range(NCH)), list(range(NCH - 1, -1, -1))]
        begins = [(0, NCHS), (NCH - 1, NCHS - 1)]
        ends = [(NCHS - 1, NCH - 1), (NCHS, 0)]
        chunks = lambda t: t.rearrange("p (c n) -> p c n", n=CH)
        chunk_end = lambda t, d: chunks(t)[:, :, CH - 1 if d == 0 else 0]
        state = lambda d, c: S[:, d, c - 1 + d]

        def updates(d):
            return [(n, c) for n, c in enumerate(c for c in order[d] if c not in ends[d])]

        with nc.Block() as block:

            @block.sync
            def _(sp):
                ph.start(sp)
                sp.dma_start(A[:, 0], masks.rearrange("m p n -> p m n")).then_inc(const_in, 16)
                sp.dma_start(gnorm[:], g_norm.to_broadcast([P, DV])).then_inc(const_in, 16)
                with sp.Fori(0, GH) as i:
                    sp.wait_ge(q_prod, CR + 2 * i)
                    sp.wait_ge(k_prod, CR + 4 * i)
                    for j, row in enumerate((C_Q, C_K)):
                        sp.dma_start(qk[:, j], proj_c[bass.ds(i * DK + row, DK)]).then_inc(qk_in, 16)
                    sp.wait_ge(z_done, CR + 2 * i)
                    ph.settle(sp)
                    for d in range(2):
                        sp.dma_start(wgate[:, d], wg[d][:, bass.ds(i * DK, DK)]).then_inc(w_in, 16)
                        sp.dma_start(bias[:, d:d + 1], bg[d].rearrange("o (p u) -> (o p) u", u=1)[bass.ds(i * DK, DK)]).then_inc(w_in, 16)
                    sp.wait_ge(o_full, CR + NT * i)
                    sp.wait_ge(o_ready, CR + NT * i)
                    for dst, grp, s in ((v, G_V, v_in), (g, G_G, g_in)):
                        src = proj_t.rearrange("(n p) c -> p n c", p=P)
                        sp.dma_start(dst[:], src[:, :, bass.ds(i * DV + grp * UW, DV)]).then_inc(s, 16)

            @block.gpsimd
            def _(pool):
                def add_scores(i, t):
                    pool.wait_ge(a_cut, CR + 2 * (NT * i + t) + 2)
                    pool.wait_ge(o_full, CR + NT * i + t - 1)
                    pool.tensor_tensor(Asum[:, t % 2], A[:, t % 2, 0], A[:, t % 2, 1], ALU.add).then_inc(a_sum, 1)

                def gate(i, t):
                    pool.wait_ge(o_scaled, CR + NT * i + t + 1)
                    pool.tensor_tensor(o_n[:, t % 2], o_n[:, t % 2], g[:, t], ALU.mult).then_inc(o_ready, 1)

                with pool.Fori(0, GH) as i:
                    pool.wait_ge(qk_in, 32 * i + 32)
                    pool.wait_ge(a_full, CR + NT * i)
                    for d in range(2):
                        pool.wait_ge(e_done, CR + 6 * i + 3 * d + 2)
                        pool.tensor_tensor(kt[:, d], qk[:, 1], e[:], ALU.mult).then_inc(k_prod, 1)
                        pool.wait_ge(e_done, CR + 6 * i + 3 * d + 3)
                        pool.wait_ge(dec_done, CR + 2 * i + d + 1)
                        pool.tensor_tensor(b[:], qk[:, 1], e[:], ALU.mult).then_inc(k_prod, 1)
                    pool.wait_ge(silu_done, CR + i + 1)
                    add_scores(i, 0)
                    for t in range(NT):
                        if t + 1 < NT:
                            add_scores(i, t + 1)
                        gate(i, t)

            @block.scalar
            def _(act):
                with act.Fori(0, GH) as i:
                    act.wait_ge(w_in, 64 * i + 64)
                    for d in range(2):
                        q = 2 * i + d
                        act.wait_ge(gates, CR + q + 1)
                        act.activation(z[:], gate_ps, ACT.Identity, bias=bias[:, d:d + 1]).then_inc(z_done, 1)
                        act.wait_ge(z_done, CR + q + 1)
                        act.wait_ge(k_prod, CR + 2 * q)
                        act.activation(e[:], z[:], ACT.Abs).then_inc(m_step, 1)
                        act.wait_ge(m_step, CR + 3 * q + 1)
                        act.activation(e[:], e[:], ACT.Exp, scale=-1.0).then_inc(m_step, 1)
                        act.wait_ge(m_step, CR + 3 * q + 2)
                        act.activation(e[:], e[:], ACT.Ln, bias=cst["one"]).then_inc(m_step, 1)
                        act.wait_ge(b_done, CR + q + 1)
                        act.wait_ge(moved, CR + 2 * NU * i)
                        act.activation(decay[:, d], chunk_end(b[:], d), ACT.Exp, scale=1.0 / GATE_NORM).then_inc(dec_done, 1)
                        act.activation(e[:], b[:], ACT.Exp, scale=1.0 / GATE_NORM).then_inc(e_done, 1)
                        act.wait_ge(q_prod, CR + q + 1)
                        act.activation(e[:], b[:], ACT.Exp, scale=-1.0 / GATE_NORM).then_inc(e_done, 1)
                        act.wait_ge(k_prod, CR + 2 * q + 1)
                        act.wait_ge(d_done, CR + q + 1)
                        act.activation(e[:], z[:], ACT.Exp, scale=1.0 / GATE_NORM).then_inc(e_done, 1)
                        act.wait_ge(kh_tp, CR + q + 1)
                        act.activation(khT[:], kh_ps, ACT.Copy).then_inc(kh_out, 1)
                    act.wait_ge(g_in, 16 * i + 16)
                    act.activation(g[:], g[:], ACT.Silu).then_inc(silu_done, 1)

                    def high(t):
                        act.wait_ge(o_tp, CR + NT * i + t + 1)
                        act.activation(act_hl[:, 0, bass.ds(2 * i, 2), t * P:(t + 1) * P], t_ps, ACT.Copy).then_inc(o_hi, 1)

                    for t in range(NT):
                        n, s = NT * i + t, t % 2
                        act.wait_ge(o_full, CR + n + 1)
                        act.wait_ge(o_tp, CR + n - 1)
                        act.activation(o_n[:, s], o_ps[s], ACT.Square, accum_out=oss[:, s:s + 1]).then_inc(ssd, 1)
                        act.wait_ge(ssd, CR + n + 1)
                        act.activation(oroot[:, s:s + 1], oss[:, s:s + 1], ACT.Sqrt, scale=1.0 / DV, bias=cst["eps"]).then_inc(rooted, 1)
                        if t > 0:
                            high(t - 1)
                    high(NT - 1)

            @block.vector
            def _(dve):
                dve.memset(starts[:], 1.0).then_inc(set_up, 1)
                dve.wait_ge(const_in, 32)
                dve.tensor_copy(mask[:], A[:, 0]).then_inc(set_up, 1)
                dve.wait_ge(set_up, CR + 2)
                dve.memset(A[:], 0.0).then_inc(set_up, 1)
                dve.memset(starts[:, ::CH], 0.0).then_inc(set_up, 1)
                dve.wait_ge(set_up, CR + 4)
                with dve.Fori(0, GH) as i:
                    dve.wait_ge(qk_in, 32 * i + 32)
                    for d in range(2):
                        q = 2 * i + d
                        dve.wait_ge(m_step, CR + 3 * q + 3)
                        dve.scalar_tensor_tensor(out=z[:], in0=z[:], scalar=0.0, in1=e[:], op0=ALU.min, op1=ALU.subtract).then_inc(lg_done, 1)
                        dve.wait_ge(lg_done, CR + q + 1)
                        dve.wait_ge(kh_tp, CR + q)
                        if d == 0:
                            dve.tensor_tensor_scan(b[:], starts[:, 0:T], z[:], 0.0, ALU.mult, ALU.add).then_inc(b_done, 1)
                        else:
                            dve.tensor_tensor_scan(b[:, ::-1], starts[:, 1:T + 1][:, ::-1], z[:, ::-1], 0.0, ALU.mult, ALU.add).then_inc(b_done, 1)
                        dve.wait_ge(b_done, CR + q + 1)
                        dve.tensor_tensor(chunks(z[:]), chunk_end(b[:], d).unsqueeze(2).broadcast_to([P, NCH, CH]), chunks(b[:]), ALU.subtract).then_inc(d_done, 1)
                        dve.wait_ge(e_done, CR + 3 * q + 1)
                        dve.wait_ge(a_full, CR + NT * i)
                        dve.wait_ge(o_full, CR + NT * i)
                        dve.scalar_tensor_tensor(out=qt[:, d], in0=qk[:, 0], scalar=float(DK) ** -0.5, in1=e[:],
                                                 op0=ALU.mult, op1=ALU.mult).then_inc(q_prod, 1)
                        dve.wait_ge(dec_done, CR + q + 1)
                        for n, c in updates(d):
                            u = NU * q + n
                            dve.wait_ge(u_full, CR + u + 1)
                            dve.wait_ge(moved, CR + u)
                            new = state(d, c + 1 - 2 * d)
                            if c in begins[d]:
                                dve.tensor_copy(new, u_ps[n % 2]).then_inc(moved, 1)
                            else:
                                dve.scalar_tensor_tensor(out=new, in0=state(d, c), scalar=decay[:, d, c:c + 1], in1=u_ps[n % 2],
                                                         op0=ALU.mult, op1=ALU.add).then_inc(moved, 1)

                    def cut(t):
                        n, s = NT * i + t, t % 2
                        dve.wait_ge(a_full, CR + n + 1)
                        dve.wait_ge(a_sum, CR + n - 1)
                        ph.settle(dve)
                        for d in range(2):
                            dve.copy_predicated(A[:, s, d], mask[:, d], a_ps[s][:, d * P:(d + 1) * P]).then_inc(a_cut, 1)

                    def low(t):
                        dve.wait_ge(o_hi, CR + NT * i + t + 1)
                        dst = [act_hl[:, j, bass.ds(2 * i, 2), t * P:(t + 1) * P] for j in range(2)]
                        dve.tensor_tensor(dst[1], t_ps, dst[0].bitcast(F32), ALU.subtract).then_inc(o_lo, 1)

                    cut(0)
                    for t in range(NT):
                        n, s = NT * i + t, t % 2
                        if t + 1 < NT:
                            cut(t + 1)
                        dve.wait_ge(rooted, CR + n + 1)
                        dve.reciprocal(oinv[:, s:s + 1], oroot[:, s:s + 1]).then_inc(o_inv, 1)
                        dve.wait_ge(o_inv, CR + n + 1)
                        dve.scalar_tensor_tensor(out=o_n[:, s], in0=o_ps[s], scalar=oinv[:, s:s + 1], in1=gnorm[:],
                                                 op0=ALU.mult, op1=ALU.mult).then_inc(o_scaled, 1)
                        if t > 0:
                            low(t - 1)
                    low(NT - 1)

            @block.tensor
            def _(pe):
                with pe.Fori(0, GH) as i:
                    pe.wait_ge(w_in, 64 * i + 64)

                    def gate_logits(d):
                        pe.wait_ge(z_done, CR + 2 * i + d)
                        for c, (a, w) in enumerate(TOK3):
                            mm = pe.matmul(pp[:, c, 0:w - a], wgate[:, d], rT[d][:, a:w], start=True, stop=True)
                        mm.then_inc(gates, 1)

                    gate_logits(0)
                    for d in range(2):
                        q = 2 * i + d
                        pe.wait_ge(k_prod, CR + 2 * q + 2)
                        pe.wait_ge(kh_out, CR + q)
                        pe.wait_ge(a_cut, CR + 2 * NT * i)
                        pe.wait_ge(o_lo, CR + NT * i)
                        for t in range(NT):
                            tr = pe.transpose(kh_ps[:, t * P:(t + 1) * P], b[:, t * P:(t + 1) * P], cst["ident"])
                        tr.then_inc(kh_tp, 1)
                        if d == 0:
                            gate_logits(1)
                        pe.wait_ge(kh_out, CR + q + 1)
                        pe.wait_ge(v_in, 16 * i + 16)
                        pe.wait_ge(o_scaled, CR + NT * i)
                        for n, c in updates(d):
                            rows = slice(c % 2 * CH, c % 2 * CH + CH)
                            pe.wait_ge(moved, CR + NU * q + n - 1)
                            pe.matmul(u_ps[n % 2], khT[rows, c // 2], v[rows, c // 2], start=True, stop=True).then_inc(u_full, 1)

                    def scores(t):
                        pe.wait_ge(a_cut, CR + 2 * (NT * i + t) - 2)
                        tok = slice(t * P, (t + 1) * P)
                        for d in range(2):
                            mm = pe.matmul(a_ps[t % 2][:, d * P:(d + 1) * P], kt[:, d, tok], qt[:, d, tok], start=True, stop=True)
                        mm.then_inc(a_full, 1)

                    def output(t):
                        out = o_ps[t % 2]
                        pe.wait_ge(a_sum, CR + NT * i + t + 1)
                        pe.wait_ge(o_scaled, CR + NT * i + t - 1)
                        parts = [(d, c) for c in (2 * t, 2 * t + 1) for d in range(2) if c not in begins[d]]
                        pe.matmul(out, Asum[:, t % 2], v[:, t], start=True, stop=False, skip_group_check=True)
                        for d, c in parts:
                            rows = slice(c % 2 * CH, c % 2 * CH + CH)
                            mm = pe.matmul(out[rows], qt[:, d, c * CH:(c + 1) * CH], state(d, c), start=False,
                                           stop=(d, c) == parts[-1], skip_group_check=True)
                        mm.then_inc(o_full, 1)

                    def turn(t):
                        n = NT * i + t
                        pe.wait_ge(o_ready, CR + n + 1)
                        pe.wait_ge(o_lo, CR + n)
                        for c in range(2):
                            tr = pe.transpose(t_ps[:, c], o_n[:, t % 2, c * P:(c + 1) * P], cst["ident"])
                        tr.then_inc(o_tp, 1)

                    pe.wait_ge(q_prod, CR + 2 * i + 2)
                    pe.wait_ge(moved, CR + 2 * NU * i + 2 * NU)
                    scores(0)
                    for t in range(NT):
                        if t + 1 < NT:
                            scores(t + 1)
                        output(t)
                        if t > 0:
                            turn(t - 1)
                    turn(NT - 1)

        ph.clear()


def finish_mixer(nc, x, merged, w_out, norm_ffn, w_router, cst, y, h2, affT):
    with ExitStack() as ctx:
        ph = Phase(nc, ctx, "fm")
        WC = 256
        NU = D // WC
        raw = ph.sb("w_raw", [P, 2, KC, WC])
        whl = [ph.sb(n, [P, KC, D], F32R) for n in ("w_hi", "w_lo")]
        wr, gamma = ph.sb("w_router", [P, KC, NE]), ph.sb("gamma", [P, D])
        mg = ph.sb("merged", [P, 2, KC, P])
        mhl = [ph.sb(n, [P, 2, KC, P], F32R) for n in ("m_hi", "m_lo")]
        xt, x1, hn = (ph.sb(n, [P, 2, D]) for n in ("x", "x1", "hn"))
        hT = ph.sb("hT", [P, KC, P])
        ssq, root, inv = (ph.sb(n, [P, 2]) for n in ("ssq", "root", "inv"))
        rmax, rsum, rinv, aff = ph.sb("rmax", [P, 1]), ph.sb("rsum", [P, 1]), ph.sb("rinv", [P, 1]), ph.sb("aff", [P, NE])
        ps_x, ps_h = ph.ps("ps_x", [P, 2, D]), ph.ps("ps_h", [P, KC, P])
        ps_r, ps_a = ph.ps("ps_r", [P, 512]), ph.ps("ps_a", [P, 512])
        w_in, c_in, m_in, x_in = ph.landed("w_in", 2), ph.landed("c_in"), ph.landed("m_in", 2), ph.landed("x_in", 2)
        w_hi, w_lo, m_hi, m_lo, x_full, x1_done, ssd, rooted, inv_done, hn_done = ph.done(
            "w_hid", "w_lod", "m_hid", "m_lod", "x_full", "x1_done", "ssd", "rooted", "inv_done", "hn_done")
        h_tp, h_out, r_full, r_max, r_exp, r_inv, a_done, a_tp, a_out = ph.done(
            "h_tp", "h_out", "r_full", "r_max", "r_exp", "r_iv", "a_done", "a_tp", "a_out")
        y_st, h_st = ph.stored("y_st", 2), ph.stored("h_st", 2)
        rows = lambda t: t.rearrange("(n p) d -> p n d", p=P)
        x_d, y_d, h_d = rows(x), rows(y), rows(h2)
        w_d = w_out.rearrange("(k p) c -> p k c", p=P)
        m_d = merged.rearrange("(k p) (n t) -> p k n t", p=P, t=P)

        def tiles(eng, body):
            with eng.Fori(0, NT // 2) as i:
                for s in range(2):
                    body(2 * i + s, s, i)

        with nc.Block() as block:

            @block.sync
            def _(sp):
                ph.start(sp)

                def body(n, s, i):
                    sp.wait_ge(x1_done, CR + n + 1)
                    sp.dma_start(y_d[:, bass.ds(n, 1)].rearrange("p o d -> p (o d)"), x1[:, s]).then_inc(y_st[s], 16)
                    sp.wait_ge(hn_done, CR + n + 1)
                    sp.dma_start(h_d[:, bass.ds(n, 1)].rearrange("p o d -> p (o d)"), hn[:, s]).then_inc(h_st[s], 16)

                tiles(sp, body)
                for s in range(2):
                    sp.wait_ge(y_st[s], ST + 16 * NT // 2)
                    sp.wait_ge(h_st[s], ST + 16 * NT // 2)

            @block.gpsimd
            def _(pool):
                pool.dma_start(gamma[:], norm_ffn.to_broadcast([P, D])).then_inc(c_in, 16)
                pool.dma_start(wr[:], w_router.rearrange("(k p) e -> p k e", p=P)).then_inc(c_in, 16)
                for u in range(NU):
                    pool.wait_ge(w_lo, CR + u - 1)
                    pool.dma_start(raw[:, u % 2], w_d[:, :, u * WC:(u + 1) * WC]).then_inc(w_in[u % 2], 16)

                def body(n, s, i):
                    pool.wait_ge(m_lo, CR + n - 1)
                    for k in range(KC):
                        pool.dma_start(mg[:, s, k], m_d[:, k, bass.ds(n, 1)].rearrange("p o t -> p (o t)")).then_inc(m_in[s], 16)
                    pool.wait_ge(x1_done, CR + n - 1)
                    pool.dma_start(xt[:, s], x_d[:, bass.ds(n, 1)].rearrange("p o d -> p (o d)")).then_inc(x_in[s], 16)

                tiles(pool, body)

            @block.scalar
            def _(act):
                for u in range(NU):
                    act.wait_ge(w_in[u % 2], 16 * (u // 2) + 16)
                    act.activation(whl[0][:, :, u * WC:(u + 1) * WC], raw[:, u % 2], ACT.Copy).then_inc(w_hi, 1)

                def high(n, s, i):
                    act.wait_ge(m_in[s], 16 * KC * i + 16 * KC)
                    act.wait_ge(x_full, CR + n - 1)
                    act.activation(mhl[0][:, s], mg[:, s], ACT.Copy).then_inc(m_hi, 1)

                def body(n, s, i):
                    high(n, s, i)
                    act.wait_ge(x1_done, CR + n + 1)
                    act.wait_ge(h_st[s], ST + 16 * i)
                    act.wait_ge(h_tp, CR + n - 1)
                    act.activation(hn[:, s], x1[:, s], ACT.Square, accum_out=ssq[:, s:s + 1]).then_inc(ssd, 1)
                    act.wait_ge(ssd, CR + n + 1)
                    act.activation(root[:, s:s + 1], ssq[:, s:s + 1], ACT.Sqrt, scale=1.0 / D, bias=cst["eps"]).then_inc(rooted, 1)
                    act.wait_ge(h_tp, CR + n + 1)
                    act.wait_ge(r_full, CR + n)
                    act.activation(hT[:], ps_h[:], ACT.Copy).then_inc(h_out, 1)
                    act.wait_ge(r_max, CR + n + 1)
                    act.activation(aff[:], ps_r[:, 0:NE], ACT.Exp, bias=rmax[:], accum_out=rsum[:]).then_inc(r_exp, 1)
                    act.wait_ge(a_tp, CR + n + 1)
                    act.activation(affT[:, bass.ds(n * P, P)], ps_a[0:NE, 0:P], ACT.Copy).then_inc(a_out, 1)

                tiles(act, body)

            @block.vector
            def _(dve):
                for u in range(NU):
                    cols = slice(u * WC, (u + 1) * WC)
                    dve.wait_ge(w_hi, CR + u + 1)
                    dve.tensor_tensor(whl[1][:, :, cols], raw[:, u % 2], whl[0][:, :, cols].bitcast(F32), ALU.subtract).then_inc(w_lo, 1)
                dve.wait_ge(c_in, 32)

                def body(n, s, i):
                    dve.wait_ge(m_hi, CR + n + 1)
                    dve.tensor_tensor(mhl[1][:, s], mg[:, s], mhl[0][:, s].bitcast(F32), ALU.subtract).then_inc(m_lo, 1)
                    dve.wait_ge(x_full, CR + n + 1)
                    dve.wait_ge(x_in[s], 16 * i + 16)
                    dve.wait_ge(y_st[s], ST + 16 * i)
                    dve.tensor_tensor(x1[:, s], ps_x[:, s], xt[:, s], ALU.add).then_inc(x1_done, 1)
                    dve.wait_ge(rooted, CR + n + 1)
                    dve.reciprocal(inv[:, s:s + 1], root[:, s:s + 1]).then_inc(inv_done, 1)
                    dve.wait_ge(inv_done, CR + n + 1)
                    dve.scalar_tensor_tensor(out=hn[:, s], in0=x1[:, s], scalar=inv[:, s:s + 1], in1=gamma[:],
                                             op0=ALU.mult, op1=ALU.mult).then_inc(hn_done, 1)
                    dve.wait_ge(r_full, CR + n + 1)
                    dve.tensor_reduce(rmax[:], ps_r[:, 0:NE], AX.X, ALU.max, negate=True).then_inc(r_max, 1)
                    dve.wait_ge(r_exp, CR + n + 1)
                    dve.reciprocal(rinv[:], rsum[:]).then_inc(r_inv, 1)
                    dve.wait_ge(r_inv, CR + n + 1)
                    dve.tensor_scalar(aff[:], aff[:], rinv[:], None, ALU.mult).then_inc(a_done, 1)

                tiles(dve, body)

            @block.tensor
            def _(pe):
                pe.wait_ge(w_lo, CR + NU)
                pe.wait_ge(c_in, 32)

                def body(n, s, i):
                    pe.wait_ge(m_lo, CR + n + 1)
                    pe.wait_ge(x1_done, CR + n - 1)
                    for c in (0, 512):
                        for k in range(KC):
                            mm = three_passes(pe, ps_x[:, s, c:c + 512], [m[:, s, k] for m in mhl],
                                              [w[:, k, c:c + 512] for w in whl], k == 0, k == KC - 1)
                    mm.then_inc(x_full, 1)
                    pe.wait_ge(hn_done, CR + n + 1)
                    pe.wait_ge(h_out, CR + n)
                    for k in range(KC):
                        tr = pe.transpose(ps_h[:, k], hn[:, s, k * P:(k + 1) * P], cst["ident"])
                    tr.then_inc(h_tp, 1)
                    pe.wait_ge(h_out, CR + n + 1)
                    for k in range(KC):
                        mm = pe.matmul(ps_r[:, 0:NE], hT[:, k], wr[:, k], start=k == 0, stop=k == KC - 1)
                    mm.then_inc(r_full, 1)
                    pe.wait_ge(a_done, CR + n + 1)
                    pe.wait_ge(a_out, CR + n)
                    pe.transpose(ps_a[0:NE, 0:P], aff[:], cst["ident"]).then_inc(a_tp, 1)

                tiles(pe, body)

        ph.clear()


def choose(nc, affT, cst, slots_i, slots_g):
    with ExitStack() as ctx:
        ph = Phase(nc, ctx, "tk")
        val, idx, idf = ph.sb("val", [NE, CT]), ph.sb("idx", [NE, CT], U32), ph.sb("idf", [NE, CT])
        ps = ph.ps("ps", [P, 4, 512])
        step, conv, turned, out = ph.done("step", "conv", "tp", "out")
        groups = [(0, CS, 0, TS), (CS, CP, TS, TP)]

        with nc.Block() as block:

            @block.sync
            def _(sp):
                ph.start(sp)

            def take(dve, r, before, c0, cn, t0, tn):
                a, k = affT[:, t0:t0 + tn], CR + 3 * (r + before)
                v8, i8 = val[:, r * 8 + c0:r * 8 + c0 + 8], idx[:, r * 8 + c0:r * 8 + c0 + 8]
                dve.wait_ge(step, k)
                dve.max(v8, a).then_inc(step, 1)
                dve.wait_ge(step, k + 1)
                dve.max_index(i8, v8, a).then_inc(step, 1)
                dve.wait_ge(step, k + 2)
                dve.match_replace(a, v8, a, -1.0).then_inc(step, 1)

            @block.vector
            def _(dve):
                for r in range(CS // 8):
                    take(dve, r, 0, *groups[0])
                for r in range(CP // 8):
                    take(dve, r, CS // 8, *groups[1])
                for c0, cn, t0, tn in groups:
                    dve.tensor_copy(idf[:, c0:c0 + cn], idx[:, c0:c0 + cn]).then_inc(conv, 1)
                dve.wait_ge(conv, CR + 2)
                dve.tensor_scalar(idf[:, CS:CT], idf[:, CS:CT], float(TS), None, ALU.add).then_inc(conv, 1)
                for j, (c0, cn, t0, tn) in enumerate(groups):
                    for q, dst in ((0, slots_i), (1, slots_g)):
                        dve.wait_ge(turned, CR + 2 * j + q + 1)
                        dve.tensor_copy(dst[j][:], ps[0:cn, 2 * j + q, 0:NE]).then_inc(out, 1)
                dve.wait_ge(out, CR + 4)

            @block.tensor
            def _(pe):
                pe.wait_ge(conv, CR + 3)
                for j, (c0, cn, t0, tn) in enumerate(groups):
                    for q, src in enumerate((idf, val)):
                        pe.transpose(ps[0:cn, 2 * j + q, 0:NE], src[:, c0:c0 + cn], cst["ident"][0:NE, 0:NE]).then_inc(turned, 1)

        ph.clear()


def experts(nc, h2, y, w_gate, w_up, w_down, slots_i, slots_g, cst):
    with ExitStack() as ctx:
        ph = Phase(nc, ctx, "ex")
        WC = 2 * P
        NG, ND = FF // WC, D // WC
        STEPS, UNITS = NG + ND, 2 * (NG + ND)
        FT, DT = FF // P, D // P
        TILES = FT + DT
        NRAW, NHL = 6, 6
        XR = 4
        EARLY = 4
        raw = ph.sb("w_raw", [P, NRAW, KC, WC])
        whl = [ph.sb(n, [P, NHL, KC, WC], F32R) for n in ("w_hi", "w_lo")]
        xe = [ph.sb(f"xe{j}", [n, D]) for j, n in enumerate((CS, CP))]
        xT = ph.sb("xT", [P, KC, 2, CT], F32R)
        hid = ph.sb("hid", [P, FT, 2, CT], F32R)
        gs, us, sg, hf = (ph.sb(n, [P, 2, CT]) for n in ("gate_sum", "up_sum", "silu", "hidden"))
        yT = ph.sb("yT", [P, 2, CT])
        ye = [ph.sb(f"ye{j}", [n, D]) for j, n in enumerate((CS, CP))]
        gate = [ph.sb(f"gate{j}", [n, 1]) for j, n in enumerate((CS, CP))]
        rows_x, rows_y = ([ph.sb(f"rows_{w}{j}", [n, 1], U32) for j, n in enumerate((CS, CP))] for w in "xy")
        ps_w = ph.ps("ps_w", [P, 3, 2, 512])
        ps_t = ph.ps("ps_t", [P, 2, 512])
        w_in, x_in = ph.landed("w_in", NRAW), ph.landed("x_in", 2)
        w_hi, w_lo, t_full, t_out, g_sum, silu_done, h_mul, h_hi, h_lo = ph.done(
            "w_hid", "w_lod", "t_full", "t_out", "g_sum", "silu_done", "h_mul", "h_hid", "h_lod")
        row_x, row_y, gate_set, x_tp, x_hi, x_lo, y_sum, y_tp, y_half, y_out = ph.done(
            "row_x", "row_y", "gate_set", "x_tp", "x_hid", "x_lod", "y_sum", "y_tp", "y_half", "y_out")
        scattered = ph.landed("scattered", 2)
        gu_d = [w.rearrange("e (k p) c -> p e k c", p=P) for w in (w_gate, w_up)]
        dn_d = w_down.rearrange("e (h k p) c -> p e h k c", p=P, k=KC)

        def sum2(dve, out, src):
            return dve.tensor_reduce(out, src[:, 0:2 * CT].rearrange("p (a t) -> p t a", a=2), AX.X, ALU.add)

        def experts_of(eng, body):
            with eng.Fori(0, NE - 1) as e:
                body(e, False)
            body(NE - 1, True)

        with nc.Block() as block:

            @block.sync
            def _(sp):
                ph.start(sp)
                with sp.Fori(0, NE) as e:
                    one = bass.ds(e, 1)
                    for j in range(UNITS):
                        sp.wait_ge(w_lo, CR + UNITS * e + j + 1 - NRAW)
                        if j < 2 * NG:
                            src = gu_d[j % 2][:, one, :, j // 2 * WC:(j // 2 + 1) * WC].rearrange("p e k c -> p (e k) c")
                        else:
                            c = (j - 2 * NG) // 2 * WC
                            src = dn_d[:, one, j % 2, :, c:c + WC].rearrange("p e k c -> p (e k) c")
                        sp.dma_start(raw[:, j % NRAW], src).then_inc(w_in[j % NRAW], 16)

            @block.gpsimd
            def _(pool):
                def gather(e):
                    for j in range(2):
                        pool.tensor_copy(rows_x[j][:], slots_i[j][:, bass.ds(e, 1)]).then_inc(row_x, 1)
                    pool.wait_ge(row_x, CR + 2 * e + 2)
                    ph.settle(pool)
                    for j in range(2):
                        pool.indirect_dma_start(xe[j][:], None, h2, bass.IndirectOffsetOnAxis(ap=rows_x[j][:, 0:1], axis=0)).then_inc(x_in[j], 16)

                def hidden(e, tiles):
                    for f in tiles:
                        q, s = FT * e + f, f % 2
                        pool.wait_ge(t_out, CR + TILES * e + f + 1)
                        pool.wait_ge(silu_done, CR + q + 1)
                        pool.tensor_tensor(hid[:, f, 0], sg[:, s], us[:, s], ALU.mult).then_inc(h_hi, 1)
                        pool.tensor_tensor(hf[:, s], sg[:, s], us[:, s], ALU.mult).then_inc(h_mul, 1)
                        pool.wait_ge(h_hi, CR + q + 1)
                        pool.wait_ge(h_mul, CR + q + 1)
                        pool.tensor_tensor(hid[:, f, 1], hf[:, s], hid[:, f, 0].bitcast(F32), ALU.subtract).then_inc(h_lo, 1)

                def body(e, last):
                    if not last:
                        for j in range(2):
                            pool.wait_ge(x_in[j], 16 * e + 16)
                        pool.wait_ge(x_tp, CR + XR * e + XR)
                        gather(e + 1)
                    for j in range(2):
                        pool.tensor_copy(gate[j][:], slots_g[j][:, bass.ds(e, 1)]).then_inc(gate_set, 1)
                    hidden(e, range(EARLY, FT))
                    for j in range(2):
                        pool.tensor_copy(rows_y[j][:], slots_i[j][:, bass.ds(e, 1)]).then_inc(row_y, 1)
                    pool.wait_ge(row_y, CR + 2 * e + 2)
                    pool.wait_ge(y_out, CR + DT * e + DT)
                    ph.settle(pool)
                    for j in range(2):
                        pool.indirect_dma_start(y, bass.IndirectOffsetOnAxis(ap=rows_y[j][:, 0:1], axis=0), ye[j][:], None,
                                                compute_op=ALU.add).then_inc(scattered[j], 16)
                    if not last:
                        hidden(e + 1, range(EARLY))
                    for j in range(2):
                        pool.wait_ge(scattered[j], 16 * e + 16)

                gather(0)
                hidden(0, range(EARLY))
                experts_of(pool, body)

            @block.scalar
            def _(act):
                def high(e, j):
                    e, j = (e, j) if j < UNITS else (e + 1, j - UNITS)
                    act.wait_ge(w_in[j % NRAW], 16 * (UNITS // NRAW * e + j // NRAW) + 16)
                    act.wait_ge(t_full, CR + TILES * e + 2 * (j // 2 - NHL // 2 + 1))
                    act.activation(whl[0][:, j % NHL], raw[:, j % NRAW], ACT.Copy).then_inc(w_hi, 1)

                def x_high(e, rounds):
                    for r in rounds:
                        act.wait_ge(x_tp, CR + XR * e + r + 1)
                        act.activation(xT[:, 2 * r:2 * r + 2, 0], ps_w[:, (FT + r) % 3, 1, 0:2 * CT].rearrange("p (k t) -> p k t", k=2), ACT.Copy).then_inc(x_hi, 1)

                def silu(e, f):
                    q, s = FT * e + f, f % 2
                    act.wait_ge(g_sum, CR + q + 1)
                    act.wait_ge(h_mul, CR + q - 1)
                    act.activation(sg[:, s], gs[:, s], ACT.Silu).then_inc(silu_done, 1)

                def leave(e, m):
                    if m == 0:
                        act.wait_ge(gate_set, CR + 2 * e + 2)
                    act.wait_ge(y_tp, CR + DT * e + m + 1)
                    act.activation(ye[0][:, m * P:(m + 1) * P], ps_t[:, m % 2, 0:CS], ACT.Copy,
                                   scale=gate[0][:]).then_inc(y_half, 1)
                    act.activation(ye[1][:, m * P:(m + 1) * P], ps_t[0:CP, m % 2, P:2 * P], ACT.Copy,
                                   scale=gate[1][:]).then_inc(y_out, 1)

                def body(e, last):
                    for s in range(STEPS):
                        if not (last and s == STEPS - 1):
                            high(e, 2 * s + 2)
                            high(e, 2 * s + 3)
                        for h in range(2):
                            m = 2 * (s - NG) + h
                            if s < NG:
                                silu(e, 2 * s + h)
                            elif m < XR and not last:
                                x_high(e + 1, (m,))
                            if m > 0:
                                leave(e, m - 1)
                    leave(e, DT - 1)

                high(0, 0)
                high(0, 1)
                x_high(0, range(XR))
                experts_of(act, body)

            @block.vector
            def _(dve):
                def low(e, j):
                    e, j = (e, j) if j < UNITS else (e + 1, j - UNITS)
                    dve.wait_ge(w_hi, CR + UNITS * e + j + 1)
                    dve.tensor_tensor(whl[1][:, j % NHL], raw[:, j % NRAW], whl[0][:, j % NHL].bitcast(F32), ALU.subtract).then_inc(w_lo, 1)

                def x_low(e, rounds):
                    for r in rounds:
                        dve.wait_ge(x_hi, CR + XR * e + r + 1)
                        dve.tensor_tensor(xT[:, 2 * r:2 * r + 2, 1], ps_w[:, (FT + r) % 3, 1, 0:2 * CT].rearrange("p (k t) -> p k t", k=2),
                                          xT[:, 2 * r:2 * r + 2, 0].bitcast(F32), ALU.subtract).then_inc(x_lo, 1)

                def tile_out(e, t):
                    dve.wait_ge(t_full, CR + TILES * e + t + 1)
                    if t < FT:
                        q, s = FT * e + t, t % 2
                        dve.wait_ge(silu_done, CR + q - 1)
                        sum2(dve, gs[:, s], ps_w[:, t % 3, 0]).then_inc(g_sum, 1)
                        dve.wait_ge(h_mul, CR + q - 1)
                        sum2(dve, us[:, s], ps_w[:, t % 3, 1]).then_inc(t_out, 1)
                    else:
                        m = t - FT
                        dve.wait_ge(y_tp, CR + DT * e + m - 1)
                        sum2(dve, yT[:, m % 2], ps_w[:, t % 3, 0]).then_inc(t_out, 1)

                def body(e, last):
                    for s in range(STEPS):
                        if not (last and s == STEPS - 1):
                            low(e, 2 * s + 2)
                            low(e, 2 * s + 3)
                        for h in range(2):
                            if 0 <= 2 * (s - NG) + h < XR and not last:
                                x_low(e + 1, (2 * (s - NG) + h,))
                            tile_out(e, 2 * s + h)

                low(0, 0)
                low(0, 1)
                x_low(0, range(XR))
                experts_of(dve, body)

            @block.tensor
            def _(pe):
                def turn_x(e, rounds):
                    for j in range(2):
                        pe.wait_ge(x_in[j], 16 * e + 16)
                    for r in rounds:
                        pe.wait_ge(x_lo, CR + XR * e + r - 2)
                        for h in range(2):
                            k, c = 2 * r + h, h * CT
                            pe.transpose(ps_w[:, (FT + r) % 3, 1, c:c + CS], xe[0][:, k * P:(k + 1) * P], cst["ident"])
                            tr = pe.transpose(ps_w[:, (FT + r) % 3, 1, c + CS:c + CT], xe[1][:, k * P:(k + 1) * P], cst["ident"][0:CP, 0:CP])
                        tr.then_inc(x_tp, 1)

                def turn_y(e, m):
                    pe.wait_ge(t_out, CR + TILES * e + FT + m + 1)
                    pe.wait_ge(y_out, CR + DT * e + m - 1)
                    pe.transpose(ps_t[0:CS, m % 2, 0:P], yT[:, m % 2, 0:CS], cst["ident"])
                    pe.transpose(ps_t[0:CP, m % 2, P:2 * P], yT[:, m % 2, CS:CT], cst["ident"]).then_inc(y_tp, 1)

                def products(bank, slot, k, cols, x, first, last):
                    pe.matmul(bank[:, 0:2 * CT], whl[0][:, slot, k, cols], x, start=first, stop=False)
                    return pe.matmul(bank[:, CT:2 * CT], whl[1][:, slot, k, cols], x[:, 0], start=False, stop=last)

                def body(e, last):
                    for s in range(STEPS):
                        pe.wait_ge(w_lo, CR + UNITS * e + 2 * s + 2)
                        if s == 0:
                            pe.wait_ge(x_lo, CR + XR * e + XR)
                        for h in range(2):
                            t, cols = 2 * s + h, slice(h * P, (h + 1) * P)
                            pe.wait_ge(t_out, CR + TILES * e + t - 2)
                            if 0 <= t - FT < XR and not last:
                                turn_x(e + 1, (t - FT,))
                            if s < NG:
                                for u in range(2):
                                    for k in range(KC):
                                        mm = products(ps_w[:, t % 3, u], (2 * s + u) % NHL, k, cols, xT[:, k], k == 0, k == KC - 1)
                            else:
                                for u in range(2):
                                    pe.wait_ge(h_lo, CR + FT * e + KC * (u + 1))
                                    for k in range(KC):
                                        mm = products(ps_w[:, t % 3, 0], (2 * s + u) % NHL, k, cols, hid[:, u * KC + k],
                                                      u + k == 0, u == 1 and k == KC - 1)
                            mm.then_inc(t_full, 1)
                            if t > FT:
                                turn_y(e, t - FT - 1)
                    turn_y(e, DT - 1)

                turn_x(0, range(XR))
                experts_of(pe, body)


def program(nc, dram):
    with ExitStack() as ctx:
        ident = ctx.enter_context(nc.sbuf_tensor("identity", [P, P], F32))
        eps = ctx.enter_context(nc.sbuf_tensor("eps", [P, 2], F32))
        slots_i = [ctx.enter_context(nc.sbuf_tensor(f"slots_i{j}", [n, NE], U32)) for j, n in enumerate((CS, CP))]
        slots_g = [ctx.enter_context(nc.sbuf_tensor(f"slots_g{j}", [n, NE], F32)) for j, n in enumerate((CS, CP))]
        scratch = lambda name, shape: nc.dram_tensor(name, shape, F32, kind="Internal").ap()
        proj_t, proj_c = scratch("proj_t", (T, NB * UW)), scratch("proj_c", (NA * UW, T))
        att_g, merged, h2 = scratch("att_gated", (D, T)), scratch("merged", (D, T)), scratch("h2", (T, D))
        cst = {"ident": ident[:], "eps": eps[:, 0:1], "one": eps[:, 1:2]}
        consts_in = ctx.enter_context(nc.semaphore("consts_in"))
        eps_set = ctx.enter_context(nc.semaphore("eps_set"))
        with nc.Block() as block:

            @block.sync
            def _(sp):
                sp.dma_start(ident[:], dram["ident"]).then_inc(consts_in, 16)
                sp.wait_ge(consts_in, 16)

            @block.vector
            def _(dve):
                dve.memset(cst["eps"], EPS).then_inc(eps_set, 1)
                dve.memset(cst["one"], 1.0).then_inc(eps_set, 1)
                dve.wait_ge(eps_set, 2)

        with ExitStack() as mixer:
            act_hl = mixer.enter_context(nc.sbuf_tensor("act_hl", [P, 2, KC, T], F32R))
            rT = [mixer.enter_context(nc.sbuf_tensor(f"codes{d}", [RANK, T], F32)) for d in range(2)]
            project(nc, dram["x"], dram["w_cols"], dram["norm_mix"], cst, act_hl, proj_t, proj_c, rT)
            with ExitStack() as kvs:
                kT = kvs.enter_context(nc.sbuf_tensor("kT", [P, 2, KVH, T], F32R))
                vv = kvs.enter_context(nc.sbuf_tensor("vv", [P, 2, NT, KVH * HD], F32R))
                keys(nc, proj_t, dram["k_norm"], dram["cos"], dram["sin"], cst, kT, vv)
                attention(nc, proj_t, dram["q_norm"], dram["cos"], dram["sin"], cst, kT, vv, act_hl)
            mix(nc, "ma", act_hl, dram["w_o_att"], proj_c[C_ZB:C_ZB + D], att_g)
            gla(nc, proj_t, proj_c, (dram["w_gk_f"], dram["w_gk_b"]), (dram["b_gk_f"], dram["b_gk_b"]),
                dram["gla_norm"], dram["masks"], rT, cst, act_hl)
            mix(nc, "mg", act_hl, dram["w_o_gla"], proj_c[C_ZA:C_ZA + D], merged, add=att_g)
        with ExitStack() as router:
            affT = router.enter_context(nc.sbuf_tensor("affT", [NE, T], F32))
            finish_mixer(nc, dram["x"], merged, dram["w_out"], dram["norm_ffn"], dram["w_router"], cst, dram["y"], h2, affT)
            choose(nc, affT, cst, slots_i, slots_g)
        experts(nc, h2, dram["y"], dram["w_e_gate"], dram["w_e_up"], dram["w_e_down"], slots_i, slots_g, cst)


W_IN_ORDER = [(3104, 4128), (4128, 4640), (1024, 2048), (2048, 3072), (0, 1024), (4640, 6688), (3072, 3104)]


def rope_tables():
    pos = np.concatenate([np.arange(TS), np.arange(TP)])
    half = HD // 2
    inv = (10000.0 ** (-np.arange(0, half, 2, dtype=np.float32) / half)).astype(np.float32)
    ang = np.concatenate([(pos // GRID_W).astype(np.float32)[:, None] * inv,
                          (pos % GRID_W).astype(np.float32)[:, None] * inv], axis=1)
    return np.cos(ang), np.sin(ang)


def chunk_masks():
    j, i = np.arange(P)[:, None], np.arange(P)[None, :]
    same = j // CH == i // CH
    return np.stack([same & (i >= j), same & (i <= j)]).astype(np.float32)


def kernel(**inputs):
    import concourse.bacc as _bacc
    from concourse import mybir as _mybir
    from concourse.bass_utils import run_bass_kernel_spmd as _run

    given = {k: np.asarray(v) for k, v in inputs.items()}
    cos, sin = rope_tables()
    arrays = {
        "x": np.concatenate([given["x_sample"][0], given["x_prompt"][0]]),
        "w_cols": np.concatenate([given["w_in"][0][:, a:b] for a, b in W_IN_ORDER], axis=1),
        "ident": np.eye(P, dtype=np.float32), "cos": cos, "sin": sin, "masks": chunk_masks(),
    }
    for name in ("norm_mix", "b_gk_f", "b_gk_b", "gla_norm", "q_norm", "k_norm", "norm_ffn"):
        arrays[name] = given[name]
    for name in ("w_gk_f", "w_gk_b", "w_o_gla", "w_o_att", "w_out", "w_router", "w_e_gate", "w_e_up", "w_e_down"):
        arrays[name] = given[name][0]
    arrays = {k: np.ascontiguousarray(v) for k, v in arrays.items()}

    nc = _bacc.Bacc("TRN2", target_bir_lowering=False, num_devices=1)
    dram = {k: nc.dram_tensor(k, v.shape, _mybir.dt.from_np(v.dtype), kind="ExternalInput").ap() for k, v in arrays.items()}
    dram["y"] = nc.dram_tensor("y", (T, D), _mybir.dt.from_np(np.dtype("float32")), kind="ExternalOutput").ap()
    program(nc, dram)
    y = _run(nc, [arrays], core_ids=[0]).results[0]["y"]
    return y[TS:][None], y[:TS][None]
```

```python
from contextlib import ExitStack

import numpy as np

import concourse.bass as bass
from concourse import mybir

ALU = mybir.AluOpType
ACT = mybir.ActivationFunctionType
AX = mybir.AxisListType
F32 = mybir.dt.float32
F32R = mybir.dt.float32r
BF16 = mybir.dt.bfloat16
U32 = mybir.dt.uint32
U8 = mybir.dt.uint8

P = 128
D = 1024
TS, TP = 1024, 256
T = TS + TP
NT, NTS = T // P, TS // P
KC = D // P
GRID_W = 64
GH, DK, DV, RANK, CH = 4, 128, 256, 16, 64
NCH, NCHS = T // CH, TS // CH
GATE_NORM = 16.0
AH, KVH, HD = 8, 2, 128
GR = AH // KVH
NE, FF = 16, 2048
CS, CP = 2 * TS // NE, 2 * TP // NE
CT = CS + CP
EPS = 1e-6
UW = 512
MU = UW // P
NB, NA = 7, 6
G_Q, G_KV, G_V, G_G = 0, 2, 3, 5
C_Q, C_K, C_ZA, C_ZB = 0, 512, 1024, 2048
TOK3 = [(0, 512), (512, 1024), (1024, T)]


CR = 8
ST = 16


class Phase:

    def __init__(self, nc, ctx, tag):
        self.nc, self.ctx, self.tag, self.counted, self.stores = nc, ctx, tag, [], []
        self.passed = self.ctx.enter_context(nc.semaphore(f"{tag}_passed"))

    def sb(self, name, shape, dt=F32):
        return self.ctx.enter_context(self.nc.sbuf_tensor(f"{self.tag}_{name}", shape, dt))

    def ps(self, name, shape):
        return self.ctx.enter_context(self.nc.psum_tensor(f"{self.tag}_{name}", shape, F32))

    def landed(self, name, n=1):
        s = [self.nc.alloc_semaphore(f"{self.tag}_{name}{i}") for i in range(n)]
        return s if n > 1 else s[0]

    def stored(self, name, n):
        s = [self.ctx.enter_context(self.nc.semaphore(f"{self.tag}_{name}{i}")) for i in range(n)]
        self.stores += s
        return s

    def done(self, *names):
        s = [self.ctx.enter_context(self.nc.semaphore(f"{self.tag}_{n}")) for n in names]
        self.counted += s
        return s if len(s) > 1 else s[0]

    def start(self, sp):
        for s in self.counted:
            sp.sem_inc(s, CR)
        for s in self.stores:
            sp.sem_inc(s, ST)

    def settle(self, eng):
        eng.sem_inc(self.passed, 1)

    def clear(self):
        with self.nc.Block() as block:

            @block.gpsimd
            def _(pool):
                for s in self.counted + self.stores + [self.passed]:
                    pool.sem_clear(s)


def three_passes(pe, out, a, b, first, last):
    pe.matmul(out, a[0], b[0], start=first, stop=False)
    pe.matmul(out, a[0], b[1], start=False, stop=False)
    return pe.matmul(out, a[1], b[0], start=False, stop=last)


def channel_tile(pe, banks, w, act, full):
    for k in range(KC):
        for part, other in ((0, 0), (0, 1), (1, 0)):
            for c, (a, b) in enumerate(TOK3):
                mm = pe.matmul(banks[:, c, 0:b - a], w(part, k), act(other, k, a, b),
                               start=(k == 0 and part == other), stop=(k == KC - 1 and part == 1))
                if k == KC - 1 and part == 1:
                    mm.then_inc(full, 1)


def project(nc, x, w_cols, norm_mix, cst, act_hl, proj_t, proj_c, rT):
    with ExitStack() as ctx:
        ph = Phase(nc, ctx, "pj")
        gamma = ph.sb("gamma", [P, D])
        ssq, root, rstd = ph.sb("ssq", [P, 2]), ph.sb("root", [P, 2]), ph.sb("rstd", [P, 2])
        raw = ph.sb("w_raw", [P, 2, KC, UW])
        xs = raw[:, 1].rearrange("p k c -> p (k c)").rearrange("p (j s d) -> p j s d", j=2, s=2)
        xt, xn = xs[:, 0], xs[:, 1]
        whi, wlo = ph.sb("w_hi", [P, 2, KC, UW], F32R), ph.sb("w_lo", [P, 2, KC, UW], F32R)
        rraw = ph.sb("r_raw", [P, KC, 2 * RANK])
        rhi, rlo = ph.sb("r_hi", [P, KC, 2 * RANK], F32R), ph.sb("r_lo", [P, KC, 2 * RANK], F32R)
        stage = ph.sb("stage", [P, 2, UW])
        ps_c, ps_t = ph.ps("ps_chan", [P, 2, 3, 512]), ph.ps("ps_tok", [P, 2, 512])
        gamma_in, x_in, w_in, r_in = ph.landed("gamma_in"), ph.landed("x_in", 2), ph.landed("w_in", 2), ph.landed("r_in")
        squared, rooted, inverted, x_ready = ph.done("squared", "rooted", "inverted", "x_ready")
        turned, h_hi, h_lo = ph.done("turned", "h_hi", "h_lo")
        w_hi, w_lo, r_hi, r_lo = ph.done("w_hid", "w_lod", "r_hid", "r_lod")
        p_full, p_out = ph.done("p_full", "p_out")
        stored = ph.stored("stored", 2)
        x_d = x.rearrange("(n p) d -> p n d", p=P)
        w_d = w_cols.rearrange("(k p) c -> p k c", p=P)
        t_d = proj_t.rearrange("(n p) c -> p n c", p=P)
        tok_n, chan_n = NB * NT, NA * MU * 3
        turn_ps = [ps_c[:, s, 0:2].rearrange("p a (k t) -> p (a k) t", t=P) for s in range(2)]
        squares = stage[:].rearrange("p s c -> p (s c)")
        pair = NT // 2

        def tiles(eng, body, before_last=None):
            with eng.Fori(0, pair - 1) as i:
                for s in range(2):
                    body(2 * i + s, s, i)
            if before_last:
                before_last()
            for s in range(2):
                body(NT - 2 + s, s, pair - 1)

        more = lambda n, ahead: not isinstance(n, int) or n + ahead < NT

        with nc.Block() as block:

            @block.sync
            def _(sp):
                def store(q, s, dst, width):
                    sp.wait_ge(p_out, CR + q + 1)
                    sp.dma_start(dst, stage[:, s, 0:width]).then_inc(stored[s], 16)

                ph.start(sp)

                def load_x(n, s, i):
                    sp.wait_ge(x_ready, CR + n - 1)
                    sp.dma_start(xt[:, s], x_d[:, bass.ds(n, 1)].rearrange("p n d -> p (n d)")).then_inc(x_in[s], 16)

                tiles(sp, load_x)
                with sp.Fori(0, NB) as n:
                    for t in range(NT):
                        store(n * NT + t, t % 2, t_d[:, t, bass.ds(n * UW, UW)], UW)
                with sp.Fori(0, NA) as n:
                    for q in range(3 * MU):
                        a, b = TOK3[q % 3]
                        store(tok_n + n * (3 * MU) + q, q % 2, proj_c[bass.ds(n * UW + q // 3 * P, P), a:b], b - a)
                for s in range(2):
                    sp.wait_ge(stored[s], ST + 16 * (tok_n + chan_n) // 2)

            @block.gpsimd
            def _(pool):
                def load_w(n, s):
                    pool.wait_ge(w_lo, CR + n - 1)
                    pool.dma_start(raw[:, s], w_d[:, :, bass.ds(n * UW, UW)]).then_inc(w_in[s], 16)

                pool.dma_start(gamma[:], norm_mix.to_broadcast([P, D])).then_inc(gamma_in, 16)
                pool.dma_start(rraw[:], w_d[:, :, (NA + NB) * UW:(NA + NB) * UW + 2 * RANK]).then_inc(r_in, 16)
                load_w(0, 0)
                pool.wait_ge(h_lo, CR + NT)
                load_w(1, 1)
                with pool.Fori(1, (NB + NA) // 2) as i:
                    for s in range(2):
                        load_w(2 * i + s, s)
                load_w(NB + NA - 1, 0)

            @block.scalar
            def _(act):
                def square(n, s, i):
                    act.wait_ge(x_in[s], 16 * i + 16)
                    act.wait_ge(squared, CR + n)
                    act.wait_ge(rooted, CR + n - 1)
                    act.activation(squares, xt[:, s], ACT.Square, accum_out=ssq[:, s:s + 1]).then_inc(squared, 1)

                def square_root(n, s):
                    act.wait_ge(squared, CR + n + 1)
                    act.wait_ge(inverted, CR + n - 1)
                    act.activation(root[:, s:s + 1], ssq[:, s:s + 1], ACT.Sqrt, scale=1.0 / D,
                                   bias=cst["eps"]).then_inc(rooted, 1)

                def tile_hi(n, s, i):
                    if more(n, 1):
                        square_root(n + 1, 1 - s)
                    if more(n, 2):
                        square(n + 2, s, i + 1)
                    act.wait_ge(turned, CR + n + 1)
                    act.activation(act_hl[:, 0, :, bass.ds(n * P, P)], turn_ps[s], ACT.Copy).then_inc(h_hi, 1)

                def hi(s, landed):
                    act.wait_ge(w_in[s], landed)
                    act.activation(whi[:, s], raw[:, s], ACT.Copy).then_inc(w_hi, 1)

                def evac(q, s, use, src, width):
                    act.wait_ge(p_full, CR + q + 1)
                    act.wait_ge(stored[s], ST + 16 * use)
                    act.activation(stage[:, s, 0:width], src, ACT.Copy).then_inc(p_out, 1)

                def evac_tok(n):
                    for t in range(NT):
                        evac(n * NT + t, t % 2, n * (NT // 2) + t // 2, ps_t[:, t % 2], UW)

                def evac_chan(n):
                    for q in range(3 * MU):
                        a, b = TOK3[q % 3]
                        evac(tok_n + n * (3 * MU) + q, q % 2, tok_n // 2 + n * (3 * MU // 2) + q // 2,
                             ps_c[:, q // 3 % 2, q % 3, 0:b - a], b - a)

                square(0, 0, 0)
                square_root(0, 0)
                square(1, 1, 0)
                tiles(act, tile_hi, lambda: hi(0, 16))
                act.wait_ge(r_in, 16)
                act.activation(rhi[:], rraw[:], ACT.Copy).then_inc(r_hi, 1)
                hi(1, 16)
                with act.Fori(0, NB // 2) as i:
                    for s in range(2):
                        evac_tok(2 * i + s)
                        hi(s, 16 * i + 32)
                evac_tok(NB - 1)
                hi(0, 16 * (NB // 2) + 32)
                with act.Fori(0, NA // 2 - 1) as i:
                    for s in range(2):
                        evac_chan(2 * i + s)
                        hi(1 - s, 16 * i + 16 * (NB // 2 + 2 + s))
                for n in range(NA - 2, NA):
                    evac_chan(n)
                for d in range(2):
                    act.wait_ge(p_full, CR + tok_n + chan_n + 1)
                    act.activation(rT[d][:], ps_c[0:RANK, d].rearrange("p c n -> p (c n)")[:, 0:T], ACT.Copy).then_inc(p_out, 1)

            @block.vector
            def _(dve):
                dve.wait_ge(gamma_in, 16)

                def norm(n, s):
                    dve.wait_ge(rooted, CR + n + 1)
                    dve.reciprocal(rstd[:, s:s + 1], root[:, s:s + 1]).then_inc(inverted, 1)
                    dve.wait_ge(inverted, CR + n + 1)
                    dve.wait_ge(turned, CR + n - 1)
                    dve.scalar_tensor_tensor(out=xn[:, s], in0=xt[:, s], scalar=rstd[:, s:s + 1], in1=gamma[:],
                                             op0=ALU.mult, op1=ALU.mult).then_inc(x_ready, 1)

                def tile_lo(n, s, i):
                    if more(n, 1):
                        norm(n + 1, 1 - s)
                    dve.wait_ge(h_hi, CR + n + 1)
                    dve.tensor_tensor(act_hl[:, 1, :, bass.ds(n * P, P)], turn_ps[s],
                                      act_hl[:, 0, :, bass.ds(n * P, P)].bitcast(F32), ALU.subtract).then_inc(h_lo, 1)

                def lo(s, n):
                    dve.wait_ge(w_hi, CR + n + 1)
                    dve.tensor_tensor(wlo[:, s], raw[:, s], whi[:, s].bitcast(F32), ALU.subtract).then_inc(w_lo, 1)

                norm(0, 0)
                tiles(dve, tile_lo, lambda: lo(0, 0))
                dve.wait_ge(r_hi, CR + 1)
                dve.tensor_tensor(rlo[:], rraw[:], rhi[:].bitcast(F32), ALU.subtract).then_inc(r_lo, 1)
                with dve.Fori(0, (NB + NA) // 2) as i:
                    for s in range(2):
                        lo(1 - s, 2 * i + s + 1)

            @block.tensor
            def _(pe):
                def turn(n, s, i):
                    pe.wait_ge(x_ready, CR + n + 1)
                    pe.wait_ge(h_lo, CR + n - 1)
                    for k in range(KC):
                        tr = pe.transpose(ps_c[:, s, k // 4, k % 4 * P:k % 4 * P + P], xn[:, s, k * P:(k + 1) * P], cst["ident"])
                    tr.then_inc(turned, 1)

                tiles(pe, turn)
                pe.wait_ge(h_lo, CR + NT)

                def unit_tok(n, s):
                    pe.wait_ge(w_lo, CR + n + 1)
                    for t in range(NT):
                        pe.wait_ge(p_out, CR + n * NT + t - 1)
                        for k in range(KC):
                            mm = three_passes(pe, ps_t[:, t % 2], [act_hl[:, j, k, t * P:(t + 1) * P] for j in range(2)],
                                              (whi[:, s, k], wlo[:, s, k]), k == 0, k == KC - 1)
                        mm.then_inc(p_full, 1)

                def unit_chan(n, s):
                    pe.wait_ge(w_lo, CR + NB + n + 1)
                    for m in range(MU):
                        pe.wait_ge(p_out, CR + tok_n + (n * MU + m - 1) * 3)
                        channel_tile(pe, ps_c[:, m % 2], lambda j, k: (whi, wlo)[j][:, s, k, m * P:(m + 1) * P],
                                     lambda j, k, a, b: act_hl[:, j, k, a:b], p_full)

                with pe.Fori(0, NB // 2) as i:
                    for s in range(2):
                        unit_tok(2 * i + s, s)
                unit_tok(NB - 1, 0)
                with pe.Fori(0, NA // 2) as i:
                    for s in range(2):
                        unit_chan(2 * i + s, 1 - s)
                pe.wait_ge(r_lo, CR + 1)
                pe.wait_ge(p_out, CR + tok_n + chan_n)
                for d in range(2):
                    for c, (a, b) in enumerate(TOK3):
                        for k in range(KC):
                            cols = slice(d * RANK, (d + 1) * RANK)
                            mm = three_passes(pe, ps_c[0:RANK, d, c, 0:b - a], (rhi[:, k, cols], rlo[:, k, cols]),
                                              [act_hl[:, j, k, a:b] for j in range(2)], k == 0, k == KC - 1)
                mm.then_inc(p_full, 1)

        ph.clear()


def pairs(t, e):
    return t.rearrange("... (d e) -> ... d e", e=2)[..., e]


def keys(nc, proj_t, k_norm, cos, sin, cst, kT, vv):
    with ExitStack() as ctx:
        ph = Phase(nc, ctx, "ky")
        W = KVH * HD
        kv = ph.sb("kv", [P, NT, 2 * W])
        kn, kr = ph.sb("normed", [P, NT, KVH, HD]), ph.sb("rotated", [P, NT, KVH, HD])
        ka, kb = ph.sb("a", [P, NT, KVH, HD // 2]), ph.sb("b", [P, NT, KVH, HD // 2])
        tabs, gk = ph.sb("tables", [P, 2, NT, HD // 2]), ph.sb("g", [P, HD])
        ss, root, inv = (ph.sb(n, [P, NT, KVH]) for n in ("ss", "root", "inv"))
        ps = ph.ps("turned", [P, KVH, T])
        kv_in, tab_in = ph.landed("kv_in", 2), ph.landed("tab_in")
        step, summed, rooted, first, turned, k_hi, k_lo, v_hi, v_lo = ph.done(
            "step", "summed", "rooted", "first", "tp", "k_hid", "k_lod", "v_hid", "v_lod")
        k = kv[:, :, 0:W].rearrange("p n (h d) -> p n h d", d=HD)
        tab = [tabs[:, j].unsqueeze(2).broadcast_to([P, NT, KVH, HD // 2]) for j in range(2)]

        with nc.Block() as block:

            @block.sync
            def _(sp):
                ph.start(sp)
                for j in range(2):
                    half = slice(j * NT // 2, (j + 1) * NT // 2)
                    sp.dma_start(kv[:, half], proj_t.rearrange("(n p) c -> p n c", p=P)[:, half, G_KV * UW:(G_KV + 1) * UW]).then_inc(kv_in[j], 16)
                for j, src in enumerate((cos, sin)):
                    sp.dma_start(tabs[:, j], src.rearrange("(n p) d -> p n d", p=P)).then_inc(tab_in, 16)
                sp.dma_start(gk[:], k_norm.to_broadcast([P, HD])).then_inc(tab_in, 16)

            @block.scalar
            def _(act):
                act.wait_ge(kv_in[0], 16)
                act.wait_ge(kv_in[1], 16)
                act.activation(vv[:, 0], kv[:, :, W:2 * W], ACT.Copy).then_inc(v_hi, 1)
                act.wait_ge(summed, CR + 1)
                act.activation(root[:], ss[:], ACT.Sqrt, scale=1.0 / HD, bias=cst["eps"]).then_inc(rooted, 1)
                act.wait_ge(turned, CR + 1)
                act.activation(kT[:, 0], ps[:], ACT.Copy).then_inc(k_hi, 1)

            @block.gpsimd
            def _(pool):
                for e in range(2):
                    pool.wait_ge(step, CR + 3 + 2 * e)
                    pool.tensor_tensor(ka[:], pairs(kn[:], e), tab[0], ALU.mult).then_inc(first, 1)

            @block.vector
            def _(dve):
                dve.wait_ge(kv_in[0], 16)
                dve.wait_ge(kv_in[1], 16)
                dve.wait_ge(tab_in, 48)
                dve.tensor_tensor(kn[:], k, k, ALU.mult).then_inc(step, 1)
                dve.wait_ge(step, CR + 1)
                dve.tensor_reduce(ss[:], kn[:], AX.X, ALU.add).then_inc(summed, 1)
                dve.wait_ge(v_hi, CR + 1)
                dve.tensor_tensor(vv[:, 1], kv[:, :, W:2 * W], vv[:, 0].bitcast(F32), ALU.subtract).then_inc(v_lo, 1)
                dve.wait_ge(rooted, CR + 1)
                dve.reciprocal(inv[:], root[:]).then_inc(summed, 1)
                dve.wait_ge(summed, CR + 2)
                dve.tensor_tensor(kn[:], k, inv[:].unsqueeze(3).broadcast_to([P, NT, KVH, HD]), ALU.mult).then_inc(step, 1)
                dve.wait_ge(step, CR + 2)
                dve.tensor_tensor(kn[:], kn[:], gk[:].unsqueeze(1).unsqueeze(1).broadcast_to([P, NT, KVH, HD]), ALU.mult).then_inc(step, 1)
                dve.wait_ge(step, CR + 3)
                for e, op in ((0, ALU.subtract), (1, ALU.add)):
                    dve.tensor_tensor(kb[:], pairs(kn[:], 1 - e), tab[1], ALU.mult).then_inc(step, 1)
                    dve.wait_ge(step, CR + 4 + 2 * e)
                    dve.wait_ge(first, CR + 1 + e)
                    dve.tensor_tensor(pairs(kr[:], e), ka[:], kb[:], op).then_inc(step, 1)
                    dve.wait_ge(step, CR + 5 + 2 * e)
                dve.wait_ge(k_hi, CR + 1)
                dve.tensor_tensor(kT[:, 1], ps[:], kT[:, 0].bitcast(F32), ALU.subtract).then_inc(k_lo, 1)

            @block.tensor
            def _(pe):
                pe.wait_ge(step, CR + 7)
                for h in range(KVH):
                    for n in range(NT):
                        tr = pe.transpose(ps[:, h, n * P:(n + 1) * P], kr[:, n, h], cst["ident"])
                tr.then_inc(turned, 1)

        ph.clear()


def attention(nc, proj_t, q_norm, cos, sin, cst, kT, vv, act_hl):
    with ExitStack() as ctx:
        ph = Phase(nc, ctx, "at")
        qT = ph.sb("qT", [P, 2, AH, P], F32R)
        pT = ph.sb("pT", [P, 2, 2, NTS, 2, P], F32R)
        prob = ph.sb("prob", [P, 2, TS])
        q_in, q_n, q_r = (ph.sb(n, [P, AH, HD]) for n in ("q_in", "q_normed", "q_rotated"))
        q_a, q_b = (ph.sb(n, [P, AH, HD // 2]) for n in ("q_a", "q_b"))
        tabs, gq, gqs = ph.sb("tables", [P, 2, NT, HD // 2]), ph.sb("g", [P, HD]), ph.sb("g_scaled", [P, HD])
        q_ss, q_root, q_inv = (ph.sb(n, [P, AH]) for n in ("q_ss", "q_root", "q_inv"))
        nmax, rsum, rinv = (ph.sb(n, [P, 2]) for n in ("nmax", "rsum", "rinv"))
        ps_s, ps_p = ph.ps("ps_scores", [P, 2, TS]), ph.ps("ps_probs", [P, 2, 4, P])
        ps_o, ps_q = ph.ps("ps_out", [P, 2, P]), ph.ps("ps_q", [P, GR, P])
        tab_in, q_land = ph.landed("tab_in"), ph.landed("q_land")
        g_ready, q_sq, q_sum, q_rt, q_iv, q_step, q_tp, q_hi, q_lo = ph.done(
            "g_ready", "q_sq", "q_sum", "q_rt", "q_iv", "q_step", "q_tp", "q_hid", "q_lod")
        s_full, s_max, s_exp, r_iv, p_ready = ph.done("s_full", "s_max", "s_exp", "r_iv", "p_ready")
        p_tp, p_hi, p_lo, o_full, o_hi, o_lo = ph.done("p_tp", "p_hid", "p_lod", "o_full", "o_hid", "o_lod")
        QS = 8
        QT = (5, 7)

        def out_slots(n, u):
            g, r0 = u // 2, 2 * (u % 2)
            src = ps_o[:]
            if isinstance(n, int) and n >= NTS:
                a = TS + TP // GR * r0
                dst = [act_hl[:, j, 2 * g + n - NTS::4, a:a + 2 * TP // GR].rearrange("p e (r q) -> p r q e", r=2) for j in range(2)]
                return dst, src.rearrange("p r (q e) -> p r q e", e=2)
            a = g + TS // GR * r0
            dst = [act_hl[:, j, bass.ds(n, 1), a:a + 2 * TS // GR - g:2].rearrange("p o (r q) -> p (o r) q", r=2) for j in range(2)]
            return dst, src

        def ahead(n, h, L):
            if h < AH:
                return n, h, L
            return n + 1, h - AH, TP if isinstance(n, int) and n >= NTS - 1 else TS

        def behind(n, h, L):
            if h >= 2:
                return n, h // 2 - 1, L
            if isinstance(n, int) and n == 0:
                return None
            return n - 1, 3, TS if not isinstance(n, int) or n <= NTS else TP

        def tiles(eng, body):
            body(0, TS, True)
            with eng.Fori(1, NTS - 1) as n:
                body(n, TS, True)
            body(NTS - 1, TS, True)
            for n in range(NTS, NT):
                body(n, TP, n < NT - 1)

        with nc.Block() as block:

            @block.sync
            def _(sp):
                ph.start(sp)
                for j, src in enumerate((cos, sin)):
                    sp.dma_start(tabs[:, j], src.rearrange("(n p) d -> p n d", p=P)).then_inc(tab_in, 16)
                sp.dma_start(gq[:], q_norm.to_broadcast([P, HD])).then_inc(tab_in, 16)

            @block.gpsimd
            def _(pool):
                def prepare(n, sl):
                    pool.dma_start(q_in[:].rearrange("p h d -> p (h d)"),
                                   proj_t.rearrange("(n p) c -> p n c", p=P)[:, sl, 0:AH * HD].rearrange("p n c -> p (n c)")
                                   ).then_inc(q_land, 16)
                    pool.wait_ge(q_land, 16 * n + 16)
                    pool.tensor_tensor(q_n[:], q_in[:], q_in[:], ALU.mult).then_inc(q_sq, 1)
                    pool.wait_ge(q_iv, CR + n + 1)
                    pool.tensor_tensor(q_n[:], q_in[:], q_inv[:].unsqueeze(2).broadcast_to([P, AH, HD]), ALU.mult).then_inc(q_step, 1)
                    b = CR + QS * n
                    pool.wait_ge(q_step, b + 1)
                    pool.tensor_tensor(q_n[:], q_n[:], gqs[:].unsqueeze(1).broadcast_to([P, AH, HD]), ALU.mult).then_inc(q_step, 1)
                    pool.wait_ge(q_step, b + 2)
                    pool.wait_ge(q_tp, CR + 2 * n)
                    pool.wait_ge(tab_in, 48)
                    cs, sn = (tabs[:, j, sl].broadcast_to([P, AH, HD // 2]) for j in range(2))
                    for e, op in ((0, ALU.subtract), (1, ALU.add)):
                        ph.settle(pool)
                        pool.tensor_tensor(q_a[:], pairs(q_n[:], e), cs, ALU.mult).then_inc(q_step, 1)
                        pool.tensor_tensor(q_b[:], pairs(q_n[:], 1 - e), sn, ALU.mult).then_inc(q_step, 1)
                        pool.wait_ge(q_step, b + 4 + 3 * e)
                        pool.tensor_tensor(pairs(q_r[:], e), q_a[:], q_b[:], op).then_inc(q_step, 1)
                        pool.wait_ge(q_step, b + 5 + 3 * e)

                pool.wait_ge(g_ready, CR + 1)
                with pool.Fori(0, NT) as n:
                    prepare(n, bass.ds(n, 1))

            @block.scalar
            def _(act):
                def q_norms(n):
                    act.wait_ge(q_sum, CR + n + 1)
                    act.activation(q_root[:], q_ss[:], ACT.Sqrt, scale=1.0 / HD, bias=cst["eps"]).then_inc(q_rt, 1)

                def q_high(n, g):
                    act.wait_ge(q_tp, CR + 2 * n + g + 1)
                    act.activation(qT[:, 0, GR * g:GR * g + GR], ps_q[:], ACT.Copy).then_inc(q_hi, 1)

                def exp(n, h, L):
                    H, s = 8 * n + h, h % 2
                    act.wait_ge(s_max, CR + H + 1)
                    act.wait_ge(p_tp, CR + 2 * H - 2)
                    act.activation(prob[:, s, 0:L], ps_s[:, s, 0:L], ACT.Exp, bias=nmax[:, s:s + 1],
                                   accum_out=rsum[:, s:s + 1]).then_inc(s_exp, 1)

                def high(n, h, L):
                    H, hb = 8 * n + h, L // P // 2
                    for j in range(2):
                        act.wait_ge(p_tp, CR + 2 * H + j + 1)
                        act.wait_ge(o_full, CR + 4 * n + h // 2 - 1)
                        act.activation(pT[:, 0, h // 2 % 2, hb * j:hb * j + hb, h % 2], ps_p[:, j, 0:hb], ACT.Copy).then_inc(p_hi, 1)

                def out_high(n, u, L):
                    dst, src = out_slots(n, u)
                    act.wait_ge(o_full, CR + 4 * n + u + 1)
                    act.activation(dst[0], src, ACT.Copy).then_inc(o_hi, 1)

                def body(n, L, more):
                    for h in range(AH):
                        if more or h + 1 < AH:
                            exp(*ahead(n, h + 1, L))
                        if h == 0 and more:
                            q_norms(n + 1)
                        if h in QT and more:
                            q_high(n + 1, QT.index(h))
                        high(n, h, L)
                        if h % 2 == 1 and behind(n, h, L):
                            out_high(*behind(n, h, L))

                q_norms(0)
                for g in range(2):
                    q_high(0, g)
                exp(0, 0, TS)
                tiles(act, body)
                out_high(NT - 1, 3, TP)

            @block.vector
            def _(dve):
                def q_norms(n):
                    dve.wait_ge(q_sq, CR + n + 1)
                    dve.tensor_reduce(q_ss[:], q_n[:], AX.X, ALU.add).then_inc(q_sum, 1)

                def q_inverse(n):
                    dve.wait_ge(q_rt, CR + n + 1)
                    dve.reciprocal(q_inv[:], q_root[:]).then_inc(q_iv, 1)

                def q_low(n, g):
                    dve.wait_ge(q_hi, CR + 2 * n + g + 1)
                    sl = slice(GR * g, GR * g + GR)
                    dve.tensor_tensor(qT[:, 1, sl], ps_q[:], qT[:, 0, sl].bitcast(F32), ALU.subtract).then_inc(q_lo, 1)

                def row_max(n, h, L):
                    H, s = 8 * n + h, h % 2
                    dve.wait_ge(s_full, CR + H + 1)
                    dve.wait_ge(s_exp, CR + H - 1)
                    dve.tensor_reduce(nmax[:, s:s + 1], ps_s[:, s, 0:L], AX.X, ALU.max, negate=True).then_inc(s_max, 1)

                def scale(n, h, L):
                    H, s = 8 * n + h, h % 2
                    dve.wait_ge(s_exp, CR + H + 1)
                    dve.reciprocal(rinv[:, s:s + 1], rsum[:, s:s + 1]).then_inc(r_iv, 1)
                    dve.wait_ge(r_iv, CR + H + 1)
                    dve.tensor_scalar(prob[:, s, 0:L], prob[:, s, 0:L], rinv[:, s:s + 1], None, ALU.mult).then_inc(p_ready, 1)

                def low(n, h, L):
                    H, hb = 8 * n + h, L // P // 2
                    for j in range(2):
                        dve.wait_ge(p_hi, CR + 2 * H + j + 1)
                        dst = slice(hb * j, hb * j + hb)
                        to = [pT[:, i, h // 2 % 2, dst, h % 2] for i in range(2)]
                        dve.tensor_tensor(to[1], ps_p[:, j, 0:hb], to[0].bitcast(F32), ALU.subtract).then_inc(p_lo, 1)

                def out_low(n, u, L):
                    dst, src = out_slots(n, u)
                    dve.wait_ge(o_hi, CR + 4 * n + u + 1)
                    dve.tensor_tensor(dst[1], src, dst[0].bitcast(F32), ALU.subtract).then_inc(o_lo, 1)

                def body(n, L, more):
                    for h in range(AH):
                        if more or h + 1 < AH:
                            scale(*ahead(n, h + 1, L))
                        if more or h + 2 < AH:
                            row_max(*ahead(n, h + 2, L))
                        if h == 0 and more:
                            q_norms(n + 1)
                        if h == 1 and more:
                            q_inverse(n + 1)
                        if h in QT and more:
                            q_low(n + 1, QT.index(h))
                        low(n, h, L)
                        if h % 2 == 1 and behind(n, h, L):
                            out_low(*behind(n, h, L))

                dve.wait_ge(tab_in, 48)
                dve.tensor_scalar(gqs[:], gq[:], float(HD) ** -0.5, None, ALU.mult).then_inc(g_ready, 1)
                q_norms(0)
                q_inverse(0)
                for g in range(2):
                    q_low(0, g)
                row_max(0, 0, TS)
                scale(0, 0, TS)
                row_max(0, 1, TS)
                tiles(dve, body)
                out_low(NT - 1, 3, TP)

            @block.tensor
            def _(pe):
                def turn_q(n, g):
                    pe.wait_ge(q_step, CR + QS * n + QS)
                    pe.wait_ge(q_lo, CR + 2 * n + g)
                    for r in range(GR):
                        tr = pe.transpose(ps_q[:, r], q_r[:, GR * g + r], cst["ident"])
                    tr.then_inc(q_tp, 1)

                def scores(n, h, L):
                    H = 8 * n + h
                    k0 = 0 if L == TS else TS
                    pe.wait_ge(q_lo, CR + 2 * n + h // GR + 1)
                    pe.wait_ge(s_exp, CR + H - 1)
                    for c in range(0, L, 512):
                        w = min(512, L)
                        mm = three_passes(pe, ps_s[:, h % 2, c:c + w], [qT[:, j, h] for j in range(2)],
                                          [kT[:, j, h // GR, k0 + c:k0 + c + w] for j in range(2)], True, True)
                    mm.then_inc(s_full, 1)

                def turn_p(n, h, L):
                    H, hb = 8 * n + h, L // P // 2
                    pe.wait_ge(p_ready, CR + H + 1)
                    for j in range(2):
                        pe.wait_ge(p_lo, CR + 2 * H + j - 1)
                        for b in range(hb):
                            kb = hb * j + b
                            tr = pe.transpose(ps_p[:, j, b], prob[:, h % 2, kb * P:(kb + 1) * P], cst["ident"])
                        tr.then_inc(p_tp, 1)

                def values(n, u, L):
                    g = u // 2
                    pe.wait_ge(p_lo, CR + 16 * n + 4 * u + 4)
                    pe.wait_ge(o_lo, CR + 4 * n + u)
                    kb0, nk = (0, NTS) if L == TS else (NTS, NT - NTS)
                    for b in range(nk):
                        mm = three_passes(pe, ps_o[:], [vv[:, j, kb0 + b, g * HD:(g + 1) * HD] for j in range(2)],
                                          [pT[:, j, u % 2, b] for j in range(2)], b == 0, b == nk - 1)
                    mm.then_inc(o_full, 1)

                def body(n, L, more):
                    for h in range(AH):
                        if more or h + 2 < AH:
                            scores(*ahead(n, h + 2, L))
                        if h in QT and more:
                            turn_q(n + 1, QT.index(h))
                        turn_p(n, h, L)
                        if h % 2 == 0 and behind(n, h, L):
                            values(*behind(n, h, L))

                for g in range(2):
                    turn_q(0, g)
                for h in range(2):
                    scores(0, h, TS)
                tiles(pe, body)
                values(NT - 1, 3, TP)

        ph.clear()


def mix(nc, tag, act_hl, w, z_rows, out, add=None):
    with ExitStack() as ctx:
        ph = Phase(nc, ctx, tag)
        WC = 2 * P
        raw = ph.sb("w_raw", [P, 2, KC, WC])
        whl = [ph.sb(n, [P, 2, KC, WC], F32R) for n in ("w_hi", "w_lo")]
        z, sig, o = ph.sb("z", [P, 2, T]), ph.sb("sig", [P, 2, T]), ph.sb("o", [P, 2, T])
        extra = ph.sb("add", [P, 2, T]) if add is not None else None
        ps = ph.ps("ps", [P, 2, 4, 512])
        w_in, z_in, a_in = ph.landed("w_in", 2), ph.landed("z_in", 2), ph.landed("a_in", 2)
        w_hi, w_lo, full, sig_done, gated, summed = ph.done("w_hid", "w_lod", "full", "sig_done", "gated", "summed")
        stored = ph.stored("stored", 2)
        w_d = w.rearrange("(k p) c -> p k c", p=P)
        NU, PU = D // WC, WC // P
        ready = summed if add is not None else gated

        NT8 = D // P
        units = [(u, u % 2) for u in range(NU)]
        tiles = [(t, t % 2, t // PU, t % PU) for t in range(NT8)]

        with nc.Block() as block:

            @block.sync
            def _(sp):
                ph.start(sp)
                for t, s, _u, _m in tiles:
                    sp.wait_ge(ready, CR + t + 1)
                    sp.dma_start(out[t * P:(t + 1) * P], o[:, s]).then_inc(stored[s], 16)
                for s in range(2):
                    sp.wait_ge(stored[s], ST + 16 * NT8 // 2)

            @block.gpsimd
            def _(pool):
                for u, s in units:
                    pool.wait_ge(w_lo, CR + u - 1)
                    pool.dma_start(raw[:, s], w_d[:, :, u * WC:(u + 1) * WC]).then_inc(w_in[s], 16)
                    for t in range(u * PU, (u + 1) * PU):
                        pool.wait_ge(gated, CR + t - 1)
                        pool.dma_start(z[:, t % 2], z_rows[t * P:(t + 1) * P]).then_inc(z_in[t % 2], 16)
                        if add is not None:
                            pool.wait_ge(summed, CR + t - 1)
                            pool.dma_start(extra[:, t % 2], add[t * P:(t + 1) * P]).then_inc(a_in[t % 2], 16)

            @block.scalar
            def _(act):
                def high(u, s):
                    act.wait_ge(w_in[s], 16 * (u // 2) + 16)
                    if u >= 2:
                        act.wait_ge(full, CR + (u - 1) * PU * 3)
                    act.activation(whl[0][:, s], raw[:, s], ACT.Copy).then_inc(w_hi, 1)

                high(0, 0)
                for t, s, u, m in tiles:
                    if m == 0 and u + 1 < NU:
                        high(u + 1, (u + 1) % 2)
                    act.wait_ge(z_in[s], 16 * (t // 2) + 16)
                    act.wait_ge(gated, CR + t - 1)
                    act.activation(sig[:, s], z[:, s], ACT.Sigmoid).then_inc(sig_done, 1)

            @block.vector
            def _(dve):
                def low(u, s):
                    dve.wait_ge(w_hi, CR + u + 1)
                    dve.tensor_tensor(whl[1][:, s], raw[:, s], whl[0][:, s].bitcast(F32), ALU.subtract).then_inc(w_lo, 1)

                low(0, 0)
                for t, s, u, m in tiles:
                    if m == 0 and u + 1 < NU:
                        low(u + 1, (u + 1) % 2)
                    dve.wait_ge(sig_done, CR + t + 1)
                    dve.wait_ge(full, CR + 3 * t + 3)
                    dve.wait_ge(stored[s], ST + 16 * (t // 2))
                    dve.tensor_tensor(o[:, s], ps[:, s, 0:3].rearrange("p c n -> p (c n)")[:, 0:T], sig[:, s], ALU.mult).then_inc(gated, 1)
                    if add is not None:
                        dve.wait_ge(gated, CR + t + 1)
                        dve.wait_ge(a_in[s], 16 * (t // 2) + 16)
                        dve.tensor_tensor(o[:, s], o[:, s], extra[:, s], ALU.add).then_inc(summed, 1)

            @block.tensor
            def _(pe):
                for t, s, u, m in tiles:
                    if m == 0:
                        pe.wait_ge(w_lo, CR + u + 1)
                    pe.wait_ge(gated, CR + t - 1)
                    channel_tile(pe, ps[:, s], lambda j, k: whl[j][:, u % 2, k, m * P:(m + 1) * P],
                                 lambda j, k, a, b: act_hl[:, j, k, a:b], full)

        ph.clear()


def gla(nc, proj_t, proj_c, wg, bg, g_norm, masks, rT, cst, act_hl):
    with ExitStack() as ctx:
        ph = Phase(nc, ctx, "gl")
        qk = ph.sb("qk", [P, 2, T])
        v, g = ph.sb("v", [P, NT, DV]), ph.sb("g", [P, NT, DV])
        wgate, bias = ph.sb("w_gate", [RANK, 2, DK]), ph.sb("bias", [P, 2])
        gnorm = ph.sb("gnorm", [P, DV])
        starts = ph.sb("starts", [P, T + CH], BF16)
        mask = ph.sb("mask", [P, 2, P], U8)
        z_b, e = [ph.sb("zb0", [P, T]), ph.sb("zb1", [P, T])], ph.sb("e", [P, T])
        decay = ph.sb("decay", [P, 2, NCH])
        qt, kt = ph.sb("q_t", [P, 2, T]), ph.sb("k_t", [P, 2, T])
        khT = ph.sb("k_hat_turned", [P, NT, DK])
        S = ph.sb("states", [P, 2, NCH - 1, DV])
        A = ph.sb("A", [P, 2, 2, P])
        flat = khT[:].rearrange("p n d -> p (n d)")
        Asum = flat[:, 0:2 * P].rearrange("p (s n) -> p s n", s=2)
        o_n = flat[:, 2 * P:2 * P + 2 * DV].rearrange("p (s n) -> p s n", s=2)
        oss, oroot, oinv = (ph.sb(n, [P, 2]) for n in ("oss", "oroot", "oinv"))
        pp = ph.ps("ps", [P, 8, 512])
        gate_ps = pp[:, 0:3].rearrange("p c n -> p (c n)")[:, 0:T]
        kh_ps = pp[:, 5:8].rearrange("p c n -> p (c n)")[:, 0:T]
        u_ps, a_ps = [pp[:, 3, 0:DV], pp[:, 4, 0:DV]], [pp[:, 5], pp[:, 6]]
        o_ps, t_ps = u_ps, pp[:, 7, 0:DV].rearrange("p (c t) -> p c t", c=2)
        const_in, qk_in, v_in, g_in, w_in = (ph.landed(n) for n in ("const_in", "qk_in", "v_in", "g_in", "w_in"))
        set_up, gates, z_done, neg_done, m_step, lg_done, b_done, d_done, e_done, dec_done = ph.done(
            "set_up", "gates", "z_done", "neg_done", "m_step", "lg_done", "b_done", "d_done", "e_done", "dec_done")
        q_prod, k_prod, kh_tp, kh_out, u_full, moved, silu_done = ph.done(
            "q_prod", "k_prod", "kh_tp", "kh_out", "u_full", "moved", "silu_done")
        a_full, a_cut, a_sum, o_full, ssd, rooted, o_inv, o_scaled, o_ready, o_tp, o_hi, o_lo = ph.done(
            "a_full", "a_cut", "a_sum", "o_full", "ssd", "rooted", "o_iv", "o_scaled", "o_ready", "o_tp", "o_hid", "o_lod")
        NU = NCH - 2
        order = [list(range(NCH)), list(range(NCH - 1, -1, -1))]
        begins = [(0, NCHS), (NCH - 1, NCHS - 1)]
        ends = [(NCHS - 1, NCH - 1), (NCHS, 0)]
        chunks = lambda t: t.rearrange("p (c n) -> p c n", n=CH)
        chunk_end = lambda t, d: chunks(t)[:, :, CH - 1 if d == 0 else 0]
        state = lambda d, c: S[:, d, c - 1 + d]

        def heads(eng, body):
            with eng.Fori(0, GH - 1) as i:
                body(i, False)
            body(GH - 1, True)

        def updates(d):
            return [(n, c) for n, c in enumerate(c for c in order[d] if c not in ends[d])]

        with nc.Block() as block:

            @block.sync
            def _(sp):
                ph.start(sp)
                sp.dma_start(A[:, 0], masks.rearrange("m p n -> p m n")).then_inc(const_in, 16)
                sp.dma_start(gnorm[:], g_norm.to_broadcast([P, DV])).then_inc(const_in, 16)
                with sp.Fori(0, GH) as i:
                    sp.wait_ge(q_prod, CR + 2 * i)
                    sp.wait_ge(k_prod, CR + 4 * i)
                    for j, row in enumerate((C_Q, C_K)):
                        sp.dma_start(qk[:, j], proj_c[bass.ds(i * DK + row, DK)]).then_inc(qk_in, 16)
                    sp.wait_ge(z_done, CR + 2 * i)
                    ph.settle(sp)
                    for d in range(2):
                        sp.dma_start(wgate[:, d], wg[d][:, bass.ds(i * DK, DK)]).then_inc(w_in, 16)
                        sp.dma_start(bias[:, d:d + 1], bg[d].rearrange("o (p u) -> (o p) u", u=1)[bass.ds(i * DK, DK)]).then_inc(w_in, 16)
                    sp.wait_ge(o_full, CR + NT * i)
                    sp.wait_ge(o_ready, CR + NT * i)
                    for dst, grp, s in ((v, G_V, v_in), (g, G_G, g_in)):
                        src = proj_t.rearrange("(n p) c -> p n c", p=P)
                        sp.dma_start(dst[:], src[:, :, bass.ds(i * DV + grp * UW, DV)]).then_inc(s, 16)

            @block.gpsimd
            def _(pool):
                def add_scores(i, t):
                    pool.wait_ge(a_cut, CR + 2 * (NT * i + t) + 2)
                    pool.wait_ge(o_full, CR + NT * i + t - 1)
                    pool.tensor_tensor(Asum[:, t % 2], A[:, t % 2, 0], A[:, t % 2, 1], ALU.add).then_inc(a_sum, 1)

                def gate(i, t):
                    pool.wait_ge(o_scaled, CR + NT * i + t + 1)
                    pool.tensor_tensor(o_n[:, t % 2], o_n[:, t % 2], g[:, t], ALU.mult).then_inc(o_ready, 1)

                with pool.Fori(0, GH) as i:
                    pool.wait_ge(qk_in, 32 * i + 32)
                    for d in range(2):
                        q = 2 * i + d
                        pool.wait_ge(e_done, CR + 3 * q + 2)
                        pool.tensor_tensor(z_b[d][:], qk[:, 1], z_b[d][:], ALU.mult).then_inc(k_prod, 1)
                        pool.wait_ge(a_full, CR + NT * i)
                        pool.wait_ge(e_done, CR + 3 * q + 3)
                        pool.tensor_tensor(kt[:, d], qk[:, 1], e[:], ALU.mult).then_inc(k_prod, 1)
                    pool.wait_ge(silu_done, CR + i + 1)
                    add_scores(i, 0)
                    for t in range(NT):
                        if t + 1 < NT:
                            add_scores(i, t + 1)
                        gate(i, t)

            @block.scalar
            def _(act):
                def gates_in(i, d):
                    act.wait_ge(w_in, 64 * i + 64)
                    act.wait_ge(e_done, CR + 3 * (2 * i + d))
                    act.wait_ge(gates, CR + 2 * i + d + 1)
                    act.activation(z_b[d][:], gate_ps, ACT.Identity, bias=bias[:, d:d + 1]).then_inc(z_done, 1)

                def soft_exp(i, d):
                    q = 2 * i + d
                    act.wait_ge(neg_done, CR + q + 1)
                    act.activation(e[:], e[:], ACT.Exp).then_inc(m_step, 1)

                def soft_ln(i, d):
                    q = 2 * i + d
                    act.wait_ge(m_step, CR + 2 * q + 1)
                    act.activation(e[:], e[:], ACT.Ln, bias=cst["one"]).then_inc(m_step, 1)

                def exponentials(i, d):
                    q, sums = 2 * i + d, z_b[1 - d]
                    act.wait_ge(b_done, CR + q + 1)
                    act.wait_ge(moved, CR + 2 * NU * i)
                    act.activation(decay[:, d], chunk_end(sums[:], d), ACT.Exp, scale=1.0 / GATE_NORM).then_inc(dec_done, 1)
                    act.activation(e[:], sums[:], ACT.Exp, scale=1.0 / GATE_NORM).then_inc(e_done, 1)
                    act.wait_ge(d_done, CR + q + 1)
                    act.activation(z_b[d][:], z_b[d][:], ACT.Exp, scale=1.0 / GATE_NORM).then_inc(e_done, 1)
                    act.wait_ge(q_prod, CR + q + 1)
                    act.activation(e[:], sums[:], ACT.Exp, scale=-1.0 / GATE_NORM).then_inc(e_done, 1)

                def k_hat_out(i, d):
                    act.wait_ge(kh_tp, CR + 2 * i + d + 1)
                    act.activation(khT[:], kh_ps, ACT.Copy).then_inc(kh_out, 1)

                def body(i, last):
                    soft_ln(i, 0)
                    exponentials(i, 0)
                    gates_in(i, 1)
                    k_hat_out(i, 0)
                    soft_exp(i, 1)
                    soft_ln(i, 1)
                    exponentials(i, 1)
                    k_hat_out(i, 1)
                    act.wait_ge(g_in, 16 * i + 16)
                    act.activation(g[:], g[:], ACT.Silu).then_inc(silu_done, 1)

                    def high(t):
                        act.wait_ge(o_tp, CR + NT * i + t + 1)
                        act.activation(act_hl[:, 0, bass.ds(2 * i, 2), t * P:(t + 1) * P], t_ps, ACT.Copy).then_inc(o_hi, 1)

                    for t in range(NT):
                        n, s = NT * i + t, t % 2
                        act.wait_ge(o_full, CR + n + 1)
                        act.wait_ge(o_tp, CR + n - 1)
                        act.activation(o_n[:, s], o_ps[s], ACT.Square, accum_out=oss[:, s:s + 1]).then_inc(ssd, 1)
                        act.wait_ge(ssd, CR + n + 1)
                        act.activation(oroot[:, s:s + 1], oss[:, s:s + 1], ACT.Sqrt, scale=1.0 / DV, bias=cst["eps"]).then_inc(rooted, 1)
                        if t > 0:
                            high(t - 1)
                        if t == NT - 3 and not last:
                            gates_in(i + 1, 0)
                    if not last:
                        soft_exp(i + 1, 0)
                    high(NT - 1)

                gates_in(0, 0)
                soft_exp(0, 0)
                heads(act, body)

            @block.vector
            def _(dve):
                dve.memset(starts[:], 1.0).then_inc(set_up, 1)
                dve.wait_ge(const_in, 32)
                dve.tensor_copy(mask[:], A[:, 0]).then_inc(set_up, 1)
                dve.wait_ge(set_up, CR + 2)
                dve.memset(A[:], 0.0).then_inc(set_up, 1)
                dve.memset(starts[:, ::CH], 0.0).then_inc(set_up, 1)
                dve.wait_ge(set_up, CR + 4)

                def negative(i, d):
                    q = 2 * i + d
                    dve.wait_ge(z_done, CR + q + 1)
                    dve.wait_ge(k_prod, CR + 2 * q)
                    dve.scalar_tensor_tensor(out=e[:], in0=z_b[d][:], scalar=-1.0, in1=z_b[d][:],
                                             op0=ALU.mult, op1=ALU.min).then_inc(neg_done, 1)

                def log_gate(i, d):
                    q = 2 * i + d
                    dve.wait_ge(m_step, CR + 2 * q + 2)
                    dve.scalar_tensor_tensor(out=z_b[d][:], in0=z_b[d][:], scalar=0.0, in1=e[:], op0=ALU.min, op1=ALU.subtract).then_inc(lg_done, 1)

                def running_sum(i, d):
                    q, z, b = 2 * i + d, z_b[d], z_b[1 - d]
                    dve.wait_ge(lg_done, CR + q + 1)
                    dve.wait_ge(kh_tp, CR + q)
                    if d == 0:
                        dve.tensor_tensor_scan(b[:], starts[:, 0:T], z[:], 0.0, ALU.mult, ALU.add).then_inc(b_done, 1)
                    else:
                        dve.tensor_tensor_scan(b[:, ::-1], starts[:, 1:T + 1][:, ::-1], z[:, ::-1], 0.0, ALU.mult, ALU.add).then_inc(b_done, 1)

                def to_end(i, d):
                    q, z, b = 2 * i + d, z_b[d], z_b[1 - d]
                    dve.wait_ge(b_done, CR + q + 1)
                    dve.tensor_tensor(chunks(z[:]), chunk_end(b[:], d).unsqueeze(2).broadcast_to([P, NCH, CH]), chunks(b[:]), ALU.subtract).then_inc(d_done, 1)

                def q_product(i, d):
                    q = 2 * i + d
                    dve.wait_ge(qk_in, 32 * i + 32)
                    dve.wait_ge(e_done, CR + 3 * q + 1)
                    dve.wait_ge(a_full, CR + NT * i)
                    dve.wait_ge(o_full, CR + NT * i)
                    dve.scalar_tensor_tensor(out=qt[:, d], in0=qk[:, 0], scalar=float(DK) ** -0.5, in1=e[:],
                                             op0=ALU.mult, op1=ALU.mult).then_inc(q_prod, 1)

                def body(i, last):
                    for step in (log_gate, running_sum, to_end, q_product):
                        step(i, 0)
                    negative(i, 1)
                    between = {5: log_gate, 7: running_sum, 9: to_end, 12: q_product}
                    for d in range(2):
                        q = 2 * i + d
                        dve.wait_ge(dec_done, CR + q + 1)
                        for n, c in updates(d):
                            u = NU * q + n
                            dve.wait_ge(u_full, CR + u + 1)
                            dve.wait_ge(moved, CR + u)
                            new = state(d, c + 1 - 2 * d)
                            if c in begins[d]:
                                dve.tensor_copy(new, u_ps[n % 2]).then_inc(moved, 1)
                            else:
                                dve.scalar_tensor_tensor(out=new, in0=state(d, c), scalar=decay[:, d, c:c + 1], in1=u_ps[n % 2],
                                                         op0=ALU.mult, op1=ALU.add).then_inc(moved, 1)
                            if d == 0 and n in between:
                                between[n](i, 1)

                    def cut(t):
                        n, s = NT * i + t, t % 2
                        dve.wait_ge(a_full, CR + n + 1)
                        dve.wait_ge(a_sum, CR + n - 1)
                        ph.settle(dve)
                        for d in range(2):
                            dve.copy_predicated(A[:, s, d], mask[:, d], a_ps[s][:, d * P:(d + 1) * P]).then_inc(a_cut, 1)

                    def low(t):
                        dve.wait_ge(o_hi, CR + NT * i + t + 1)
                        dst = [act_hl[:, j, bass.ds(2 * i, 2), t * P:(t + 1) * P] for j in range(2)]
                        dve.tensor_tensor(dst[1], t_ps, dst[0].bitcast(F32), ALU.subtract).then_inc(o_lo, 1)

                    cut(0)
                    for t in range(NT):
                        n, s = NT * i + t, t % 2
                        if t + 1 < NT:
                            cut(t + 1)
                        dve.wait_ge(rooted, CR + n + 1)
                        dve.reciprocal(oinv[:, s:s + 1], oroot[:, s:s + 1]).then_inc(o_inv, 1)
                        dve.wait_ge(o_inv, CR + n + 1)
                        dve.scalar_tensor_tensor(out=o_n[:, s], in0=o_ps[s], scalar=oinv[:, s:s + 1], in1=gnorm[:],
                                                 op0=ALU.mult, op1=ALU.mult).then_inc(o_scaled, 1)
                        if t > 0:
                            low(t - 1)
                        if t == NT - 2 and not last:
                            negative(i + 1, 0)
                    low(NT - 1)

                negative(0, 0)
                heads(dve, body)

            @block.tensor
            def _(pe):
                def gate_logits(i, d):
                    pe.wait_ge(w_in, 64 * i + 64)
                    pe.wait_ge(z_done, CR + 2 * i + d)
                    for c, (a, w) in enumerate(TOK3):
                        mm = pe.matmul(pp[:, c, 0:w - a], wgate[:, d], rT[d][:, a:w], start=True, stop=True)
                    mm.then_inc(gates, 1)

                def body(i, last):
                    gate_logits(i, 1)
                    for d in range(2):
                        q = 2 * i + d
                        pe.wait_ge(k_prod, CR + 2 * q + 1)
                        pe.wait_ge(kh_out, CR + q)
                        pe.wait_ge(a_cut, CR + 2 * NT * i)
                        pe.wait_ge(o_lo, CR + NT * i)
                        for t in range(NT):
                            tr = pe.transpose(kh_ps[:, t * P:(t + 1) * P], z_b[d][:, t * P:(t + 1) * P], cst["ident"])
                        tr.then_inc(kh_tp, 1)
                        pe.wait_ge(kh_out, CR + q + 1)
                        pe.wait_ge(v_in, 16 * i + 16)
                        pe.wait_ge(o_scaled, CR + NT * i)
                        for n, c in updates(d):
                            rows = slice(c % 2 * CH, c % 2 * CH + CH)
                            pe.wait_ge(moved, CR + NU * q + n - 1)
                            pe.matmul(u_ps[n % 2], khT[rows, c // 2], v[rows, c // 2], start=True, stop=True).then_inc(u_full, 1)

                    def scores(t):
                        pe.wait_ge(a_cut, CR + 2 * (NT * i + t) - 2)
                        tok = slice(t * P, (t + 1) * P)
                        for d in range(2):
                            mm = pe.matmul(a_ps[t % 2][:, d * P:(d + 1) * P], kt[:, d, tok], qt[:, d, tok], start=True, stop=True)
                        mm.then_inc(a_full, 1)

                    def output(t):
                        out = o_ps[t % 2]
                        pe.wait_ge(a_sum, CR + NT * i + t + 1)
                        pe.wait_ge(o_scaled, CR + NT * i + t - 1)
                        parts = [(d, c) for c in (2 * t, 2 * t + 1) for d in range(2) if c not in begins[d]]
                        pe.matmul(out, Asum[:, t % 2], v[:, t], start=True, stop=False, skip_group_check=True)
                        for d, c in parts:
                            rows = slice(c % 2 * CH, c % 2 * CH + CH)
                            mm = pe.matmul(out[rows], qt[:, d, c * CH:(c + 1) * CH], state(d, c), start=False,
                                           stop=(d, c) == parts[-1], skip_group_check=True)
                        mm.then_inc(o_full, 1)

                    def turn(t):
                        n = NT * i + t
                        pe.wait_ge(o_ready, CR + n + 1)
                        pe.wait_ge(o_lo, CR + n)
                        for c in range(2):
                            tr = pe.transpose(t_ps[:, c], o_n[:, t % 2, c * P:(c + 1) * P], cst["ident"])
                        tr.then_inc(o_tp, 1)

                    pe.wait_ge(q_prod, CR + 2 * i + 2)
                    pe.wait_ge(k_prod, CR + 4 * i + 4)
                    pe.wait_ge(moved, CR + 2 * NU * i + 2 * NU)
                    scores(0)
                    for t in range(NT):
                        if t + 1 < NT:
                            scores(t + 1)
                        output(t)
                        if t > 0:
                            turn(t - 1)
                        if t == NT - 4 and not last:
                            gate_logits(i + 1, 0)
                    turn(NT - 1)

                gate_logits(0, 0)
                heads(pe, body)

        ph.clear()


def finish_mixer(nc, x, merged, w_out, norm_ffn, w_router, cst, y, h2, affT):
    with ExitStack() as ctx:
        ph = Phase(nc, ctx, "fm")
        WC = 256
        NU = D // WC
        raw = ph.sb("w_raw", [P, NU, KC, WC])
        whl = [ph.sb(n, [P, KC, D], F32R) for n in ("w_hi", "w_lo")]
        wr, gamma = ph.sb("w_router", [P, KC, NE]), ph.sb("gamma", [P, D])
        mg = ph.sb("merged", [P, 2, KC, P])
        mhl = [ph.sb(n, [P, 2, KC, P], F32R) for n in ("m_hi", "m_lo")]
        xt, x1, hn = (ph.sb(n, [P, 2, D]) for n in ("x", "x1", "hn"))
        hT = ph.sb("hT", [P, KC, P])
        ssq, root, inv = (ph.sb(n, [P, 2]) for n in ("ssq", "root", "inv"))
        rmax, rsum, rinv, aff = ph.sb("rmax", [P, 1]), ph.sb("rsum", [P, 1]), ph.sb("rinv", [P, 1]), ph.sb("aff", [P, NE])
        ps_x, ps_h = ph.ps("ps_x", [P, 2, D]), ph.ps("ps_h", [P, KC, P])
        ps_r, ps_a = ph.ps("ps_r", [P, 512]), ph.ps("ps_a", [P, 512])
        w_in, c_in, m_in, x_in = ph.landed("w_in", NU), ph.landed("c_in"), ph.landed("m_in", 2), ph.landed("x_in", 2)
        w_hi, w_lo, m_hi, m_lo, x_full, x1_done, ssd, rooted, inv_done, hn_done = ph.done(
            "w_hid", "w_lod", "m_hid", "m_lod", "x_full", "x1_done", "ssd", "rooted", "inv_done", "hn_done")
        h_tp, h_out, r_full, r_max, r_exp, r_inv, a_done, a_tp, a_out = ph.done(
            "h_tp", "h_out", "r_full", "r_max", "r_exp", "r_iv", "a_done", "a_tp", "a_out")
        y_st, h_st = ph.stored("y_st", 2), ph.stored("h_st", 2)
        rows = lambda t: t.rearrange("(n p) d -> p n d", p=P)
        x_d, y_d, h_d = rows(x), rows(y), rows(h2)
        w_d = w_out.rearrange("(k p) c -> p k c", p=P)
        m_d = merged.rearrange("(k p) t -> p k t", p=P)

        def tiles(eng, body):
            for s in range(2):
                body(s, s, 0)
            with eng.Fori(1, NT // 2 - 1) as i:
                for s in range(2):
                    body(2 * i + s, s, i)
            for s in range(2):
                body(NT - 2 + s, s, NT // 2 - 1)

        last = lambda n, ahead: isinstance(n, int) and n + ahead >= NT
        first = lambda n: isinstance(n, int) and n == 0

        with nc.Block() as block:

            @block.sync
            def _(sp):
                ph.start(sp)
                for u in range(NU):
                    sp.dma_start(raw[:, u], w_d[:, :, u * WC:(u + 1) * WC]).then_inc(w_in[u], 16)

                def body(n, s, i):
                    sp.wait_ge(x1_done, CR + n + 1)
                    sp.dma_start(y_d[:, bass.ds(n, 1)].rearrange("p o d -> p (o d)"), x1[:, s]).then_inc(y_st[s], 16)
                    sp.wait_ge(hn_done, CR + n + 1)
                    sp.dma_start(h_d[:, bass.ds(n, 1)].rearrange("p o d -> p (o d)"), hn[:, s]).then_inc(h_st[s], 16)

                tiles(sp, body)
                for s in range(2):
                    sp.wait_ge(y_st[s], ST + 16 * NT // 2)
                    sp.wait_ge(h_st[s], ST + 16 * NT // 2)

            @block.gpsimd
            def _(pool):
                pool.dma_start(gamma[:], norm_ffn.to_broadcast([P, D])).then_inc(c_in, 16)
                pool.dma_start(wr[:], w_router.rearrange("(k p) e -> p k e", p=P)).then_inc(c_in, 16)
                def body(n, s, i):
                    pool.wait_ge(m_lo, CR + n - 1)
                    pool.dma_start(mg[:, s], m_d[:, :, bass.ds(n * P, P)]).then_inc(m_in[s], 16)
                    pool.wait_ge(x1_done, CR + n - 1)
                    pool.dma_start(xt[:, s], x_d[:, bass.ds(n, 1)].rearrange("p o d -> p (o d)")).then_inc(x_in[s], 16)

                tiles(pool, body)

            @block.scalar
            def _(act):
                def high(n, s, i):
                    act.wait_ge(m_in[s], 16 * i + 16)
                    act.wait_ge(x_full, CR + n - 1)
                    act.activation(mhl[0][:, s], mg[:, s], ACT.Copy).then_inc(m_hi, 1)

                def aff_out(n):
                    act.wait_ge(a_tp, CR + n + 1)
                    act.activation(affT[:, bass.ds(n * P, P)], ps_a[0:NE, 0:P], ACT.Copy).then_inc(a_out, 1)

                def body(n, s, i):
                    if not last(n, 2):
                        high(n + 2, s, i + 1)
                    act.wait_ge(x1_done, CR + n + 1)
                    act.wait_ge(h_st[s], ST + 16 * i)
                    act.wait_ge(h_tp, CR + n - 1)
                    act.activation(hn[:, s], x1[:, s], ACT.Square, accum_out=ssq[:, s:s + 1]).then_inc(ssd, 1)
                    act.wait_ge(ssd, CR + n + 1)
                    act.activation(root[:, s:s + 1], ssq[:, s:s + 1], ACT.Sqrt, scale=1.0 / D, bias=cst["eps"]).then_inc(rooted, 1)
                    act.wait_ge(h_tp, CR + n + 1)
                    act.wait_ge(r_full, CR + n)
                    act.activation(hT[:], ps_h[:], ACT.Copy).then_inc(h_out, 1)
                    if not first(n):
                        aff_out(n - 1)
                    act.wait_ge(r_max, CR + n + 1)
                    act.activation(aff[:], ps_r[:, 0:NE], ACT.Exp, bias=rmax[:], accum_out=rsum[:]).then_inc(r_exp, 1)

                high(0, 0, 0)
                for u in range(NU):
                    act.wait_ge(w_in[u], 16)
                    act.activation(whl[0][:, :, u * WC:(u + 1) * WC], raw[:, u], ACT.Copy).then_inc(w_hi, 1)
                high(1, 1, 0)
                tiles(act, body)
                aff_out(NT - 1)

            @block.vector
            def _(dve):
                def low(n, s):
                    dve.wait_ge(m_hi, CR + n + 1)
                    dve.tensor_tensor(mhl[1][:, s], mg[:, s], mhl[0][:, s].bitcast(F32), ALU.subtract).then_inc(m_lo, 1)

                low(0, 0)
                for u in range(NU):
                    cols = slice(u * WC, (u + 1) * WC)
                    dve.wait_ge(w_hi, CR + u + 1)
                    dve.tensor_tensor(whl[1][:, :, cols], raw[:, u], whl[0][:, :, cols].bitcast(F32), ALU.subtract).then_inc(w_lo, 1)
                low(1, 1)
                dve.wait_ge(c_in, 32)

                def body(n, s, i):
                    dve.wait_ge(x_full, CR + n + 1)
                    dve.wait_ge(x_in[s], 16 * i + 16)
                    dve.wait_ge(y_st[s], ST + 16 * i)
                    dve.tensor_tensor(x1[:, s], ps_x[:, s], xt[:, s], ALU.add).then_inc(x1_done, 1)
                    if not last(n, 2):
                        low(n + 2, s)
                    dve.wait_ge(rooted, CR + n + 1)
                    dve.reciprocal(inv[:, s:s + 1], root[:, s:s + 1]).then_inc(inv_done, 1)
                    dve.wait_ge(inv_done, CR + n + 1)
                    dve.scalar_tensor_tensor(out=hn[:, s], in0=x1[:, s], scalar=inv[:, s:s + 1], in1=gamma[:],
                                             op0=ALU.mult, op1=ALU.mult).then_inc(hn_done, 1)
                    dve.wait_ge(r_full, CR + n + 1)
                    dve.tensor_reduce(rmax[:], ps_r[:, 0:NE], AX.X, ALU.max, negate=True).then_inc(r_max, 1)
                    dve.wait_ge(r_exp, CR + n + 1)
                    dve.reciprocal(rinv[:], rsum[:]).then_inc(r_inv, 1)
                    dve.wait_ge(r_inv, CR + n + 1)
                    dve.tensor_scalar(aff[:], aff[:], rinv[:], None, ALU.mult).then_inc(a_done, 1)

                tiles(dve, body)

            @block.tensor
            def _(pe):
                def products(n, s, half):
                    pe.wait_ge(m_lo, CR + n + 1)
                    pe.wait_ge(x1_done, CR + n - 1)
                    c = 512 * half
                    for k in range(KC):
                        mm = three_passes(pe, ps_x[:, s, c:c + 512], [m[:, s, k] for m in mhl],
                                          [w[:, k, c:c + 512] for w in whl], k == 0, k == KC - 1)
                    if half == 1:
                        mm.then_inc(x_full, 1)

                def turn_aff(n):
                    pe.wait_ge(a_done, CR + n + 1)
                    pe.wait_ge(a_out, CR + n)
                    pe.transpose(ps_a[0:NE, 0:P], aff[:], cst["ident"]).then_inc(a_tp, 1)

                def body(n, s, i):
                    if not last(n, 1):
                        products(n + 1, 1 - s, 0)
                    if not first(n):
                        turn_aff(n - 1)
                    pe.wait_ge(hn_done, CR + n + 1)
                    pe.wait_ge(h_out, CR + n)
                    for k in range(KC):
                        tr = pe.transpose(ps_h[:, k], hn[:, s, k * P:(k + 1) * P], cst["ident"])
                    tr.then_inc(h_tp, 1)
                    if not last(n, 1):
                        products(n + 1, 1 - s, 1)
                    pe.wait_ge(h_out, CR + n + 1)
                    for k in range(KC):
                        mm = pe.matmul(ps_r[:, 0:NE], hT[:, k], wr[:, k], start=k == 0, stop=k == KC - 1)
                    mm.then_inc(r_full, 1)

                for half in range(2):
                    pe.wait_ge(w_lo, CR + (half + 1) * NU // 2)
                    products(0, 0, half)
                pe.wait_ge(c_in, 32)
                tiles(pe, body)
                turn_aff(NT - 1)

        ph.clear()


def choose(nc, affT, cst, slots_i, slots_g):
    with ExitStack() as ctx:
        ph = Phase(nc, ctx, "tk")
        val, idx, idf = ph.sb("val", [NE, CT]), ph.sb("idx", [NE, CT], U32), ph.sb("idf", [NE, CT])
        ps = ph.ps("ps", [P, 4, 512])
        step, conv, turned, out = ph.done("step", "conv", "tp", "out")
        groups = [(0, CS, 0, TS), (CS, CP, TS, TP)]

        with nc.Block() as block:

            @block.sync
            def _(sp):
                ph.start(sp)

            def take(dve, r, before, c0, cn, t0, tn):
                a, k = affT[:, t0:t0 + tn], CR + 3 * (r + before)
                v8, i8 = val[:, r * 8 + c0:r * 8 + c0 + 8], idx[:, r * 8 + c0:r * 8 + c0 + 8]
                dve.wait_ge(step, k)
                dve.max(v8, a).then_inc(step, 1)
                dve.wait_ge(step, k + 1)
                dve.max_index(i8, v8, a).then_inc(step, 1)
                dve.wait_ge(step, k + 2)
                dve.match_replace(a, v8, a, -1.0).then_inc(step, 1)

            @block.vector
            def _(dve):
                for r in range(CS // 8):
                    take(dve, r, 0, *groups[0])
                for r in range(CP // 8):
                    take(dve, r, CS // 8, *groups[1])
                for c0, cn, t0, tn in groups:
                    dve.tensor_copy(idf[:, c0:c0 + cn], idx[:, c0:c0 + cn]).then_inc(conv, 1)
                dve.wait_ge(conv, CR + 2)
                dve.tensor_scalar(idf[:, CS:CT], idf[:, CS:CT], float(TS), None, ALU.add).then_inc(conv, 1)
                for j, (c0, cn, t0, tn) in enumerate(groups):
                    for q, dst in ((0, slots_i), (1, slots_g)):
                        dve.wait_ge(turned, CR + 2 * j + q + 1)
                        dve.tensor_copy(dst[j][:], ps[0:cn, 2 * j + q, 0:NE]).then_inc(out, 1)
                dve.wait_ge(out, CR + 4)

            @block.tensor
            def _(pe):
                pe.wait_ge(conv, CR + 3)
                for j, (c0, cn, t0, tn) in enumerate(groups):
                    for q, src in enumerate((idf, val)):
                        pe.transpose(ps[0:cn, 2 * j + q, 0:NE], src[:, c0:c0 + cn], cst["ident"][0:NE, 0:NE]).then_inc(turned, 1)

        ph.clear()


def experts(nc, h2, y, w_gate, w_up, w_down, slots_i, slots_g, cst):
    with ExitStack() as ctx:
        ph = Phase(nc, ctx, "ex")
        WC = 2 * P
        NG, ND = FF // WC, D // WC
        STEPS, UNITS = NG + ND, 2 * (NG + ND)
        FT, DT = FF // P, D // P
        TILES = FT + DT
        NRAW, NHL = 6, 6
        XR = 4
        EARLY = 4
        raw = ph.sb("w_raw", [P, NRAW, KC, WC])
        whl = [ph.sb(n, [P, NHL, KC, WC], F32R) for n in ("w_hi", "w_lo")]
        xe = [ph.sb(f"xe{j}", [n, D]) for j, n in enumerate((CS, CP))]
        xT = ph.sb("xT", [P, KC, 2, CT], F32R)
        hid = ph.sb("hid", [P, FT, 2, CT], F32R)
        gs, us, sg, hf = (ph.sb(n, [P, 2, CT]) for n in ("gate_sum", "up_sum", "silu", "hidden"))
        yT = ph.sb("yT", [P, 2, CT])
        ye = [ph.sb(f"ye{j}", [n, D]) for j, n in enumerate((CS, CP))]
        gate = [ph.sb(f"gate{j}", [n, 1]) for j, n in enumerate((CS, CP))]
        rows_x, rows_y = ([ph.sb(f"rows_{w}{j}", [n, 1], U32) for j, n in enumerate((CS, CP))] for w in "xy")
        ps_w = ph.ps("ps_w", [P, 3, 2, 512])
        ps_t = ph.ps("ps_t", [P, 2, 512])
        w_in, x_in = ph.landed("w_in", NRAW), ph.landed("x_in", 2)
        w_hi, w_lo, t_full, t_out, g_sum, silu_done, h_mul, h_hi, h_lo = ph.done(
            "w_hid", "w_lod", "t_full", "t_out", "g_sum", "silu_done", "h_mul", "h_hid", "h_lod")
        row_x, row_y, gate_set, x_tp, x_hi, x_lo, y_sum, y_tp, y_half, y_out = ph.done(
            "row_x", "row_y", "gate_set", "x_tp", "x_hid", "x_lod", "y_sum", "y_tp", "y_half", "y_out")
        scattered = ph.landed("scattered", 2)
        gu_d = [w.rearrange("e (k p) c -> p e k c", p=P) for w in (w_gate, w_up)]
        dn_d = w_down.rearrange("e (h k p) c -> p e h k c", p=P, k=KC)

        def sum2(dve, out, src):
            return dve.tensor_reduce(out, src[:, 0:2 * CT].rearrange("p (a t) -> p t a", a=2), AX.X, ALU.add)

        def experts_of(eng, body):
            with eng.Fori(0, NE - 1) as e:
                body(e, False)
            body(NE - 1, True)

        with nc.Block() as block:

            @block.sync
            def _(sp):
                ph.start(sp)
                with sp.Fori(0, NE) as e:
                    one = bass.ds(e, 1)
                    for j in range(UNITS):
                        sp.wait_ge(w_lo, CR + UNITS * e + j + 1 - NRAW)
                        if j < 2 * NG:
                            src = gu_d[j % 2][:, one, :, j // 2 * WC:(j // 2 + 1) * WC].rearrange("p e k c -> p (e k) c")
                        else:
                            c = (j - 2 * NG) // 2 * WC
                            src = dn_d[:, one, j % 2, :, c:c + WC].rearrange("p e k c -> p (e k) c")
                        sp.dma_start(raw[:, j % NRAW], src).then_inc(w_in[j % NRAW], 16)

            @block.gpsimd
            def _(pool):
                def gather(e):
                    for j in range(2):
                        pool.tensor_copy(rows_x[j][:], slots_i[j][:, bass.ds(e, 1)]).then_inc(row_x, 1)
                    pool.wait_ge(row_x, CR + 2 * e + 2)
                    ph.settle(pool)
                    for j in range(2):
                        pool.indirect_dma_start(xe[j][:], None, h2, bass.IndirectOffsetOnAxis(ap=rows_x[j][:, 0:1], axis=0)).then_inc(x_in[j], 16)

                def hidden(e, tiles):
                    for f in tiles:
                        q, s = FT * e + f, f % 2
                        pool.wait_ge(t_out, CR + TILES * e + f + 1)
                        pool.wait_ge(silu_done, CR + q + 1)
                        pool.tensor_tensor(hid[:, f, 0], sg[:, s], us[:, s], ALU.mult).then_inc(h_hi, 1)
                        pool.tensor_tensor(hf[:, s], sg[:, s], us[:, s], ALU.mult).then_inc(h_mul, 1)
                        pool.wait_ge(h_hi, CR + q + 1)
                        pool.wait_ge(h_mul, CR + q + 1)
                        pool.tensor_tensor(hid[:, f, 1], hf[:, s], hid[:, f, 0].bitcast(F32), ALU.subtract).then_inc(h_lo, 1)

                def body(e, last):
                    if not last:
                        for j in range(2):
                            pool.wait_ge(x_in[j], 16 * e + 16)
                        pool.wait_ge(x_tp, CR + XR * e + XR)
                        gather(e + 1)
                    for j in range(2):
                        pool.tensor_copy(gate[j][:], slots_g[j][:, bass.ds(e, 1)]).then_inc(gate_set, 1)
                    hidden(e, range(EARLY, FT))
                    for j in range(2):
                        pool.tensor_copy(rows_y[j][:], slots_i[j][:, bass.ds(e, 1)]).then_inc(row_y, 1)
                    pool.wait_ge(row_y, CR + 2 * e + 2)
                    pool.wait_ge(y_out, CR + DT * e + DT)
                    ph.settle(pool)
                    for j in range(2):
                        pool.indirect_dma_start(y, bass.IndirectOffsetOnAxis(ap=rows_y[j][:, 0:1], axis=0), ye[j][:], None,
                                                compute_op=ALU.add).then_inc(scattered[j], 16)
                    if not last:
                        hidden(e + 1, range(EARLY))
                    for j in range(2):
                        pool.wait_ge(scattered[j], 16 * e + 16)

                gather(0)
                hidden(0, range(EARLY))
                experts_of(pool, body)

            @block.scalar
            def _(act):
                def high(e, j):
                    e, j = (e, j) if j < UNITS else (e + 1, j - UNITS)
                    act.wait_ge(w_in[j % NRAW], 16 * (UNITS // NRAW * e + j // NRAW) + 16)
                    act.wait_ge(t_full, CR + TILES * e + 2 * (j // 2 - NHL // 2 + 1))
                    act.activation(whl[0][:, j % NHL], raw[:, j % NRAW], ACT.Copy).then_inc(w_hi, 1)

                def x_high(e, rounds):
                    for r in rounds:
                        act.wait_ge(x_tp, CR + XR * e + r + 1)
                        act.activation(xT[:, 2 * r:2 * r + 2, 0], ps_w[:, (FT + r) % 3, 1, 0:2 * CT].rearrange("p (k t) -> p k t", k=2), ACT.Copy).then_inc(x_hi, 1)

                def silu(e, f):
                    q, s = FT * e + f, f % 2
                    act.wait_ge(g_sum, CR + q + 1)
                    act.wait_ge(h_mul, CR + q - 1)
                    act.activation(sg[:, s], gs[:, s], ACT.Silu).then_inc(silu_done, 1)

                def leave(e, m):
                    if m == 0:
                        act.wait_ge(gate_set, CR + 2 * e + 2)
                    act.wait_ge(y_tp, CR + DT * e + m + 1)
                    act.activation(ye[0][:, m * P:(m + 1) * P], ps_t[:, m % 2, 0:CS], ACT.Copy,
                                   scale=gate[0][:]).then_inc(y_half, 1)
                    act.activation(ye[1][:, m * P:(m + 1) * P], ps_t[0:CP, m % 2, P:2 * P], ACT.Copy,
                                   scale=gate[1][:]).then_inc(y_out, 1)

                def body(e, last):
                    for s in range(STEPS):
                        if not (last and s == STEPS - 1):
                            high(e, 2 * s + 2)
                            high(e, 2 * s + 3)
                        for h in range(2):
                            m = 2 * (s - NG) + h
                            if s < NG:
                                silu(e, 2 * s + h)
                            elif m < XR and not last:
                                x_high(e + 1, (m,))
                            if m > 0:
                                leave(e, m - 1)
                    leave(e, DT - 1)

                high(0, 0)
                high(0, 1)
                x_high(0, range(XR))
                experts_of(act, body)

            @block.vector
            def _(dve):
                def low(e, j):
                    e, j = (e, j) if j < UNITS else (e + 1, j - UNITS)
                    dve.wait_ge(w_hi, CR + UNITS * e + j + 1)
                    dve.tensor_tensor(whl[1][:, j % NHL], raw[:, j % NRAW], whl[0][:, j % NHL].bitcast(F32), ALU.subtract).then_inc(w_lo, 1)

                def x_low(e, rounds):
                    for r in rounds:
                        dve.wait_ge(x_hi, CR + XR * e + r + 1)
                        dve.tensor_tensor(xT[:, 2 * r:2 * r + 2, 1], ps_w[:, (FT + r) % 3, 1, 0:2 * CT].rearrange("p (k t) -> p k t", k=2),
                                          xT[:, 2 * r:2 * r + 2, 0].bitcast(F32), ALU.subtract).then_inc(x_lo, 1)

                def tile_out(e, t):
                    dve.wait_ge(t_full, CR + TILES * e + t + 1)
                    if t < FT:
                        q, s = FT * e + t, t % 2
                        dve.wait_ge(silu_done, CR + q - 1)
                        sum2(dve, gs[:, s], ps_w[:, t % 3, 0]).then_inc(g_sum, 1)
                        dve.wait_ge(h_mul, CR + q - 1)
                        sum2(dve, us[:, s], ps_w[:, t % 3, 1]).then_inc(t_out, 1)
                    else:
                        m = t - FT
                        dve.wait_ge(y_tp, CR + DT * e + m - 1)
                        sum2(dve, yT[:, m % 2], ps_w[:, t % 3, 0]).then_inc(t_out, 1)

                def body(e, last):
                    for s in range(STEPS):
                        if not (last and s == STEPS - 1):
                            low(e, 2 * s + 2)
                            low(e, 2 * s + 3)
                        for h in range(2):
                            if 0 <= 2 * (s - NG) + h < XR and not last:
                                x_low(e + 1, (2 * (s - NG) + h,))
                            tile_out(e, 2 * s + h)

                low(0, 0)
                low(0, 1)
                x_low(0, range(XR))
                experts_of(dve, body)

            @block.tensor
            def _(pe):
                def turn_x(e, rounds):
                    for j in range(2):
                        pe.wait_ge(x_in[j], 16 * e + 16)
                    for r in rounds:
                        pe.wait_ge(x_lo, CR + XR * e + r - 2)
                        for h in range(2):
                            k, c = 2 * r + h, h * CT
                            pe.transpose(ps_w[:, (FT + r) % 3, 1, c:c + CS], xe[0][:, k * P:(k + 1) * P], cst["ident"])
                            tr = pe.transpose(ps_w[:, (FT + r) % 3, 1, c + CS:c + CT], xe[1][:, k * P:(k + 1) * P], cst["ident"][0:CP, 0:CP])
                        tr.then_inc(x_tp, 1)

                def turn_y(e, m):
                    pe.wait_ge(t_out, CR + TILES * e + FT + m + 1)
                    pe.wait_ge(y_out, CR + DT * e + m - 1)
                    pe.transpose(ps_t[0:CS, m % 2, 0:P], yT[:, m % 2, 0:CS], cst["ident"])
                    pe.transpose(ps_t[0:CP, m % 2, P:2 * P], yT[:, m % 2, CS:CT], cst["ident"]).then_inc(y_tp, 1)

                def products(bank, slot, k, cols, x, first, last):
                    pe.matmul(bank[:, 0:2 * CT], whl[0][:, slot, k, cols], x, start=first, stop=False)
                    return pe.matmul(bank[:, CT:2 * CT], whl[1][:, slot, k, cols], x[:, 0], start=False, stop=last)

                def body(e, last):
                    for s in range(STEPS):
                        pe.wait_ge(w_lo, CR + UNITS * e + 2 * s + 2)
                        if s == 0:
                            pe.wait_ge(x_lo, CR + XR * e + XR)
                        for h in range(2):
                            t, cols = 2 * s + h, slice(h * P, (h + 1) * P)
                            pe.wait_ge(t_out, CR + TILES * e + t - 2)
                            if 0 <= t - FT < XR and not last:
                                turn_x(e + 1, (t - FT,))
                            if s < NG:
                                for u in range(2):
                                    for k in range(KC):
                                        mm = products(ps_w[:, t % 3, u], (2 * s + u) % NHL, k, cols, xT[:, k], k == 0, k == KC - 1)
                            else:
                                for u in range(2):
                                    pe.wait_ge(h_lo, CR + FT * e + KC * (u + 1))
                                    for k in range(KC):
                                        mm = products(ps_w[:, t % 3, 0], (2 * s + u) % NHL, k, cols, hid[:, u * KC + k],
                                                      u + k == 0, u == 1 and k == KC - 1)
                            mm.then_inc(t_full, 1)
                            if t > FT:
                                turn_y(e, t - FT - 1)
                    turn_y(e, DT - 1)

                turn_x(0, range(XR))
                experts_of(pe, body)


def program(nc, dram):
    with ExitStack() as ctx:
        ident = ctx.enter_context(nc.sbuf_tensor("identity", [P, P], F32))
        eps = ctx.enter_context(nc.sbuf_tensor("eps", [P, 2], F32))
        slots_i = [ctx.enter_context(nc.sbuf_tensor(f"slots_i{j}", [n, NE], U32)) for j, n in enumerate((CS, CP))]
        slots_g = [ctx.enter_context(nc.sbuf_tensor(f"slots_g{j}", [n, NE], F32)) for j, n in enumerate((CS, CP))]
        scratch = lambda name, shape: nc.dram_tensor(name, shape, F32, kind="Internal").ap()
        proj_t, proj_c = scratch("proj_t", (T, NB * UW)), scratch("proj_c", (NA * UW, T))
        att_g, merged, h2 = scratch("att_gated", (D, T)), scratch("merged", (D, T)), scratch("h2", (T, D))
        cst = {"ident": ident[:], "eps": eps[:, 0:1], "one": eps[:, 1:2]}
        consts_in = ctx.enter_context(nc.semaphore("consts_in"))
        eps_set = ctx.enter_context(nc.semaphore("eps_set"))
        with nc.Block() as block:

            @block.sync
            def _(sp):
                sp.dma_start(ident[:], dram["ident"]).then_inc(consts_in, 16)
                sp.wait_ge(consts_in, 16)

            @block.vector
            def _(dve):
                dve.memset(cst["eps"], EPS).then_inc(eps_set, 1)
                dve.memset(cst["one"], 1.0).then_inc(eps_set, 1)
                dve.wait_ge(eps_set, 2)

        with ExitStack() as mixer:
            act_hl = mixer.enter_context(nc.sbuf_tensor("act_hl", [P, 2, KC, T], F32R))
            rT = [mixer.enter_context(nc.sbuf_tensor(f"codes{d}", [RANK, T], F32)) for d in range(2)]
            project(nc, dram["x"], dram["w_cols"], dram["norm_mix"], cst, act_hl, proj_t, proj_c, rT)
            with ExitStack() as kvs:
                kT = kvs.enter_context(nc.sbuf_tensor("kT", [P, 2, KVH, T], F32R))
                vv = kvs.enter_context(nc.sbuf_tensor("vv", [P, 2, NT, KVH * HD], F32R))
                keys(nc, proj_t, dram["k_norm"], dram["cos"], dram["sin"], cst, kT, vv)
                attention(nc, proj_t, dram["q_norm"], dram["cos"], dram["sin"], cst, kT, vv, act_hl)
            mix(nc, "ma", act_hl, dram["w_o_att"], proj_c[C_ZB:C_ZB + D], att_g)
            gla(nc, proj_t, proj_c, (dram["w_gk_f"], dram["w_gk_b"]), (dram["b_gk_f"], dram["b_gk_b"]),
                dram["gla_norm"], dram["masks"], rT, cst, act_hl)
            mix(nc, "mg", act_hl, dram["w_o_gla"], proj_c[C_ZA:C_ZA + D], merged, add=att_g)
        with ExitStack() as router:
            affT = router.enter_context(nc.sbuf_tensor("affT", [NE, T], F32))
            finish_mixer(nc, dram["x"], merged, dram["w_out"], dram["norm_ffn"], dram["w_router"], cst, dram["y"], h2, affT)
            choose(nc, affT, cst, slots_i, slots_g)
        experts(nc, h2, dram["y"], dram["w_e_gate"], dram["w_e_up"], dram["w_e_down"], slots_i, slots_g, cst)


W_IN_ORDER = [(3104, 4128), (4128, 4640), (1024, 2048), (2048, 3072), (0, 1024), (4640, 6688), (3072, 3104)]


def rope_tables():
    pos = np.concatenate([np.arange(TS), np.arange(TP)])
    half = HD // 2
    inv = (10000.0 ** (-np.arange(0, half, 2, dtype=np.float32) / half)).astype(np.float32)
    ang = np.concatenate([(pos // GRID_W).astype(np.float32)[:, None] * inv,
                          (pos % GRID_W).astype(np.float32)[:, None] * inv], axis=1)
    return np.cos(ang), np.sin(ang)


def chunk_masks():
    j, i = np.arange(P)[:, None], np.arange(P)[None, :]
    same = j // CH == i // CH
    return np.stack([same & (i >= j), same & (i <= j)]).astype(np.float32)


def kernel(**inputs):
    import concourse.bacc as _bacc
    from concourse import mybir as _mybir
    from concourse.bass_utils import run_bass_kernel_spmd as _run

    given = {k: np.asarray(v) for k, v in inputs.items()}
    cos, sin = rope_tables()
    arrays = {
        "x": np.concatenate([given["x_sample"][0], given["x_prompt"][0]]),
        "w_cols": np.concatenate([given["w_in"][0][:, a:b] for a, b in W_IN_ORDER], axis=1),
        "ident": np.eye(P, dtype=np.float32), "cos": cos, "sin": sin, "masks": chunk_masks(),
    }
    for name in ("norm_mix", "b_gk_f", "b_gk_b", "gla_norm", "q_norm", "k_norm", "norm_ffn"):
        arrays[name] = given[name]
    for name in ("w_gk_f", "w_gk_b", "w_o_gla", "w_o_att", "w_out", "w_router", "w_e_gate", "w_e_up", "w_e_down"):
        arrays[name] = given[name][0]
    arrays = {k: np.ascontiguousarray(v) for k, v in arrays.items()}

    nc = _bacc.Bacc("TRN2", target_bir_lowering=False, num_devices=1)
    dram = {k: nc.dram_tensor(k, v.shape, _mybir.dt.from_np(v.dtype), kind="ExternalInput").ap() for k, v in arrays.items()}
    dram["y"] = nc.dram_tensor("y", (T, D), _mybir.dt.from_np(np.dtype("float32")), kind="ExternalOutput").ap()
    program(nc, dram)
    y = _run(nc, [arrays], core_ids=[0]).results[0]["y"]
    return y[TS:][None], y[:TS][None]
```

```python
from contextlib import ExitStack

import numpy as np

import concourse.bass as bass
from concourse import mybir

ALU = mybir.AluOpType
ACT = mybir.ActivationFunctionType
AX = mybir.AxisListType
F32 = mybir.dt.float32
F32R = mybir.dt.float32r
BF16 = mybir.dt.bfloat16
U32 = mybir.dt.uint32
U8 = mybir.dt.uint8

P = 128
D = 1024
TS, TP = 1024, 256
T = TS + TP
NT, NTS = T // P, TS // P
KC = D // P
GRID_W = 64
GH, DK, DV, RANK, CH = 4, 128, 256, 16, 64
NCH, NCHS = T // CH, TS // CH
GATE_NORM = 16.0
AH, KVH, HD = 8, 2, 128
GR = AH // KVH
HEADS = AH + KVH
NE, FF = 16, 2048
CS, CP = 2 * TS // NE, 2 * TP // NE
CT = CS + CP
EPS = 1e-6
UW = 512
MU = UW // P
NB, NA = 7, 6
G_Q, G_KV, G_V, G_G = 0, 2, 3, 5
C_Q, C_K, C_ZA, C_ZB = 0, 512, 1024, 2048
TOK3 = [(0, 512), (512, 1024), (1024, T)]


CR = 8
ST = 16


class Phase:

    def __init__(self, nc, ctx, tag):
        self.nc, self.ctx, self.tag, self.counted, self.stores = nc, ctx, tag, [], []
        self.passed = self.ctx.enter_context(nc.semaphore(f"{tag}_passed"))

    def sb(self, name, shape, dt=F32):
        return self.ctx.enter_context(self.nc.sbuf_tensor(f"{self.tag}_{name}", shape, dt))

    def ps(self, name, shape):
        return self.ctx.enter_context(self.nc.psum_tensor(f"{self.tag}_{name}", shape, F32))

    def landed(self, name, n=1):
        s = [self.nc.alloc_semaphore(f"{self.tag}_{name}{i}") for i in range(n)]
        return s if n > 1 else s[0]

    def stored(self, name, n):
        s = [self.ctx.enter_context(self.nc.semaphore(f"{self.tag}_{name}{i}")) for i in range(n)]
        self.stores += s
        return s

    def done(self, *names):
        s = [self.ctx.enter_context(self.nc.semaphore(f"{self.tag}_{n}")) for n in names]
        self.counted += s
        return s if len(s) > 1 else s[0]

    def start(self, sp):
        for s in self.counted:
            sp.sem_inc(s, CR)
        for s in self.stores:
            sp.sem_inc(s, ST)

    def settle(self, eng):
        eng.sem_inc(self.passed, 1)

    def clear(self):
        with self.nc.Block() as block:

            @block.gpsimd
            def _(pool):
                nums = sorted(s.num for s in self.counted + self.stores + [self.passed])
                begins = [n for n in nums if n - 1 not in nums]
                ends = [n + 1 for n in nums if n + 1 not in nums]
                for a, b in zip(begins, ends):
                    pool.sem_clear(range(a, b))


def three_passes(pe, out, a, b, first, last):
    pe.matmul(out, a[0], b[0], start=first, stop=False)
    pe.matmul(out, a[0], b[1], start=False, stop=False)
    return pe.matmul(out, a[1], b[0], start=False, stop=last)


def channel_tile(pe, banks, w, act, full):
    for k in range(KC):
        for part, other in ((0, 0), (0, 1), (1, 0)):
            for c, (a, b) in enumerate(TOK3):
                mm = pe.matmul(banks[:, c, 0:b - a], w(part, k), act(other, k, a, b),
                               start=(k == 0 and part == other), stop=(k == KC - 1 and part == 1))
                if k == KC - 1 and part == 1:
                    mm.then_inc(full, 1)


def pairs(t, e):
    return t.rearrange("... (d e) -> ... d e", e=2)[..., e]


def project(nc, x, w_cols, norm_mix, qk_norms, cos, sin, cst, act_hl, proj_t, proj_c, rT, ss):
    with ExitStack() as ctx:
        ph = Phase(nc, ctx, "pj")
        gamma = ph.sb("gamma", [P, D])
        ssq, root, rstd = ph.sb("ssq", [P, 2]), ph.sb("root", [P, 2]), ph.sb("rstd", [P, 2])
        raw = ph.sb("w_raw", [P, 2, KC, UW])
        xs = raw[:, 1].rearrange("p k c -> p (k c)").rearrange("p (j s d) -> p j s d", j=2, s=2)
        xt, xn = xs[:, 0], xs[:, 1]
        whi, wlo = ph.sb("w_hi", [P, 2, KC, UW], F32R), ph.sb("w_lo", [P, 2, KC, UW], F32R)
        rraw = ph.sb("r_raw", [P, KC, 2 * RANK])
        rhi, rlo = ph.sb("r_hi", [P, KC, 2 * RANK], F32R), ph.sb("r_lo", [P, KC, 2 * RANK], F32R)
        stage = ph.sb("stage", [P, 2, UW])
        ps_c, ps_t = ph.ps("ps_chan", [P, 2, 3, 512]), ph.ps("ps_tok", [P, 2, 512])
        gamma_in, x_in, w_in, r_in = ph.landed("gamma_in"), ph.landed("x_in", 2), ph.landed("w_in", 2), ph.landed("r_in")
        squared, rooted, inverted, x_ready = ph.done("squared", "rooted", "inverted", "x_ready")
        turned, h_hi, h_lo = ph.done("turned", "h_hi", "h_lo")
        w_hi, w_lo, r_hi, r_lo = ph.done("w_hid", "w_lod", "r_hid", "r_lod")
        p_full, p_out = ph.done("p_full", "p_out")
        stored = ph.stored("stored", 2)
        HH = HEADS // 2
        heads = gamma[:, 0:HH * HD].rearrange("p (h d) -> p h d", d=HD)
        scaled, first, second = ph.sb("h_scaled", [P, HH, HD]), ph.sb("h_first", [P, HH, HD // 2]), ph.sb("h_second", [P, HH, HD // 2])
        tab, gains = ph.sb("tables", [P, 2, HD // 2]), ph.sb("qk_gains", [P, 2, HD])
        gains_in, tab_in, h_in, h_back = (ph.landed(n) for n in ("gains_in", "tab_in", "h_in", "h_back"))
        h_step = ph.done("h_step")
        WIDTHS = [HD >> i for i in range(1, HD.bit_length())]
        HSTEPS = 10 + len(WIDTHS)
        x_d = x.rearrange("(n p) d -> p n d", p=P)
        w_d = w_cols.rearrange("(k p) c -> p k c", p=P)
        t_d = proj_t.rearrange("(n p) c -> p n c", p=P)
        tok_n, chan_n = NB * NT, NA * MU * 3
        turn_ps = [ps_c[:, s, 0:2].rearrange("p a (k t) -> p (a k) t", t=P) for s in range(2)]
        squares = stage[:].rearrange("p s c -> p (s c)")
        pair = NT // 2

        def tiles(eng, body, before_last=None):
            with eng.Fori(0, pair - 1) as i:
                for s in range(2):
                    body(2 * i + s, s, i)
            if before_last:
                before_last()
            for s in range(2):
                body(NT - 2 + s, s, pair - 1)

        more = lambda n, ahead: not isinstance(n, int) or n + ahead < NT

        with nc.Block() as block:

            @block.sync
            def _(sp):
                def store(q, s, dst, width):
                    sp.wait_ge(p_out, CR + q + 1)
                    sp.dma_start(dst, stage[:, s, 0:width]).then_inc(stored[s], 16)

                ph.start(sp)

                def load_x(n, s, i):
                    sp.wait_ge(x_ready, CR + n - 1)
                    sp.dma_start(xt[:, s], x_d[:, bass.ds(n, 1)].rearrange("p n d -> p (n d)")).then_inc(x_in[s], 16)

                tiles(sp, load_x, lambda: sp.dma_start(raw[:, 0], w_d[:, :, 0:UW]).then_inc(w_in[0], 16))
                sp.wait_ge(h_lo, CR + NT)
                sp.dma_start(raw[:, 1], w_d[:, :, UW:2 * UW]).then_inc(w_in[1], 16)
                with sp.Fori(0, NB) as n:
                    for t in range(NT):
                        store(n * NT + t, t % 2, t_d[:, t, bass.ds(n * UW, UW)], UW)
                with sp.Fori(0, NA) as n:
                    for q in range(3 * MU):
                        a, b = TOK3[q % 3]
                        store(tok_n + n * (3 * MU) + q, q % 2, proj_c[bass.ds(n * UW + q // 3 * P, P), a:b], b - a)
                for s in range(2):
                    sp.wait_ge(stored[s], ST + 16 * (tok_n + chan_n) // 2)

            @block.gpsimd
            def _(pool):
                pool.dma_start(gamma[:], norm_mix.to_broadcast([P, D])).then_inc(gamma_in, 16)
                pool.dma_start(rraw[:], w_d[:, :, (NA + NB) * UW:(NA + NB) * UW + 2 * RANK]).then_inc(r_in, 16)
                pool.wait_ge(h_lo, CR + NT)
                for j, g in enumerate(qk_norms):
                    pool.dma_start(gains[:, j], g.to_broadcast([P, HD])).then_inc(gains_in, 16)
                pool.wait_ge(gains_in, 32)
                for s in range(2):
                    pool.wait_ge(stored[s], ST + 16 * G_V * NT // 2)

                def rotate(n, h):
                    c = 2 * n + h
                    b = CR + HSTEPS * c
                    rows = t_d[:, bass.ds(n, 1), h * HH * HD:(h + 1) * HH * HD].rearrange("p n c -> p (n c)")
                    flat = gamma[:, 0:HH * HD]
                    pool.dma_start(flat, rows).then_inc(h_in, 16)
                    if h == 0:
                        for j, src in enumerate((cos, sin)):
                            pool.dma_start(tab[:, j], src.rearrange("(n p) d -> p n d", p=P)[:, bass.ds(n, 1)].rearrange("p n d -> p (n d)")
                                           ).then_inc(tab_in, 16)
                        pool.wait_ge(tab_in, 32 * n + 32)
                    pool.wait_ge(h_in, 16 * c + 16)
                    pool.tensor_tensor(scaled[:], heads, heads, ALU.mult).then_inc(h_step, 1)
                    pool.wait_ge(h_step, b + 1)
                    for i, w in enumerate(WIDTHS):
                        pool.tensor_tensor(scaled[:, :, 0:w], scaled[:, :, 0:w], scaled[:, :, w:2 * w], ALU.add).then_inc(h_step, 1)
                        pool.wait_ge(h_step, b + 2 + i)
                    ph.settle(pool)
                    pool.tensor_copy(ss[:, bass.ds(n, 1), h * HH:(h + 1) * HH].rearrange("p n h -> p (n h)"), scaled[:, :, 0]).then_inc(h_step, 1)
                    b = b + len(WIDTHS)
                    pool.wait_ge(h_step, b + 2)
                    for sl, g in ((slice(0, 3), 0), (slice(3, HH), h)):
                        pool.tensor_tensor(scaled[:, sl], heads[:, sl],
                                           gains[:, g:g + 1].broadcast_to([P, sl.stop - sl.start, HD]), ALU.mult).then_inc(h_step, 1)
                    pool.wait_ge(h_step, b + 4)
                    cs, sn = (tab[:, j:j + 1].broadcast_to([P, HH, HD // 2]) for j in range(2))
                    for e, op in ((0, ALU.subtract), (1, ALU.add)):
                        pool.tensor_tensor(first[:], pairs(scaled[:], e), cs, ALU.mult).then_inc(h_step, 1)
                        pool.tensor_tensor(second[:], pairs(scaled[:], 1 - e), sn, ALU.mult).then_inc(h_step, 1)
                        pool.wait_ge(h_step, b + 6 + 3 * e)
                        pool.tensor_tensor(pairs(heads, e), first[:], second[:], op).then_inc(h_step, 1)
                        pool.wait_ge(h_step, b + 7 + 3 * e)
                    ph.settle(pool)
                    pool.dma_start(rows, flat).then_inc(h_back, 16)
                    pool.wait_ge(h_back, 16 * c + 16)
                    ph.settle(pool)

                with pool.Fori(0, NT) as n:
                    for h in range(2):
                        rotate(n, h)

            @block.scalar
            def _(act):
                def square(n, s, i):
                    act.wait_ge(x_in[s], 16 * i + 16)
                    act.wait_ge(squared, CR + n)
                    act.wait_ge(rooted, CR + n - 1)
                    act.activation(squares, xt[:, s], ACT.Square, accum_out=ssq[:, s:s + 1]).then_inc(squared, 1)

                def square_root(n, s):
                    act.wait_ge(squared, CR + n + 1)
                    act.wait_ge(inverted, CR + n - 1)
                    act.activation(root[:, s:s + 1], ssq[:, s:s + 1], ACT.Sqrt, scale=1.0 / D,
                                   bias=cst["eps"]).then_inc(rooted, 1)

                def tile_hi(n, s, i):
                    if more(n, 1):
                        square_root(n + 1, 1 - s)
                    if more(n, 2):
                        square(n + 2, s, i + 1)
                    act.wait_ge(turned, CR + n + 1)
                    act.activation(act_hl[:, 0, :, bass.ds(n * P, P)], turn_ps[s], ACT.Copy).then_inc(h_hi, 1)

                def load_w(n, s):
                    act.wait_ge(w_lo, CR + n - 1)
                    act.dma_start(raw[:, s], w_d[:, :, bass.ds(n * UW, UW)]).then_inc(w_in[s], 16)

                def hi(s, landed):
                    act.wait_ge(w_in[s], landed)
                    act.activation(whi[:, s], raw[:, s], ACT.Copy).then_inc(w_hi, 1)

                def evac(q, s, use, src, width):
                    act.wait_ge(p_full, CR + q + 1)
                    act.wait_ge(stored[s], ST + 16 * use)
                    act.activation(stage[:, s, 0:width], src, ACT.Copy).then_inc(p_out, 1)

                def evac_tok(n):
                    for t in range(NT):
                        evac(n * NT + t, t % 2, n * (NT // 2) + t // 2, ps_t[:, t % 2], UW)

                def evac_chan(n):
                    for q in range(3 * MU):
                        a, b = TOK3[q % 3]
                        evac(tok_n + n * (3 * MU) + q, q % 2, tok_n // 2 + n * (3 * MU // 2) + q // 2,
                             ps_c[:, q // 3 % 2, q % 3, 0:b - a], b - a)

                square(0, 0, 0)
                square_root(0, 0)
                square(1, 1, 0)
                tiles(act, tile_hi, lambda: hi(0, 16))
                act.wait_ge(r_in, 16)
                act.activation(rhi[:], rraw[:], ACT.Copy).then_inc(r_hi, 1)
                hi(1, 16)
                with act.Fori(0, NB // 2) as i:
                    for s in range(2):
                        load_w(2 * i + s + 2, s)
                        evac_tok(2 * i + s)
                        hi(s, 16 * i + 32)
                load_w(NB + 1, 0)
                evac_tok(NB - 1)
                hi(0, 16 * (NB // 2) + 32)
                with act.Fori(0, NA // 2 - 1) as i:
                    for s in range(2):
                        load_w(2 * i + s + NB + 2, 1 - s)
                        evac_chan(2 * i + s)
                        hi(1 - s, 16 * i + 16 * (NB // 2 + 2 + s))
                for n in range(NA - 2, NA):
                    evac_chan(n)
                for d in range(2):
                    act.wait_ge(p_full, CR + tok_n + chan_n + 1)
                    act.activation(rT[d][:], ps_c[0:RANK, d].rearrange("p c n -> p (c n)")[:, 0:T], ACT.Copy).then_inc(p_out, 1)

            @block.vector
            def _(dve):
                dve.wait_ge(gamma_in, 16)

                def norm(n, s):
                    dve.wait_ge(rooted, CR + n + 1)
                    dve.reciprocal(rstd[:, s:s + 1], root[:, s:s + 1]).then_inc(inverted, 1)
                    dve.wait_ge(inverted, CR + n + 1)
                    dve.wait_ge(turned, CR + n - 1)
                    dve.scalar_tensor_tensor(out=xn[:, s], in0=xt[:, s], scalar=rstd[:, s:s + 1], in1=gamma[:],
                                             op0=ALU.mult, op1=ALU.mult).then_inc(x_ready, 1)

                def tile_lo(n, s, i):
                    if more(n, 1):
                        norm(n + 1, 1 - s)
                    dve.wait_ge(h_hi, CR + n + 1)
                    dve.tensor_tensor(act_hl[:, 1, :, bass.ds(n * P, P)], turn_ps[s],
                                      act_hl[:, 0, :, bass.ds(n * P, P)].bitcast(F32), ALU.subtract).then_inc(h_lo, 1)

                def lo(s, n):
                    dve.wait_ge(w_hi, CR + n + 1)
                    dve.tensor_tensor(wlo[:, s], raw[:, s], whi[:, s].bitcast(F32), ALU.subtract).then_inc(w_lo, 1)

                norm(0, 0)
                tiles(dve, tile_lo, lambda: lo(0, 0))
                dve.wait_ge(r_hi, CR + 1)
                dve.tensor_tensor(rlo[:], rraw[:], rhi[:].bitcast(F32), ALU.subtract).then_inc(r_lo, 1)
                with dve.Fori(0, (NB + NA) // 2) as i:
                    for s in range(2):
                        lo(1 - s, 2 * i + s + 1)

            @block.tensor
            def _(pe):
                def turn(n, s, i):
                    pe.wait_ge(x_ready, CR + n + 1)
                    pe.wait_ge(h_lo, CR + n - 1)
                    for k in range(KC):
                        tr = pe.transpose(ps_c[:, s, k // 4, k % 4 * P:k % 4 * P + P], xn[:, s, k * P:(k + 1) * P], cst["ident"])
                    tr.then_inc(turned, 1)

                tiles(pe, turn)
                pe.wait_ge(h_lo, CR + NT)

                def unit_tok(n, s):
                    pe.wait_ge(w_lo, CR + n + 1)
                    for t in range(NT):
                        pe.wait_ge(p_out, CR + n * NT + t - 1)
                        for k in range(KC):
                            mm = three_passes(pe, ps_t[:, t % 2], [act_hl[:, j, k, t * P:(t + 1) * P] for j in range(2)],
                                              (whi[:, s, k], wlo[:, s, k]), k == 0, k == KC - 1)
                        mm.then_inc(p_full, 1)

                def unit_chan(n, s):
                    pe.wait_ge(w_lo, CR + NB + n + 1)
                    for m in range(MU):
                        pe.wait_ge(p_out, CR + tok_n + (n * MU + m - 1) * 3)
                        channel_tile(pe, ps_c[:, m % 2], lambda j, k: (whi, wlo)[j][:, s, k, m * P:(m + 1) * P],
                                     lambda j, k, a, b: act_hl[:, j, k, a:b], p_full)

                with pe.Fori(0, NB // 2) as i:
                    for s in range(2):
                        unit_tok(2 * i + s, s)
                unit_tok(NB - 1, 0)
                with pe.Fori(0, NA // 2) as i:
                    for s in range(2):
                        unit_chan(2 * i + s, 1 - s)
                pe.wait_ge(r_lo, CR + 1)
                pe.wait_ge(p_out, CR + tok_n + chan_n)
                for d in range(2):
                    for c, (a, b) in enumerate(TOK3):
                        for k in range(KC):
                            cols = slice(d * RANK, (d + 1) * RANK)
                            mm = three_passes(pe, ps_c[0:RANK, d, c, 0:b - a], (rhi[:, k, cols], rlo[:, k, cols]),
                                              [act_hl[:, j, k, a:b] for j in range(2)], k == 0, k == KC - 1)
                mm.then_inc(p_full, 1)

        ph.clear()


def keys(nc, proj_t, ss, inv, cst, kT, vv):
    with ExitStack() as ctx:
        ph = Phase(nc, ctx, "ky")
        W = KVH * HD
        kv = ph.sb("kv", [P, NT, 2 * W])
        kr, root = ph.sb("normed", [P, NT, KVH, HD]), ph.sb("root", [P, NT, HEADS])
        ps = ph.ps("turned", [P, KVH, T])
        kv_in = ph.landed("kv_in", 2)
        rooted, inverted, normed, turned, k_hi, k_lo, v_hi, v_lo = ph.done(
            "rooted", "inverted", "normed", "tp", "k_hid", "k_lod", "v_hid", "v_lod")
        k = kv[:, :, 0:W].rearrange("p n (h d) -> p n h d", d=HD)

        with nc.Block() as block:

            @block.sync
            def _(sp):
                ph.start(sp)
                for j in range(2):
                    half = slice(j * NT // 2, (j + 1) * NT // 2)
                    sp.dma_start(kv[:, half], proj_t.rearrange("(n p) c -> p n c", p=P)[:, half, G_KV * UW:(G_KV + 1) * UW]).then_inc(kv_in[j], 16)

            @block.scalar
            def _(act):
                act.activation(root[:, :, 0:AH], ss[:, :, 0:AH], ACT.Sqrt, bias=cst["eps_hd"]).then_inc(rooted, 1)
                act.activation(root[:, :, AH:], ss[:, :, AH:], ACT.Sqrt, scale=1.0 / HD, bias=cst["eps"]).then_inc(rooted, 1)
                act.wait_ge(kv_in[0], 16)
                act.wait_ge(kv_in[1], 16)
                act.activation(vv[:, 0], kv[:, :, W:2 * W], ACT.Copy).then_inc(v_hi, 1)
                act.wait_ge(turned, CR + 1)
                act.activation(kT[:, 0], ps[:], ACT.Copy).then_inc(k_hi, 1)

            @block.vector
            def _(dve):
                dve.wait_ge(rooted, CR + 2)
                dve.reciprocal(inv[:], root[:]).then_inc(inverted, 1)
                dve.wait_ge(inverted, CR + 1)
                for j in range(2):
                    half = slice(j * NT // 2, (j + 1) * NT // 2)
                    dve.wait_ge(kv_in[j], 16)
                    dve.tensor_tensor(kr[:, half], k[:, half], inv[:, half, AH:].unsqueeze(3).broadcast_to([P, NT // 2, KVH, HD]),
                                      ALU.mult).then_inc(normed, 1)
                dve.wait_ge(v_hi, CR + 1)
                dve.tensor_tensor(vv[:, 1], kv[:, :, W:2 * W], vv[:, 0].bitcast(F32), ALU.subtract).then_inc(v_lo, 1)
                dve.wait_ge(k_hi, CR + 1)
                dve.tensor_tensor(kT[:, 1], ps[:], kT[:, 0].bitcast(F32), ALU.subtract).then_inc(k_lo, 1)

            @block.tensor
            def _(pe):
                for n in range(NT):
                    if n % (NT // 2) == 0:
                        pe.wait_ge(normed, CR + 1 + n // (NT // 2))
                    for h in range(KVH):
                        tr = pe.transpose(ps[:, h, n * P:(n + 1) * P], kr[:, n, h], cst["ident"])
                tr.then_inc(turned, 1)

        ph.clear()


def attention(nc, proj_t, inv, cst, kT, vv, act_hl):
    with ExitStack() as ctx:
        ph = Phase(nc, ctx, "at")
        qT = ph.sb("qT", [P, 2, AH, P], F32R)
        pT = ph.sb("pT", [P, 2, 2, NTS, 2, P], F32R)
        prob = ph.sb("prob", [P, 2, TS])
        q_in, q_r = ph.sb("q_in", [P, AH, HD]), ph.sb("q_normed", [P, AH, HD])
        nmax, rsum, rinv = (ph.sb(n, [P, 2]) for n in ("nmax", "rsum", "rinv"))
        ps_s, ps_p = ph.ps("ps_scores", [P, 2, TS]), ph.ps("ps_probs", [P, 2, 4, P])
        ps_o, ps_q = ph.ps("ps_out", [P, 2, P]), ph.ps("ps_q", [P, GR, P])
        q_land = ph.landed("q_land")
        q_ready, q_tp, q_hi, q_lo = ph.done("q_ready", "q_tp", "q_hid", "q_lod")
        s_full, s_max, s_exp, r_iv, p_ready = ph.done("s_full", "s_max", "s_exp", "r_iv", "p_ready")
        p_tp, p_hi, p_lo, o_full, o_hi, o_lo = ph.done("p_tp", "p_hid", "p_lod", "o_full", "o_hid", "o_lod")
        QT = (5, 7)

        def out_slots(n, u):
            g, r0 = u // 2, 2 * (u % 2)
            src = ps_o[:]
            if isinstance(n, int) and n >= NTS:
                a = TS + TP // GR * r0
                dst = [act_hl[:, j, 2 * g + n - NTS::4, a:a + 2 * TP // GR].rearrange("p e (r q) -> p r q e", r=2) for j in range(2)]
                return dst, src.rearrange("p r (q e) -> p r q e", e=2)
            a = g + TS // GR * r0
            dst = [act_hl[:, j, bass.ds(n, 1), a:a + 2 * TS // GR - g:2].rearrange("p o (r q) -> p (o r) q", r=2) for j in range(2)]
            return dst, src

        def ahead(n, h, L):
            if h < AH:
                return n, h, L
            return n + 1, h - AH, TP if isinstance(n, int) and n >= NTS - 1 else TS

        def behind(n, h, L, by=1):
            u = h // 2 - by
            if u >= 0:
                return n, u, L
            if isinstance(n, int) and n == 0:
                return None
            return n - 1, u + 4, TS if not isinstance(n, int) or n <= NTS else TP

        def tiles(eng, body):
            body(0, TS, True)
            with eng.Fori(1, NTS - 1) as n:
                body(n, TS, True)
            body(NTS - 1, TS, True)
            for n in range(NTS, NT):
                body(n, TP, n < NT - 1)

        with nc.Block() as block:

            @block.sync
            def _(sp):
                ph.start(sp)

            @block.gpsimd
            def _(pool):
                with pool.Fori(0, NT) as n:
                    pool.wait_ge(q_ready, CR + n)
                    pool.dma_start(q_in[:].rearrange("p h d -> p (h d)"),
                                   proj_t.rearrange("(n p) c -> p n c", p=P)[:, bass.ds(n, 1), 0:AH * HD].rearrange("p n c -> p (n c)")
                                   ).then_inc(q_land, 16)
                    pool.wait_ge(q_land, 16 * n + 16)
                    pool.wait_ge(q_tp, CR + 2 * n)
                    ph.settle(pool)
                    rms = inv[:, bass.ds(n, 1), 0:AH].rearrange("p n h -> p (n h)").unsqueeze(2).broadcast_to([P, AH, HD])
                    pool.tensor_tensor(q_r[:], q_in[:], rms, ALU.mult).then_inc(q_ready, 1)

            @block.scalar
            def _(act):
                def q_high(n, g):
                    act.wait_ge(q_tp, CR + 2 * n + g + 1)
                    act.activation(qT[:, 0, GR * g:GR * g + GR], ps_q[:], ACT.Copy).then_inc(q_hi, 1)

                def exp(n, h, L):
                    H, s = 8 * n + h, h % 2
                    act.wait_ge(s_max, CR + H + 1)
                    act.wait_ge(p_tp, CR + 2 * H - 2)
                    act.activation(prob[:, s, 0:L], ps_s[:, s, 0:L], ACT.Exp, bias=nmax[:, s:s + 1],
                                   accum_out=rsum[:, s:s + 1]).then_inc(s_exp, 1)

                def high(n, h, L):
                    H, hb = 8 * n + h, L // P // 2
                    for j in range(2):
                        act.wait_ge(p_tp, CR + 2 * H + j + 1)
                        act.wait_ge(o_full, CR + 4 * n + h // 2 - 1)
                        act.activation(pT[:, 0, h // 2 % 2, hb * j:hb * j + hb, h % 2], ps_p[:, j, 0:hb], ACT.Copy).then_inc(p_hi, 1)

                def out_high(n, u, L):
                    dst, src = out_slots(n, u)
                    act.wait_ge(o_full, CR + 4 * n + u + 1)
                    act.activation(dst[0], src, ACT.Copy).then_inc(o_hi, 1)

                def body(n, L, more):
                    for h in range(AH):
                        if h % 2 == 0 and behind(n, h, L, 2):
                            out_high(*behind(n, h, L, 2))
                        if more or h + 1 < AH:
                            exp(*ahead(n, h + 1, L))
                        if h in QT and more:
                            q_high(n + 1, QT.index(h))
                        high(n, h, L)

                for g in range(2):
                    q_high(0, g)
                exp(0, 0, TS)
                tiles(act, body)
                for u in (2, 3):
                    out_high(NT - 1, u, TP)

            @block.vector
            def _(dve):
                def q_low(n, g):
                    dve.wait_ge(q_hi, CR + 2 * n + g + 1)
                    sl = slice(GR * g, GR * g + GR)
                    dve.tensor_tensor(qT[:, 1, sl], ps_q[:], qT[:, 0, sl].bitcast(F32), ALU.subtract).then_inc(q_lo, 1)

                def row_max(n, h, L):
                    H, s = 8 * n + h, h % 2
                    dve.wait_ge(s_full, CR + H + 1)
                    dve.wait_ge(s_exp, CR + H - 1)
                    dve.tensor_reduce(nmax[:, s:s + 1], ps_s[:, s, 0:L], AX.X, ALU.max, negate=True).then_inc(s_max, 1)

                def scale(n, h, L):
                    H, s = 8 * n + h, h % 2
                    dve.wait_ge(s_exp, CR + H + 1)
                    dve.reciprocal(rinv[:, s:s + 1], rsum[:, s:s + 1]).then_inc(r_iv, 1)
                    dve.wait_ge(r_iv, CR + H + 1)
                    dve.tensor_scalar(prob[:, s, 0:L], prob[:, s, 0:L], rinv[:, s:s + 1], None, ALU.mult).then_inc(p_ready, 1)

                def low(n, h, L):
                    H, hb = 8 * n + h, L // P // 2
                    for j in range(2):
                        dve.wait_ge(p_hi, CR + 2 * H + j + 1)
                        dst = slice(hb * j, hb * j + hb)
                        to = [pT[:, i, h // 2 % 2, dst, h % 2] for i in range(2)]
                        dve.tensor_tensor(to[1], ps_p[:, j, 0:hb], to[0].bitcast(F32), ALU.subtract).then_inc(p_lo, 1)

                def out_low(n, u, L):
                    dst, src = out_slots(n, u)
                    dve.wait_ge(o_hi, CR + 4 * n + u + 1)
                    dve.tensor_tensor(dst[1], src, dst[0].bitcast(F32), ALU.subtract).then_inc(o_lo, 1)

                def body(n, L, more):
                    for h in range(AH):
                        if h % 2 == 0 and behind(n, h, L, 2):
                            out_low(*behind(n, h, L, 2))
                        if more or h + 1 < AH:
                            scale(*ahead(n, h + 1, L))
                        if more or h + 2 < AH:
                            row_max(*ahead(n, h + 2, L))
                        if h in QT and more:
                            q_low(n + 1, QT.index(h))
                        low(n, h, L)

                for g in range(2):
                    q_low(0, g)
                row_max(0, 0, TS)
                scale(0, 0, TS)
                row_max(0, 1, TS)
                tiles(dve, body)
                for u in (2, 3):
                    out_low(NT - 1, u, TP)

            @block.tensor
            def _(pe):
                def turn_q(n, g):
                    pe.wait_ge(q_ready, CR + n + 1)
                    pe.wait_ge(q_lo, CR + 2 * n + g)
                    for r in range(GR):
                        tr = pe.transpose(ps_q[:, r], q_r[:, GR * g + r], cst["ident"])
                    tr.then_inc(q_tp, 1)

                def scores(n, h, L):
                    H = 8 * n + h
                    k0 = 0 if L == TS else TS
                    pe.wait_ge(q_lo, CR + 2 * n + h // GR + 1)
                    pe.wait_ge(s_exp, CR + H - 1)
                    for c in range(0, L, 512):
                        w = min(512, L)
                        mm = three_passes(pe, ps_s[:, h % 2, c:c + w], [qT[:, j, h] for j in range(2)],
                                          [kT[:, j, h // GR, k0 + c:k0 + c + w] for j in range(2)], True, True)
                    mm.then_inc(s_full, 1)

                def turn_p(n, h, L):
                    H, hb = 8 * n + h, L // P // 2
                    pe.wait_ge(p_ready, CR + H + 1)
                    for j in range(2):
                        pe.wait_ge(p_lo, CR + 2 * H + j - 1)
                        for b in range(hb):
                            kb = hb * j + b
                            tr = pe.transpose(ps_p[:, j, b], prob[:, h % 2, kb * P:(kb + 1) * P], cst["ident"])
                        tr.then_inc(p_tp, 1)

                def values(n, u, L, half):
                    g = u // 2
                    pe.wait_ge(p_lo, CR + 16 * n + 4 * u + 4)
                    pe.wait_ge(o_lo, CR + 4 * n + u)
                    kb0, nk = (0, NTS) if L == TS else (NTS, NT - NTS)
                    for b in range(half * nk // 2, (half + 1) * nk // 2):
                        mm = three_passes(pe, ps_o[:], [vv[:, j, kb0 + b, g * HD:(g + 1) * HD] for j in range(2)],
                                          [pT[:, j, u % 2, b] for j in range(2)], b == 0, b == nk - 1)
                    if half == 1:
                        mm.then_inc(o_full, 1)

                def body(n, L, more):
                    for h in range(AH):
                        if more or h + 2 < AH:
                            scores(*ahead(n, h + 2, L))
                        if h in QT and more:
                            turn_q(n + 1, QT.index(h))
                        turn_p(n, h, L)
                        if behind(n, h, L):
                            values(*behind(n, h, L), h % 2)

                for g in range(2):
                    turn_q(0, g)
                for h in range(2):
                    scores(0, h, TS)
                tiles(pe, body)
                for half in range(2):
                    values(NT - 1, 3, TP, half)

        ph.clear()


def mix(nc, tag, act_hl, w, z_rows, out, add=None):
    with ExitStack() as ctx:
        ph = Phase(nc, ctx, tag)
        WC = 2 * P
        raw = ph.sb("w_raw", [P, 2, KC, WC])
        whl = [ph.sb(n, [P, 2, KC, WC], F32R) for n in ("w_hi", "w_lo")]
        z, sig, o = ph.sb("z", [P, 2, T]), ph.sb("sig", [P, 2, T]), ph.sb("o", [P, 2, T])
        extra = ph.sb("add", [P, 2, T]) if add is not None else None
        ps = ph.ps("ps", [P, 2, 4, 512])
        w_in, z_in, a_in = ph.landed("w_in", 2), ph.landed("z_in", 2), ph.landed("a_in", 2)
        w_hi, w_lo, full, sig_done, gated, summed = ph.done("w_hid", "w_lod", "full", "sig_done", "gated", "summed")
        stored = ph.stored("stored", 2)
        w_d = w.rearrange("(k p) c -> p k c", p=P)
        NU, PU = D // WC, WC // P
        ready = summed if add is not None else gated

        NT8 = D // P
        units = [(u, u % 2) for u in range(NU)]
        tiles = [(t, t % 2, t // PU, t % PU) for t in range(NT8)]

        with nc.Block() as block:

            @block.sync
            def _(sp):
                ph.start(sp)
                for t, s, _u, _m in tiles:
                    sp.wait_ge(ready, CR + t + 1)
                    sp.dma_start(out[t * P:(t + 1) * P], o[:, s]).then_inc(stored[s], 16)
                for s in range(2):
                    sp.wait_ge(stored[s], ST + 16 * NT8 // 2)

            @block.gpsimd
            def _(pool):
                for u, s in units:
                    pool.wait_ge(w_lo, CR + u - 1)
                    pool.dma_start(raw[:, s], w_d[:, :, u * WC:(u + 1) * WC]).then_inc(w_in[s], 16)
                    for t in range(u * PU, (u + 1) * PU):
                        pool.wait_ge(gated, CR + t - 1)
                        pool.dma_start(z[:, t % 2], z_rows[t * P:(t + 1) * P]).then_inc(z_in[t % 2], 16)
                        if add is not None:
                            pool.wait_ge(summed, CR + t - 1)
                            pool.dma_start(extra[:, t % 2], add[t * P:(t + 1) * P]).then_inc(a_in[t % 2], 16)

            @block.scalar
            def _(act):
                def high(u, s):
                    act.wait_ge(w_in[s], 16 * (u // 2) + 16)
                    if u >= 2:
                        act.wait_ge(full, CR + (u - 1) * PU * 3)
                    act.activation(whl[0][:, s], raw[:, s], ACT.Copy).then_inc(w_hi, 1)

                high(0, 0)
                for t, s, u, m in tiles:
                    if m == 0 and u + 1 < NU:
                        high(u + 1, (u + 1) % 2)
                    act.wait_ge(z_in[s], 16 * (t // 2) + 16)
                    act.wait_ge(gated, CR + t - 1)
                    act.activation(sig[:, s], z[:, s], ACT.Sigmoid).then_inc(sig_done, 1)

            @block.vector
            def _(dve):
                def low(u, s):
                    dve.wait_ge(w_hi, CR + u + 1)
                    dve.tensor_tensor(whl[1][:, s], raw[:, s], whl[0][:, s].bitcast(F32), ALU.subtract).then_inc(w_lo, 1)

                low(0, 0)
                for t, s, u, m in tiles:
                    if m == 0 and u + 1 < NU:
                        low(u + 1, (u + 1) % 2)
                    dve.wait_ge(sig_done, CR + t + 1)
                    dve.wait_ge(full, CR + 3 * t + 3)
                    dve.wait_ge(stored[s], ST + 16 * (t // 2))
                    dve.tensor_tensor(o[:, s], ps[:, s, 0:3].rearrange("p c n -> p (c n)")[:, 0:T], sig[:, s], ALU.mult).then_inc(gated, 1)
                    if add is not None:
                        dve.wait_ge(gated, CR + t + 1)
                        dve.wait_ge(a_in[s], 16 * (t // 2) + 16)
                        dve.tensor_tensor(o[:, s], o[:, s], extra[:, s], ALU.add).then_inc(summed, 1)

            @block.tensor
            def _(pe):
                for t, s, u, m in tiles:
                    if m == 0:
                        pe.wait_ge(w_lo, CR + u + 1)
                    pe.wait_ge(gated, CR + t - 1)
                    channel_tile(pe, ps[:, s], lambda j, k: whl[j][:, u % 2, k, m * P:(m + 1) * P],
                                 lambda j, k, a, b: act_hl[:, j, k, a:b], full)

        ph.clear()


def gla(nc, proj_t, proj_c, wg, bg, g_norm, masks, rT, cst, act_hl):
    with ExitStack() as ctx:
        ph = Phase(nc, ctx, "gl")
        qk = ph.sb("qk", [P, 2, T])
        v, g = ph.sb("v", [P, NT, DV]), ph.sb("g", [P, NT, DV])
        wgate, bias = ph.sb("w_gate", [RANK, 2, DK]), ph.sb("bias", [P, 2])
        gnorm = ph.sb("gnorm", [P, DV])
        starts = ph.sb("starts", [P, T + CH], BF16)
        mask = ph.sb("mask", [P, 2, P], U8)
        z_b, e = [ph.sb("zb0", [P, T]), ph.sb("zb1", [P, T])], ph.sb("e", [P, T])
        decay = ph.sb("decay", [P, 2, NCH])
        qt, kt = ph.sb("q_t", [P, 2, T]), ph.sb("k_t", [P, 2, T])
        khT = ph.sb("k_hat_turned", [P, NT, DK])
        S = ph.sb("states", [P, 2, NCH - 1, DV])
        A = ph.sb("A", [P, 2, 2, P])
        flat = khT[:].rearrange("p n d -> p (n d)")
        Asum = flat[:, 0:2 * P].rearrange("p (s n) -> p s n", s=2)
        o_n = flat[:, 2 * P:2 * P + 2 * DV].rearrange("p (s n) -> p s n", s=2)
        oss, oroot, oinv = (ph.sb(n, [P, 2]) for n in ("oss", "oroot", "oinv"))
        pp = ph.ps("ps", [P, 8, 512])
        gate_ps = pp[:, 0:3].rearrange("p c n -> p (c n)")[:, 0:T]
        kh_ps = pp[:, 5:8].rearrange("p c n -> p (c n)")[:, 0:T]
        u_ps, a_ps = [pp[:, 3, 0:DV], pp[:, 4, 0:DV]], [pp[:, 5], pp[:, 6]]
        o_ps, t_ps = u_ps, pp[:, 7, 0:DV].rearrange("p (c t) -> p c t", c=2)
        const_in, qk_in, v_in, g_in, w_in = (ph.landed(n) for n in ("const_in", "qk_in", "v_in", "g_in", "w_in"))
        set_up, gates, z_done, neg_done, m_step, lg_done, b_done, d_done, e_done, dec_done = ph.done(
            "set_up", "gates", "z_done", "neg_done", "m_step", "lg_done", "b_done", "d_done", "e_done", "dec_done")
        q_prod, k_prod, kh_tp, kh_out, u_full, moved, silu_done = ph.done(
            "q_prod", "k_prod", "kh_tp", "kh_out", "u_full", "moved", "silu_done")
        a_full, a_cut, a_sum, o_full, ssd, rooted, o_inv, o_scaled, o_ready, o_tp, o_hi, o_lo = ph.done(
            "a_full", "a_cut", "a_sum", "o_full", "ssd", "rooted", "o_iv", "o_scaled", "o_ready", "o_tp", "o_hid", "o_lod")
        NU = NCH - 2
        order = [list(range(NCH)), list(range(NCH - 1, -1, -1))]
        begins = [(0, NCHS), (NCH - 1, NCHS - 1)]
        ends = [(NCHS - 1, NCH - 1), (NCHS, 0)]
        chunks = lambda t: t.rearrange("p (c n) -> p c n", n=CH)
        chunk_end = lambda t, d: chunks(t)[:, :, CH - 1 if d == 0 else 0]
        state = lambda d, c: S[:, d, c - 1 + d]

        def heads(eng, body):
            with eng.Fori(0, GH - 1) as i:
                body(i, False)
            body(GH - 1, True)

        def updates(d):
            return [(n, c) for n, c in enumerate(c for c in order[d] if c not in ends[d])]

        with nc.Block() as block:

            @block.sync
            def _(sp):
                ph.start(sp)
                sp.dma_start(A[:, 0], masks.rearrange("m p n -> p m n")).then_inc(const_in, 16)
                sp.dma_start(gnorm[:], g_norm.to_broadcast([P, DV])).then_inc(const_in, 16)
                with sp.Fori(0, GH) as i:
                    sp.wait_ge(q_prod, CR + 2 * i)
                    sp.wait_ge(k_prod, CR + 4 * i)
                    for j, row in enumerate((C_Q, C_K)):
                        sp.dma_start(qk[:, j], proj_c[bass.ds(i * DK + row, DK)]).then_inc(qk_in, 16)
                    sp.wait_ge(z_done, CR + 2 * i)
                    ph.settle(sp)
                    for d in range(2):
                        sp.dma_start(wgate[:, d], wg[d][:, bass.ds(i * DK, DK)]).then_inc(w_in, 16)
                        sp.dma_start(bias[:, d:d + 1], bg[d].rearrange("o (p u) -> (o p) u", u=1)[bass.ds(i * DK, DK)]).then_inc(w_in, 16)
                    sp.wait_ge(o_full, CR + NT * i)
                    sp.wait_ge(o_ready, CR + NT * i)
                    for dst, grp, s in ((v, G_V, v_in), (g, G_G, g_in)):
                        src = proj_t.rearrange("(n p) c -> p n c", p=P)
                        sp.dma_start(dst[:], src[:, :, bass.ds(i * DV + grp * UW, DV)]).then_inc(s, 16)

            @block.gpsimd
            def _(pool):
                def add_scores(i, t):
                    pool.wait_ge(a_cut, CR + 2 * (NT * i + t) + 2)
                    pool.wait_ge(o_full, CR + NT * i + t - 1)
                    pool.tensor_tensor(Asum[:, t % 2], A[:, t % 2, 0], A[:, t % 2, 1], ALU.add).then_inc(a_sum, 1)

                def gate(i, t):
                    pool.wait_ge(o_scaled, CR + NT * i + t + 1)
                    pool.tensor_tensor(o_n[:, t % 2], o_n[:, t % 2], g[:, t], ALU.mult).then_inc(o_ready, 1)

                with pool.Fori(0, GH) as i:
                    pool.wait_ge(qk_in, 32 * i + 32)
                    for d in range(2):
                        q = 2 * i + d
                        pool.wait_ge(e_done, CR + 3 * q + 2)
                        pool.tensor_tensor(z_b[d][:], qk[:, 1], z_b[d][:], ALU.mult).then_inc(k_prod, 1)
                        pool.wait_ge(a_full, CR + NT * i)
                        pool.wait_ge(e_done, CR + 3 * q + 3)
                        pool.tensor_tensor(kt[:, d], qk[:, 1], e[:], ALU.mult).then_inc(k_prod, 1)
                    pool.wait_ge(silu_done, CR + i + 1)
                    add_scores(i, 0)
                    for t in range(NT):
                        if t + 1 < NT:
                            add_scores(i, t + 1)
                        gate(i, t)

            @block.scalar
            def _(act):
                def gates_in(i, d):
                    act.wait_ge(w_in, 64 * i + 64)
                    act.wait_ge(e_done, CR + 3 * (2 * i + d))
                    act.wait_ge(gates, CR + 2 * i + d + 1)
                    act.activation(z_b[d][:], gate_ps, ACT.Identity, bias=bias[:, d:d + 1]).then_inc(z_done, 1)

                def soft_exp(i, d):
                    q = 2 * i + d
                    act.wait_ge(neg_done, CR + q + 1)
                    act.activation(e[:], e[:], ACT.Exp).then_inc(m_step, 1)

                def soft_ln(i, d):
                    q = 2 * i + d
                    act.wait_ge(m_step, CR + 2 * q + 1)
                    act.activation(e[:], e[:], ACT.Ln, bias=cst["one"]).then_inc(m_step, 1)

                def exponentials(i, d):
                    q, sums = 2 * i + d, z_b[1 - d]
                    act.wait_ge(b_done, CR + q + 1)
                    act.wait_ge(moved, CR + 2 * NU * i)
                    act.activation(decay[:, d], chunk_end(sums[:], d), ACT.Exp, scale=1.0 / GATE_NORM).then_inc(dec_done, 1)
                    act.activation(e[:], sums[:], ACT.Exp, scale=1.0 / GATE_NORM).then_inc(e_done, 1)
                    act.wait_ge(d_done, CR + q + 1)
                    act.activation(z_b[d][:], z_b[d][:], ACT.Exp, scale=1.0 / GATE_NORM).then_inc(e_done, 1)
                    act.wait_ge(q_prod, CR + q + 1)
                    act.activation(e[:], sums[:], ACT.Exp, scale=-1.0 / GATE_NORM).then_inc(e_done, 1)

                def k_hat_out(i, d):
                    act.wait_ge(kh_tp, CR + 2 * i + d + 1)
                    act.activation(khT[:], kh_ps, ACT.Copy).then_inc(kh_out, 1)

                def body(i, last):
                    soft_ln(i, 0)
                    exponentials(i, 0)
                    gates_in(i, 1)
                    k_hat_out(i, 0)
                    soft_exp(i, 1)
                    soft_ln(i, 1)
                    exponentials(i, 1)
                    k_hat_out(i, 1)
                    act.wait_ge(g_in, 16 * i + 16)
                    act.activation(g[:], g[:], ACT.Silu).then_inc(silu_done, 1)

                    def high(t):
                        act.wait_ge(o_tp, CR + NT * i + t + 1)
                        act.activation(act_hl[:, 0, bass.ds(2 * i, 2), t * P:(t + 1) * P], t_ps, ACT.Copy).then_inc(o_hi, 1)

                    for t in range(NT):
                        n, s = NT * i + t, t % 2
                        act.wait_ge(o_full, CR + n + 1)
                        act.wait_ge(o_tp, CR + n - 1)
                        act.activation(o_n[:, s], o_ps[s], ACT.Square, accum_out=oss[:, s:s + 1]).then_inc(ssd, 1)
                        act.wait_ge(ssd, CR + n + 1)
                        act.activation(oroot[:, s:s + 1], oss[:, s:s + 1], ACT.Sqrt, scale=1.0 / DV, bias=cst["eps"]).then_inc(rooted, 1)
                        if t > 0:
                            high(t - 1)
                        if t == NT - 3 and not last:
                            gates_in(i + 1, 0)
                    if not last:
                        soft_exp(i + 1, 0)
                    high(NT - 1)

                gates_in(0, 0)
                soft_exp(0, 0)
                heads(act, body)

            @block.vector
            def _(dve):
                dve.memset(starts[:], 1.0).then_inc(set_up, 1)
                dve.wait_ge(const_in, 32)
                dve.tensor_copy(mask[:], A[:, 0]).then_inc(set_up, 1)
                dve.wait_ge(set_up, CR + 2)
                dve.memset(A[:], 0.0).then_inc(set_up, 1)
                dve.memset(starts[:, ::CH], 0.0).then_inc(set_up, 1)
                dve.wait_ge(set_up, CR + 4)

                def negative(i, d):
                    q = 2 * i + d
                    dve.wait_ge(z_done, CR + q + 1)
                    dve.wait_ge(k_prod, CR + 2 * q)
                    dve.scalar_tensor_tensor(out=e[:], in0=z_b[d][:], scalar=-1.0, in1=z_b[d][:],
                                             op0=ALU.mult, op1=ALU.min).then_inc(neg_done, 1)

                def log_gate(i, d):
                    q = 2 * i + d
                    dve.wait_ge(m_step, CR + 2 * q + 2)
                    dve.scalar_tensor_tensor(out=z_b[d][:], in0=z_b[d][:], scalar=0.0, in1=e[:], op0=ALU.min, op1=ALU.subtract).then_inc(lg_done, 1)

                def running_sum(i, d):
                    q, z, b = 2 * i + d, z_b[d], z_b[1 - d]
                    dve.wait_ge(lg_done, CR + q + 1)
                    dve.wait_ge(kh_tp, CR + q)
                    if d == 0:
                        dve.tensor_tensor_scan(b[:], starts[:, 0:T], z[:], 0.0, ALU.mult, ALU.add).then_inc(b_done, 1)
                    else:
                        dve.tensor_tensor_scan(b[:, ::-1], starts[:, 1:T + 1][:, ::-1], z[:, ::-1], 0.0, ALU.mult, ALU.add).then_inc(b_done, 1)

                def to_end(i, d):
                    q, z, b = 2 * i + d, z_b[d], z_b[1 - d]
                    dve.wait_ge(b_done, CR + q + 1)
                    dve.tensor_tensor(chunks(z[:]), chunk_end(b[:], d).unsqueeze(2).broadcast_to([P, NCH, CH]), chunks(b[:]), ALU.subtract).then_inc(d_done, 1)

                def q_product(i, d):
                    q = 2 * i + d
                    dve.wait_ge(qk_in, 32 * i + 32)
                    dve.wait_ge(e_done, CR + 3 * q + 1)
                    dve.wait_ge(a_full, CR + NT * i)
                    dve.wait_ge(o_full, CR + NT * i)
                    dve.scalar_tensor_tensor(out=qt[:, d], in0=qk[:, 0], scalar=float(DK) ** -0.5, in1=e[:],
                                             op0=ALU.mult, op1=ALU.mult).then_inc(q_prod, 1)

                def body(i, last):
                    for step in (log_gate, running_sum, to_end, q_product):
                        step(i, 0)
                    negative(i, 1)
                    between = {5: log_gate, 7: running_sum, 9: to_end, 12: q_product}
                    for d in range(2):
                        q = 2 * i + d
                        dve.wait_ge(dec_done, CR + q + 1)
                        for n, c in updates(d):
                            u = NU * q + n
                            dve.wait_ge(u_full, CR + u + 1)
                            dve.wait_ge(moved, CR + u)
                            new = state(d, c + 1 - 2 * d)
                            if c in begins[d]:
                                dve.tensor_copy(new, u_ps[n % 2]).then_inc(moved, 1)
                            else:
                                dve.scalar_tensor_tensor(out=new, in0=state(d, c), scalar=decay[:, d, c:c + 1], in1=u_ps[n % 2],
                                                         op0=ALU.mult, op1=ALU.add).then_inc(moved, 1)
                            if d == 0 and n in between:
                                between[n](i, 1)

                    def cut(t):
                        n, s = NT * i + t, t % 2
                        dve.wait_ge(a_full, CR + n + 1)
                        dve.wait_ge(a_sum, CR + n - 1)
                        ph.settle(dve)
                        for d in range(2):
                            dve.copy_predicated(A[:, s, d], mask[:, d], a_ps[s][:, d * P:(d + 1) * P]).then_inc(a_cut, 1)

                    def low(t):
                        dve.wait_ge(o_hi, CR + NT * i + t + 1)
                        dst = [act_hl[:, j, bass.ds(2 * i, 2), t * P:(t + 1) * P] for j in range(2)]
                        dve.tensor_tensor(dst[1], t_ps, dst[0].bitcast(F32), ALU.subtract).then_inc(o_lo, 1)

                    cut(0)
                    for t in range(NT):
                        n, s = NT * i + t, t % 2
                        if t + 1 < NT:
                            cut(t + 1)
                        dve.wait_ge(rooted, CR + n + 1)
                        dve.reciprocal(oinv[:, s:s + 1], oroot[:, s:s + 1]).then_inc(o_inv, 1)
                        dve.wait_ge(o_inv, CR + n + 1)
                        dve.scalar_tensor_tensor(out=o_n[:, s], in0=o_ps[s], scalar=oinv[:, s:s + 1], in1=gnorm[:],
                                                 op0=ALU.mult, op1=ALU.mult).then_inc(o_scaled, 1)
                        if t > 0:
                            low(t - 1)
                        if t == NT - 2 and not last:
                            negative(i + 1, 0)
                    low(NT - 1)

                negative(0, 0)
                heads(dve, body)

            @block.tensor
            def _(pe):
                def gate_logits(i, d):
                    pe.wait_ge(w_in, 64 * i + 64)
                    pe.wait_ge(z_done, CR + 2 * i + d)
                    for c, (a, w) in enumerate(TOK3):
                        mm = pe.matmul(pp[:, c, 0:w - a], wgate[:, d], rT[d][:, a:w], start=True, stop=True)
                    mm.then_inc(gates, 1)

                def body(i, last):
                    gate_logits(i, 1)
                    for d in range(2):
                        q = 2 * i + d
                        pe.wait_ge(k_prod, CR + 2 * q + 1)
                        pe.wait_ge(kh_out, CR + q)
                        pe.wait_ge(a_cut, CR + 2 * NT * i)
                        pe.wait_ge(o_lo, CR + NT * i)
                        for t in range(NT):
                            tr = pe.transpose(kh_ps[:, t * P:(t + 1) * P], z_b[d][:, t * P:(t + 1) * P], cst["ident"])
                        tr.then_inc(kh_tp, 1)
                        pe.wait_ge(kh_out, CR + q + 1)
                        pe.wait_ge(v_in, 16 * i + 16)
                        pe.wait_ge(o_scaled, CR + NT * i)
                        for n, c in updates(d):
                            rows = slice(c % 2 * CH, c % 2 * CH + CH)
                            pe.wait_ge(moved, CR + NU * q + n - 1)
                            pe.matmul(u_ps[n % 2], khT[rows, c // 2], v[rows, c // 2], start=True, stop=True).then_inc(u_full, 1)

                    def scores(t):
                        pe.wait_ge(a_cut, CR + 2 * (NT * i + t) - 2)
                        tok = slice(t * P, (t + 1) * P)
                        for d in range(2):
                            mm = pe.matmul(a_ps[t % 2][:, d * P:(d + 1) * P], kt[:, d, tok], qt[:, d, tok], start=True, stop=True)
                        mm.then_inc(a_full, 1)

                    def output(t):
                        out = o_ps[t % 2]
                        pe.wait_ge(a_sum, CR + NT * i + t + 1)
                        pe.wait_ge(o_scaled, CR + NT * i + t - 1)
                        parts = [(d, c) for c in (2 * t, 2 * t + 1) for d in range(2) if c not in begins[d]]
                        pe.matmul(out, Asum[:, t % 2], v[:, t], start=True, stop=False, skip_group_check=True)
                        for d, c in parts:
                            rows = slice(c % 2 * CH, c % 2 * CH + CH)
                            mm = pe.matmul(out[rows], qt[:, d, c * CH:(c + 1) * CH], state(d, c), start=False,
                                           stop=(d, c) == parts[-1], skip_group_check=True)
                        mm.then_inc(o_full, 1)

                    def turn(t):
                        n = NT * i + t
                        pe.wait_ge(o_ready, CR + n + 1)
                        pe.wait_ge(o_lo, CR + n)
                        for c in range(2):
                            tr = pe.transpose(t_ps[:, c], o_n[:, t % 2, c * P:(c + 1) * P], cst["ident"])
                        tr.then_inc(o_tp, 1)

                    pe.wait_ge(q_prod, CR + 2 * i + 2)
                    pe.wait_ge(k_prod, CR + 4 * i + 4)
                    pe.wait_ge(moved, CR + 2 * NU * i + 2 * NU)
                    scores(0)
                    for t in range(NT):
                        if t + 1 < NT:
                            scores(t + 1)
                        output(t)
                        if t > 0:
                            turn(t - 1)
                        if t == NT - 4 and not last:
                            gate_logits(i + 1, 0)
                    turn(NT - 1)

                gate_logits(0, 0)
                heads(pe, body)

        ph.clear()


def finish_mixer(nc, x, merged, w_out, norm_ffn, w_router, cst, y, h2, affT):
    with ExitStack() as ctx:
        ph = Phase(nc, ctx, "fm")
        WC = 256
        NU = D // WC
        raw = ph.sb("w_raw", [P, NU, KC, WC])
        whl = [ph.sb(n, [P, KC, D], F32R) for n in ("w_hi", "w_lo")]
        wr, gamma = ph.sb("w_router", [P, KC, NE]), ph.sb("gamma", [P, D])
        mg = ph.sb("merged", [P, 2, KC, P])
        mhl = [ph.sb(n, [P, 2, KC, P], F32R) for n in ("m_hi", "m_lo")]
        xt, x1, hn = (ph.sb(n, [P, 2, D]) for n in ("x", "x1", "hn"))
        hT = ph.sb("hT", [P, KC, P])
        ssq, root, inv = (ph.sb(n, [P, 2]) for n in ("ssq", "root", "inv"))
        rmax, rsum, rinv, aff = ph.sb("rmax", [P, 1]), ph.sb("rsum", [P, 1]), ph.sb("rinv", [P, 1]), ph.sb("aff", [P, NE])
        ps_x, ps_h = ph.ps("ps_x", [P, 2, D]), ph.ps("ps_h", [P, KC, P])
        ps_r, ps_a = ph.ps("ps_r", [P, 512]), ph.ps("ps_a", [P, 512])
        w_in, c_in, m_in, x_in = ph.landed("w_in", NU), ph.landed("c_in"), ph.landed("m_in", 2), ph.landed("x_in", 2)
        w_hi, w_lo, m_hi, m_lo, x_full, x1_done, ssd, rooted, inv_done, hn_done = ph.done(
            "w_hid", "w_lod", "m_hid", "m_lod", "x_full", "x1_done", "ssd", "rooted", "inv_done", "hn_done")
        h_tp, h_out, r_full, r_max, r_exp, r_inv, a_done, a_tp, a_out = ph.done(
            "h_tp", "h_out", "r_full", "r_max", "r_exp", "r_iv", "a_done", "a_tp", "a_out")
        y_st, h_st = ph.stored("y_st", 2), ph.stored("h_st", 2)
        rows = lambda t: t.rearrange("(n p) d -> p n d", p=P)
        x_d, y_d, h_d = rows(x), rows(y), rows(h2)
        w_d = w_out.rearrange("(k p) c -> p k c", p=P)
        m_d = merged.rearrange("(k p) t -> p k t", p=P)

        def tiles(eng, body):
            for s in range(2):
                body(s, s, 0)
            with eng.Fori(1, NT // 2 - 1) as i:
                for s in range(2):
                    body(2 * i + s, s, i)
            for s in range(2):
                body(NT - 2 + s, s, NT // 2 - 1)

        last = lambda n, ahead: isinstance(n, int) and n + ahead >= NT
        first = lambda n: isinstance(n, int) and n == 0

        with nc.Block() as block:

            @block.sync
            def _(sp):
                ph.start(sp)
                for u in range(NU):
                    sp.dma_start(raw[:, u], w_d[:, :, u * WC:(u + 1) * WC]).then_inc(w_in[u], 16)

                def body(n, s, i):
                    sp.wait_ge(x1_done, CR + n + 1)
                    sp.dma_start(y_d[:, bass.ds(n, 1)].rearrange("p o d -> p (o d)"), x1[:, s]).then_inc(y_st[s], 16)
                    sp.wait_ge(hn_done, CR + n + 1)
                    sp.dma_start(h_d[:, bass.ds(n, 1)].rearrange("p o d -> p (o d)"), hn[:, s]).then_inc(h_st[s], 16)

                tiles(sp, body)
                for s in range(2):
                    sp.wait_ge(y_st[s], ST + 16 * NT // 2)
                    sp.wait_ge(h_st[s], ST + 16 * NT // 2)

            @block.gpsimd
            def _(pool):
                pool.dma_start(gamma[:], norm_ffn.to_broadcast([P, D])).then_inc(c_in, 16)
                pool.dma_start(wr[:], w_router.rearrange("(k p) e -> p k e", p=P)).then_inc(c_in, 16)
                def body(n, s, i):
                    pool.wait_ge(m_lo, CR + n - 1)
                    pool.dma_start(mg[:, s], m_d[:, :, bass.ds(n * P, P)]).then_inc(m_in[s], 16)
                    pool.wait_ge(x1_done, CR + n - 1)
                    pool.dma_start(xt[:, s], x_d[:, bass.ds(n, 1)].rearrange("p o d -> p (o d)")).then_inc(x_in[s], 16)

                tiles(pool, body)

            @block.scalar
            def _(act):
                def high(n, s, i):
                    act.wait_ge(m_in[s], 16 * i + 16)
                    act.wait_ge(x_full, CR + n - 1)
                    act.activation(mhl[0][:, s], mg[:, s], ACT.Copy).then_inc(m_hi, 1)

                def aff_out(n):
                    act.wait_ge(a_tp, CR + n + 1)
                    act.activation(affT[:, bass.ds(n * P, P)], ps_a[0:NE, 0:P], ACT.Copy).then_inc(a_out, 1)

                def body(n, s, i):
                    if not last(n, 2):
                        high(n + 2, s, i + 1)
                    act.wait_ge(x1_done, CR + n + 1)
                    act.wait_ge(h_st[s], ST + 16 * i)
                    act.wait_ge(h_tp, CR + n - 1)
                    act.activation(hn[:, s], x1[:, s], ACT.Square, accum_out=ssq[:, s:s + 1]).then_inc(ssd, 1)
                    act.wait_ge(ssd, CR + n + 1)
                    act.activation(root[:, s:s + 1], ssq[:, s:s + 1], ACT.Sqrt, scale=1.0 / D, bias=cst["eps"]).then_inc(rooted, 1)
                    act.wait_ge(h_tp, CR + n + 1)
                    act.wait_ge(r_full, CR + n)
                    act.activation(hT[:], ps_h[:], ACT.Copy).then_inc(h_out, 1)
                    if not first(n):
                        aff_out(n - 1)
                    act.wait_ge(r_max, CR + n + 1)
                    act.activation(aff[:], ps_r[:, 0:NE], ACT.Exp, bias=rmax[:], accum_out=rsum[:]).then_inc(r_exp, 1)

                high(0, 0, 0)
                for u in range(NU):
                    act.wait_ge(w_in[u], 16)
                    act.activation(whl[0][:, :, u * WC:(u + 1) * WC], raw[:, u], ACT.Copy).then_inc(w_hi, 1)
                high(1, 1, 0)
                tiles(act, body)
                aff_out(NT - 1)

            @block.vector
            def _(dve):
                def low(n, s):
                    dve.wait_ge(m_hi, CR + n + 1)
                    dve.tensor_tensor(mhl[1][:, s], mg[:, s], mhl[0][:, s].bitcast(F32), ALU.subtract).then_inc(m_lo, 1)

                low(0, 0)
                for u in range(NU):
                    cols = slice(u * WC, (u + 1) * WC)
                    dve.wait_ge(w_hi, CR + u + 1)
                    dve.tensor_tensor(whl[1][:, :, cols], raw[:, u], whl[0][:, :, cols].bitcast(F32), ALU.subtract).then_inc(w_lo, 1)
                low(1, 1)
                dve.wait_ge(c_in, 32)

                def body(n, s, i):
                    dve.wait_ge(x_full, CR + n + 1)
                    dve.wait_ge(x_in[s], 16 * i + 16)
                    dve.wait_ge(y_st[s], ST + 16 * i)
                    dve.tensor_tensor(x1[:, s], ps_x[:, s], xt[:, s], ALU.add).then_inc(x1_done, 1)
                    if not last(n, 2):
                        low(n + 2, s)
                    dve.wait_ge(rooted, CR + n + 1)
                    dve.reciprocal(inv[:, s:s + 1], root[:, s:s + 1]).then_inc(inv_done, 1)
                    dve.wait_ge(inv_done, CR + n + 1)
                    dve.scalar_tensor_tensor(out=hn[:, s], in0=x1[:, s], scalar=inv[:, s:s + 1], in1=gamma[:],
                                             op0=ALU.mult, op1=ALU.mult).then_inc(hn_done, 1)
                    dve.wait_ge(r_full, CR + n + 1)
                    dve.tensor_reduce(rmax[:], ps_r[:, 0:NE], AX.X, ALU.max, negate=True).then_inc(r_max, 1)
                    dve.wait_ge(r_exp, CR + n + 1)
                    dve.reciprocal(rinv[:], rsum[:]).then_inc(r_inv, 1)
                    dve.wait_ge(r_inv, CR + n + 1)
                    dve.tensor_scalar(aff[:], aff[:], rinv[:], None, ALU.mult).then_inc(a_done, 1)

                tiles(dve, body)

            @block.tensor
            def _(pe):
                def products(n, s, half):
                    pe.wait_ge(m_lo, CR + n + 1)
                    pe.wait_ge(x1_done, CR + n - 1)
                    c = 512 * half
                    for k in range(KC):
                        mm = three_passes(pe, ps_x[:, s, c:c + 512], [m[:, s, k] for m in mhl],
                                          [w[:, k, c:c + 512] for w in whl], k == 0, k == KC - 1)
                    if half == 1:
                        mm.then_inc(x_full, 1)

                def turn_aff(n):
                    pe.wait_ge(a_done, CR + n + 1)
                    pe.wait_ge(a_out, CR + n)
                    pe.transpose(ps_a[0:NE, 0:P], aff[:], cst["ident"]).then_inc(a_tp, 1)

                def body(n, s, i):
                    if not last(n, 1):
                        products(n + 1, 1 - s, 0)
                    if not first(n):
                        turn_aff(n - 1)
                    pe.wait_ge(hn_done, CR + n + 1)
                    pe.wait_ge(h_out, CR + n)
                    for k in range(KC):
                        tr = pe.transpose(ps_h[:, k], hn[:, s, k * P:(k + 1) * P], cst["ident"])
                    tr.then_inc(h_tp, 1)
                    if not last(n, 1):
                        products(n + 1, 1 - s, 1)
                    pe.wait_ge(h_out, CR + n + 1)
                    for k in range(KC):
                        mm = pe.matmul(ps_r[:, 0:NE], hT[:, k], wr[:, k], start=k == 0, stop=k == KC - 1)
                    mm.then_inc(r_full, 1)

                for half in range(2):
                    pe.wait_ge(w_lo, CR + (half + 1) * NU // 2)
                    products(0, 0, half)
                pe.wait_ge(c_in, 32)
                tiles(pe, body)
                turn_aff(NT - 1)

        ph.clear()


def choose(nc, affT, cst, slots_i, slots_g):
    with ExitStack() as ctx:
        ph = Phase(nc, ctx, "tk")
        HW, ROWS = TS // 2, 3 * 32
        vals = ph.sb("aff", [ROWS, HW])
        lists = ph.sb("lists", [ROWS, 4, CS])
        idx, offset = ph.sb("idx", [ROWS, CS], U32), ph.sb("offset", [ROWS, 1])
        a_first, diff = ph.sb("a_first", [CS, NE]), ph.sb("diff", [CS, NE])
        b_sb = ph.sb("b", [CS, 2, NE])
        ps = ph.ps("ps", [P, 4, 512])
        moved_in = ph.landed("moved_in")
        step, filled, conv, turned, out = ph.done("step", "filled", "conv", "tp", "out")
        parts = [(0, HW), (HW, TS), (TS, T)]

        with nc.Block() as block:

            @block.sync
            def _(sp):
                ph.start(sp)
                sp.wait_ge(filled, CR + 1)
                for i, (a, b) in enumerate(parts):
                    sp.dma_start(vals[32 * i:32 * i + NE, 0:b - a], affT[:, a:b]).then_inc(moved_in, 16)

            @block.vector
            def _(dve):
                dve.memset(vals[:], -1.0).then_inc(filled, 1)
                for i, (a, _b) in enumerate(parts):
                    dve.memset(offset[32 * i:32 * i + 32], float(a)).then_inc(filled, 1)
                dve.wait_ge(moved_in, 16 * len(parts))
                for r in range(CS // 8):
                    k, v8 = CR + 3 * r, lists[:, 0, r * 8:r * 8 + 8]
                    dve.wait_ge(step, k)
                    dve.max(v8, vals[:]).then_inc(step, 1)
                    dve.wait_ge(step, k + 1)
                    dve.max_index(idx[:, r * 8:r * 8 + 8], v8, vals[:]).then_inc(step, 1)
                    dve.wait_ge(step, k + 2)
                    dve.match_replace(vals[:], v8, vals[:], -1.0).then_inc(step, 1)
                dve.wait_ge(step, CR + 3 * (CS // 8))
                dve.tensor_copy(lists[:, 1], idx[:]).then_inc(conv, 1)
                dve.wait_ge(conv, CR + 1)
                dve.wait_ge(filled, CR + 4)
                dve.tensor_scalar(lists[:, 1], lists[:, 1], offset[:], None, ALU.add).then_inc(conv, 1)
                dve.wait_ge(conv, CR + 2)
                dve.tensor_copy(lists[:, 2:4], lists[:, 0:2, ::-1]).then_inc(conv, 1)
                dve.wait_ge(turned, CR + 4)
                (a_val, a_row), (b_val, b_row) = ([ps[0:CS, j + q, c:c + NE] for q in range(2)] for j, c in ((0, 0), (2, 32)))
                for q, src in enumerate((b_val, b_row)):
                    dve.tensor_copy(b_sb[:, q], src).then_inc(out, 1)
                for q, dst in enumerate((slots_g, slots_i)):
                    dve.tensor_copy(dst[1][:], ps[0:CP, q, 64:64 + NE]).then_inc(out, 1)
                dve.wait_ge(out, CR + 4)
                dve.tensor_tensor(a_first[:], a_val, b_sb[:, 0], ALU.is_ge).then_inc(out, 1)
                dve.tensor_tensor(slots_g[0][:], a_val, b_sb[:, 0], ALU.max).then_inc(out, 1)
                dve.tensor_tensor(diff[:], a_row, b_sb[:, 1], ALU.subtract).then_inc(out, 1)
                dve.wait_ge(out, CR + 7)
                dve.tensor_tensor(diff[:], diff[:], a_first[:], ALU.mult).then_inc(out, 1)
                dve.wait_ge(out, CR + 8)
                dve.tensor_tensor(slots_i[0][:], diff[:], b_sb[:, 1], ALU.add).then_inc(out, 1)
                dve.wait_ge(out, CR + 9)

            @block.tensor
            def _(pe):
                pe.wait_ge(conv, CR + 3)
                for j in range(4):
                    pe.transpose(ps[0:CS, j, 0:ROWS], lists[:, j], cst["ident"][0:ROWS, 0:ROWS]).then_inc(turned, 1)

        ph.clear()


def experts(nc, h2, y, w_gate, w_up, w_down, slots_i, slots_g, cst):
    with ExitStack() as ctx:
        ph = Phase(nc, ctx, "ex")
        WC = 2 * P
        NG, ND = FF // WC, D // WC
        STEPS, UNITS = NG + ND, 2 * (NG + ND)
        FT, DT = FF // P, D // P
        TILES = FT + DT
        NRAW, NHL = 6, 6
        XR = 4
        EARLY = 4
        raw = ph.sb("w_raw", [P, NRAW, KC, WC])
        whl = [ph.sb(n, [P, NHL, KC, WC], F32R) for n in ("w_hi", "w_lo")]
        xe = [ph.sb(f"xe{j}", [n, D]) for j, n in enumerate((CS, CP))]
        xT = ph.sb("xT", [P, KC, 2, CT], F32R)
        hid = ph.sb("hid", [P, FT, 2, CT], F32R)
        gs, us, sg, hf = (ph.sb(n, [P, 2, CT]) for n in ("gate_sum", "up_sum", "silu", "hidden"))
        yT = ph.sb("yT", [P, 2, CT])
        ye = [ph.sb(f"ye{j}", [n, D]) for j, n in enumerate((CS, CP))]
        gate = [ph.sb(f"gate{j}", [n, 1]) for j, n in enumerate((CS, CP))]
        rows_x, rows_y = ([ph.sb(f"rows_{w}{j}", [n, 1], U32) for j, n in enumerate((CS, CP))] for w in "xy")
        ps_w = ph.ps("ps_w", [P, 3, 2, 512])
        ps_t = ph.ps("ps_t", [P, 2, 512])
        w_in, x_in = ph.landed("w_in", NRAW), ph.landed("x_in", 2)
        w_hi, w_lo, t_full, t_out, g_sum, silu_done, h_mul, h_hi, h_lo = ph.done(
            "w_hid", "w_lod", "t_full", "t_out", "g_sum", "silu_done", "h_mul", "h_hid", "h_lod")
        row_x, row_y, gate_set, x_tp, x_hi, x_lo, y_tp, y_half, y_out = ph.done(
            "row_x", "row_y", "gate_set", "x_tp", "x_hid", "x_lod", "y_tp", "y_half", "y_out")
        scattered = ph.landed("scattered", 2)
        gu_d = [w.rearrange("e (k p) c -> p e k c", p=P) for w in (w_gate, w_up)]
        dn_d = w_down.rearrange("e (h k p) c -> p e h k c", p=P, k=KC)

        def sum2(dve, out, src):
            return dve.tensor_reduce(out, src[:, 0:2 * CT].rearrange("p (a t) -> p t a", a=2), AX.X, ALU.add)

        def experts_of(eng, body):
            with eng.Fori(0, NE - 1) as e:
                body(e, False)
            body(NE - 1, True)

        with nc.Block() as block:

            @block.sync
            def _(sp):
                ph.start(sp)
                with sp.Fori(0, NE) as e:
                    one = bass.ds(e, 1)
                    for j in range(UNITS):
                        sp.wait_ge(w_lo, CR + UNITS * e + j + 1 - NRAW)
                        if j < 2 * NG:
                            src = gu_d[j % 2][:, one, :, j // 2 * WC:(j // 2 + 1) * WC].rearrange("p e k c -> p (e k) c")
                        else:
                            c = (j - 2 * NG) // 2 * WC
                            src = dn_d[:, one, j % 2, :, c:c + WC].rearrange("p e k c -> p (e k) c")
                        sp.dma_start(raw[:, j % NRAW], src).then_inc(w_in[j % NRAW], 16)

            @block.gpsimd
            def _(pool):
                def gather(e):
                    for j in range(2):
                        pool.tensor_copy(rows_x[j][:], slots_i[j][:, bass.ds(e, 1)]).then_inc(row_x, 1)
                    pool.wait_ge(row_x, CR + 2 * e + 2)
                    ph.settle(pool)
                    for j in range(2):
                        pool.indirect_dma_start(xe[j][:], None, h2, bass.IndirectOffsetOnAxis(ap=rows_x[j][:, 0:1], axis=0)).then_inc(x_in[j], 16)

                def hidden(e, tiles):
                    for f in tiles:
                        q, s = FT * e + f, f % 2
                        pool.wait_ge(t_out, CR + TILES * e + f + 1)
                        pool.wait_ge(silu_done, CR + q + 1)
                        pool.tensor_tensor(hid[:, f, 0], sg[:, s], us[:, s], ALU.mult).then_inc(h_hi, 1)
                        pool.tensor_tensor(hf[:, s], sg[:, s], us[:, s], ALU.mult).then_inc(h_mul, 1)
                        pool.wait_ge(h_hi, CR + q + 1)
                        pool.wait_ge(h_mul, CR + q + 1)
                        pool.tensor_tensor(hid[:, f, 1], hf[:, s], hid[:, f, 0].bitcast(F32), ALU.subtract).then_inc(h_lo, 1)

                def body(e, last):
                    if not last:
                        for j in range(2):
                            pool.wait_ge(x_in[j], 16 * e + 16)
                        pool.wait_ge(x_tp, CR + XR * e + XR)
                        gather(e + 1)
                    for j in range(2):
                        pool.tensor_copy(gate[j][:], slots_g[j][:, bass.ds(e, 1)]).then_inc(gate_set, 1)
                    hidden(e, range(EARLY, FT))
                    for j in range(2):
                        pool.tensor_copy(rows_y[j][:], slots_i[j][:, bass.ds(e, 1)]).then_inc(row_y, 1)
                    pool.wait_ge(row_y, CR + 2 * e + 2)
                    pool.wait_ge(y_out, CR + DT * e + DT)
                    ph.settle(pool)
                    for j in range(2):
                        pool.indirect_dma_start(y, bass.IndirectOffsetOnAxis(ap=rows_y[j][:, 0:1], axis=0), ye[j][:], None,
                                                compute_op=ALU.add).then_inc(scattered[j], 16)
                    if not last:
                        hidden(e + 1, range(EARLY))
                    for j in range(2):
                        pool.wait_ge(scattered[j], 16 * e + 16)

                gather(0)
                hidden(0, range(EARLY))
                experts_of(pool, body)

            @block.scalar
            def _(act):
                def high(e, j):
                    e, j = (e, j) if j < UNITS else (e + 1, j - UNITS)
                    act.wait_ge(w_in[j % NRAW], 16 * (UNITS // NRAW * e + j // NRAW) + 16)
                    act.wait_ge(t_full, CR + TILES * e + 2 * (j // 2 - NHL // 2 + 1))
                    act.activation(whl[0][:, j % NHL], raw[:, j % NRAW], ACT.Copy).then_inc(w_hi, 1)

                def x_high(e, rounds):
                    for r in rounds:
                        act.wait_ge(x_tp, CR + XR * e + r + 1)
                        act.activation(xT[:, 2 * r:2 * r + 2, 0], ps_w[:, (FT + r) % 3, 1, 0:2 * CT].rearrange("p (k t) -> p k t", k=2), ACT.Copy).then_inc(x_hi, 1)

                def silu(e, f):
                    q, s = FT * e + f, f % 2
                    act.wait_ge(g_sum, CR + q + 1)
                    act.wait_ge(h_mul, CR + q - 1)
                    act.activation(sg[:, s], gs[:, s], ACT.Silu).then_inc(silu_done, 1)

                def leave(e, m):
                    if m == 0:
                        act.wait_ge(gate_set, CR + 2 * e + 2)
                    act.wait_ge(y_tp, CR + DT * e + m + 1)
                    act.activation(ye[0][:, m * P:(m + 1) * P], ps_t[:, m % 2, 0:CS], ACT.Copy,
                                   scale=gate[0][:]).then_inc(y_half, 1)
                    act.activation(ye[1][:, m * P:(m + 1) * P], ps_t[0:CP, m % 2, P:2 * P], ACT.Copy,
                                   scale=gate[1][:]).then_inc(y_out, 1)

                def body(e, last):
                    for s in range(STEPS):
                        if not (last and s == STEPS - 1):
                            high(e, 2 * s + 2)
                            high(e, 2 * s + 3)
                        for h in range(2):
                            m = 2 * (s - NG) + h
                            if s < NG:
                                silu(e, 2 * s + h)
                            elif m < XR and not last:
                                x_high(e + 1, (m,))
                            if m > 0:
                                leave(e, m - 1)
                    leave(e, DT - 1)

                high(0, 0)
                high(0, 1)
                x_high(0, range(XR))
                experts_of(act, body)

            @block.vector
            def _(dve):
                def low(e, j):
                    e, j = (e, j) if j < UNITS else (e + 1, j - UNITS)
                    dve.wait_ge(w_hi, CR + UNITS * e + j + 1)
                    dve.tensor_tensor(whl[1][:, j % NHL], raw[:, j % NRAW], whl[0][:, j % NHL].bitcast(F32), ALU.subtract).then_inc(w_lo, 1)

                def x_low(e, rounds):
                    for r in rounds:
                        dve.wait_ge(x_hi, CR + XR * e + r + 1)
                        dve.tensor_tensor(xT[:, 2 * r:2 * r + 2, 1], ps_w[:, (FT + r) % 3, 1, 0:2 * CT].rearrange("p (k t) -> p k t", k=2),
                                          xT[:, 2 * r:2 * r + 2, 0].bitcast(F32), ALU.subtract).then_inc(x_lo, 1)

                def tile_out(e, t):
                    dve.wait_ge(t_full, CR + TILES * e + t + 1)
                    if t < FT:
                        q, s = FT * e + t, t % 2
                        dve.wait_ge(silu_done, CR + q - 1)
                        sum2(dve, gs[:, s], ps_w[:, t % 3, 0]).then_inc(g_sum, 1)
                        dve.wait_ge(h_mul, CR + q - 1)
                        sum2(dve, us[:, s], ps_w[:, t % 3, 1]).then_inc(t_out, 1)
                    else:
                        m = t - FT
                        dve.wait_ge(y_tp, CR + DT * e + m - 1)
                        sum2(dve, yT[:, m % 2], ps_w[:, t % 3, 0]).then_inc(t_out, 1)

                def body(e, last):
                    for s in range(STEPS):
                        if not (last and s == STEPS - 1):
                            low(e, 2 * s + 2)
                            low(e, 2 * s + 3)
                        for h in range(2):
                            if 0 <= 2 * (s - NG) + h < XR and not last:
                                x_low(e + 1, (2 * (s - NG) + h,))
                            tile_out(e, 2 * s + h)

                low(0, 0)
                low(0, 1)
                x_low(0, range(XR))
                experts_of(dve, body)

            @block.tensor
            def _(pe):
                def turn_x(e, rounds):
                    for j in range(2):
                        pe.wait_ge(x_in[j], 16 * e + 16)
                    for r in rounds:
                        pe.wait_ge(x_lo, CR + XR * e + r - 2)
                        for h in range(2):
                            k, c = 2 * r + h, h * CT
                            pe.transpose(ps_w[:, (FT + r) % 3, 1, c:c + CS], xe[0][:, k * P:(k + 1) * P], cst["ident"])
                            tr = pe.transpose(ps_w[:, (FT + r) % 3, 1, c + CS:c + CT], xe[1][:, k * P:(k + 1) * P], cst["ident"][0:CP, 0:CP])
                        tr.then_inc(x_tp, 1)

                def turn_y(e, m):
                    pe.wait_ge(t_out, CR + TILES * e + FT + m + 1)
                    pe.wait_ge(y_out, CR + DT * e + m - 1)
                    pe.transpose(ps_t[0:CS, m % 2, 0:P], yT[:, m % 2, 0:CS], cst["ident"])
                    pe.transpose(ps_t[0:CP, m % 2, P:2 * P], yT[:, m % 2, CS:CT], cst["ident"]).then_inc(y_tp, 1)

                def products(bank, slot, k, cols, x, first, last):
                    pe.matmul(bank[:, 0:2 * CT], whl[0][:, slot, k, cols], x, start=first, stop=False)
                    return pe.matmul(bank[:, CT:2 * CT], whl[1][:, slot, k, cols], x[:, 0], start=False, stop=last)

                def gate_up(e, s, t, h):
                    for u in range(2):
                        for k in range(KC):
                            mm = products(ps_w[:, t % 3, u], (2 * s + u) % NHL, k, slice(h * P, (h + 1) * P), xT[:, k], k == 0, k == KC - 1)
                    mm.then_inc(t_full, 1)

                def down(e, s, t, h, u):
                    pe.wait_ge(h_lo, CR + FT * e + KC * (u + 1))
                    for k in range(KC):
                        mm = products(ps_w[:, t % 3, 0], (2 * s + u) % NHL, k, slice(h * P, (h + 1) * P), hid[:, u * KC + k],
                                      u + k == 0, u == 1 and k == KC - 1)
                    if u == 1:
                        mm.then_inc(t_full, 1)

                def body(e, last):
                    for s in range(STEPS):
                        pe.wait_ge(w_lo, CR + UNITS * e + 2 * s + 2)
                        if s == 0:
                            pe.wait_ge(x_lo, CR + XR * e + XR)
                        order = [(h, u) for u in range(2) for h in range(2)] if s == NG else [(h, u) for h in range(2) for u in range(2)]
                        for h, u in order:
                            t = 2 * s + h
                            if u == 0:
                                pe.wait_ge(t_out, CR + TILES * e + t - 2)
                                if 0 <= t - FT < XR and not last:
                                    turn_x(e + 1, (t - FT,))
                            if s >= NG:
                                down(e, s, t, h, u)
                            elif u == 0:
                                gate_up(e, s, t, h)
                            if t > FT and u == 1:
                                turn_y(e, t - FT - 1)
                    turn_y(e, DT - 1)

                turn_x(0, range(XR))
                experts_of(pe, body)


def program(nc, dram):
    with ExitStack() as ctx:
        ident = ctx.enter_context(nc.sbuf_tensor("identity", [P, P], F32))
        eps = ctx.enter_context(nc.sbuf_tensor("eps", [P, 3], F32))
        slots_i = [ctx.enter_context(nc.sbuf_tensor(f"slots_i{j}", [n, NE], U32)) for j, n in enumerate((CS, CP))]
        slots_g = [ctx.enter_context(nc.sbuf_tensor(f"slots_g{j}", [n, NE], F32)) for j, n in enumerate((CS, CP))]
        scratch = lambda name, shape: nc.dram_tensor(name, shape, F32, kind="Internal").ap()
        proj_t, proj_c = scratch("proj_t", (T, NB * UW)), scratch("proj_c", (NA * UW, T))
        att_g, merged, h2 = scratch("att_gated", (D, T)), scratch("merged", (D, T)), scratch("h2", (T, D))
        cst = {"ident": ident[:], "eps": eps[:, 0:1], "one": eps[:, 1:2], "eps_hd": eps[:, 2:3]}
        consts_in = ctx.enter_context(nc.semaphore("consts_in"))
        eps_set = ctx.enter_context(nc.semaphore("eps_set"))
        with nc.Block() as block:

            @block.sync
            def _(sp):
                sp.dma_start(ident[:], dram["ident"]).then_inc(consts_in, 16)
                sp.wait_ge(consts_in, 16)

            @block.vector
            def _(dve):
                dve.memset(cst["eps"], EPS).then_inc(eps_set, 1)
                dve.memset(cst["one"], 1.0).then_inc(eps_set, 1)
                dve.memset(cst["eps_hd"], HD * EPS).then_inc(eps_set, 1)
                dve.wait_ge(eps_set, 3)

        with ExitStack() as mixer:
            act_hl = mixer.enter_context(nc.sbuf_tensor("act_hl", [P, 2, KC, T], F32R))
            rT = [mixer.enter_context(nc.sbuf_tensor(f"codes{d}", [RANK, T], F32)) for d in range(2)]
            ss = mixer.enter_context(nc.sbuf_tensor("head_squares", [P, NT, HEADS], F32))
            project(nc, dram["x"], dram["w_cols"], dram["norm_mix"], (dram["q_norm"], dram["k_norm"]), dram["cos"], dram["sin"],
                    cst, act_hl, proj_t, proj_c, rT, ss)
            with ExitStack() as kvs:
                kT = kvs.enter_context(nc.sbuf_tensor("kT", [P, 2, KVH, T], F32R))
                vv = kvs.enter_context(nc.sbuf_tensor("vv", [P, 2, NT, KVH * HD], F32R))
                inv = kvs.enter_context(nc.sbuf_tensor("head_inverses", [P, NT, HEADS], F32))
                keys(nc, proj_t, ss, inv, cst, kT, vv)
                attention(nc, proj_t, inv, cst, kT, vv, act_hl)
            mix(nc, "ma", act_hl, dram["w_o_att"], proj_c[C_ZB:C_ZB + D], att_g)
            gla(nc, proj_t, proj_c, (dram["w_gk_f"], dram["w_gk_b"]), (dram["b_gk_f"], dram["b_gk_b"]),
                dram["gla_norm"], dram["masks"], rT, cst, act_hl)
            mix(nc, "mg", act_hl, dram["w_o_gla"], proj_c[C_ZA:C_ZA + D], merged, add=att_g)
        with ExitStack() as router:
            affT = router.enter_context(nc.sbuf_tensor("affT", [NE, T], F32))
            finish_mixer(nc, dram["x"], merged, dram["w_out"], dram["norm_ffn"], dram["w_router"], cst, dram["y"], h2, affT)
            choose(nc, affT, cst, slots_i, slots_g)
        experts(nc, h2, dram["y"], dram["w_e_gate"], dram["w_e_up"], dram["w_e_down"], slots_i, slots_g, cst)


W_IN_ORDER = [(3104, 4128), (4128, 4640), (1024, 2048), (2048, 3072), (0, 1024), (4640, 6688), (3072, 3104)]


def rope_tables():
    pos = np.concatenate([np.arange(TS), np.arange(TP)])
    half = HD // 2
    inv = (10000.0 ** (-np.arange(0, half, 2, dtype=np.float32) / half)).astype(np.float32)
    ang = np.concatenate([(pos // GRID_W).astype(np.float32)[:, None] * inv,
                          (pos % GRID_W).astype(np.float32)[:, None] * inv], axis=1)
    return np.cos(ang), np.sin(ang)


def chunk_masks():
    j, i = np.arange(P)[:, None], np.arange(P)[None, :]
    same = j // CH == i // CH
    return np.stack([same & (i >= j), same & (i <= j)]).astype(np.float32)


def kernel(**inputs):
    import concourse.bacc as _bacc
    from concourse import mybir as _mybir
    from concourse.bass_utils import run_bass_kernel_spmd as _run

    given = {k: np.asarray(v) for k, v in inputs.items()}
    cos, sin = rope_tables()
    arrays = {
        "x": np.concatenate([given["x_sample"][0], given["x_prompt"][0]]),
        "w_cols": np.concatenate([given["w_in"][0][:, a:b] for a, b in W_IN_ORDER], axis=1),
        "ident": np.eye(P, dtype=np.float32), "cos": cos, "sin": sin, "masks": chunk_masks(),
    }
    for name in ("norm_mix", "b_gk_f", "b_gk_b", "gla_norm", "q_norm", "k_norm", "norm_ffn"):
        arrays[name] = given[name]
    for name in ("w_gk_f", "w_gk_b", "w_o_gla", "w_o_att", "w_out", "w_router", "w_e_gate", "w_e_up", "w_e_down"):
        arrays[name] = given[name][0]
    arrays = {k: np.ascontiguousarray(v) for k, v in arrays.items()}

    nc = _bacc.Bacc("TRN2", target_bir_lowering=False, num_devices=1)
    dram = {k: nc.dram_tensor(k, v.shape, _mybir.dt.from_np(v.dtype), kind="ExternalInput").ap() for k, v in arrays.items()}
    dram["y"] = nc.dram_tensor("y", (T, D), _mybir.dt.from_np(np.dtype("float32")), kind="ExternalOutput").ap()
    program(nc, dram)
    y = _run(nc, [arrays], core_ids=[0]).results[0]["y"]
    return y[TS:][None], y[:TS][None]
```
